# Optimizing a Trainium2 kernel written in Bass

```python
import math
import jax, jax.numpy as jnp
from jax import lax
import numpy as np

D_MODEL = 1024
BATCH = 1
SEQ = 256
DEPTH = 1

GRID_W = 64
CTX_LEN = 256
MIX_DIM = D_MODEL
ATT_DIM = MIX_DIM // 2
CONV_DIM = MIX_DIM - ATT_DIM
HEAD_DIM = 64
N_HEADS = ATT_DIM // HEAD_DIM
NA_ROWS = 8
NA_COLS = 16
CONV_WIDTH = 31
D_FF = 4 * D_MODEL
IN_PROJ_DIM = 3 * ATT_DIM + 2 * CONV_DIM
N_MOD = 6
ROPE_BASE = 10000.0
EPS = 1e-6


def rms_norm(x, g):
    xf = x.astype(jnp.float32)
    y = xf * lax.rsqrt(jnp.mean(xf * xf, axis=-1, keepdims=True) + EPS)
    return (y * g.astype(jnp.float32)).astype(x.dtype)

def modulate(h, shift, scale):
    return h * (1 + scale) + shift

def split_heads(t):
    b, l, _ = t.shape
    return t.reshape(b, l, N_HEADS, HEAD_DIM)

def split_proj(p):
    q = split_heads(p[..., :ATT_DIM])
    k = split_heads(p[..., ATT_DIM:2 * ATT_DIM])
    v = split_heads(p[..., 2 * ATT_DIM:3 * ATT_DIM])
    u = p[..., 3 * ATT_DIM:]
    return q, k, v, u

def rope_half(xh, pos):
    n_pairs = xh.shape[-1] // 2
    inv_freq = ROPE_BASE ** (-jnp.arange(n_pairs, dtype=jnp.float32) / n_pairs)
    ang = pos.astype(jnp.float32)[:, None] * inv_freq[None, :]
    cos = jnp.cos(ang)[None, :, None, :]
    sin = jnp.sin(ang)[None, :, None, :]
    x1 = xh[..., :n_pairs].astype(jnp.float32)
    x2 = xh[..., n_pairs:].astype(jnp.float32)
    return jnp.concatenate([x1 * cos - x2 * sin, x2 * cos + x1 * sin], axis=-1).astype(xh.dtype)

def axial_rope(x, row_pos, col_pos):
    half = HEAD_DIM // 2
    return jnp.concatenate([rope_half(x[..., :half], row_pos),
                            rope_half(x[..., half:], col_pos)], axis=-1)

def conformer_conv(u, kernel, bias, ln_g, ln_b):
    a, b = jnp.split(u, 2, axis=-1)
    h = a * jax.nn.sigmoid(b)
    pad = CONV_WIDTH // 2
    h = lax.conv_general_dilated(h, kernel[:, None, :].astype(h.dtype), window_strides=(1,),
                                 padding=[(pad, pad)], dimension_numbers=('NWC', 'WIO', 'NWC'),
                                 feature_group_count=CONV_DIM) + bias
    hf = h.astype(jnp.float32)
    mu = jnp.mean(hf, axis=-1, keepdims=True)
    var = jnp.mean(jnp.square(hf - mu), axis=-1, keepdims=True)
    hn = (hf - mu) * lax.rsqrt(var + EPS) * ln_g + ln_b
    return jax.nn.silu(hn).astype(u.dtype)

def sq_relu_mlp(h, w1, w2):
    return jnp.square(jax.nn.relu(h @ w1)) @ w2

def context_attention(q, k, v):
    b, lc = q.shape[0], q.shape[1]
    s = jnp.einsum('bqhd,bkhd->bhqk', q, k).astype(jnp.float32) * HEAD_DIM ** -0.5
    p = jax.nn.softmax(s, axis=-1).astype(v.dtype)
    o = jnp.einsum('bhqk,bkhd->bqhd', p, v)
    return o.reshape(b, lc, ATT_DIM)

def neighbourhood_attention(q_rot, q, k_rot, v, k_ctx, v_ctx, rpb):
    b, l, h, dh = q.shape
    rows = l // GRID_W
    kr = min(NA_ROWS, rows)
    scale = dh ** -0.5
    q_rot_g = q_rot.reshape(b, rows, GRID_W, h, dh).transpose(1, 0, 2, 3, 4)
    q_g = q.reshape(b, rows, GRID_W, h, dh).transpose(1, 0, 2, 3, 4)
    k_g = k_rot.reshape(b, rows, GRID_W, h, dh)
    v_g = v.reshape(b, rows, GRID_W, h, dh)
    row_start = np.clip(np.arange(rows) - kr // 2, 0, rows - kr).astype(np.int32)
    col_start = np.clip(np.arange(GRID_W) - NA_COLS // 2, 0, GRID_W - NA_COLS)
    col_idx = (col_start[:, None] + np.arange(NA_COLS)[None, :]).astype(np.int32)
    col_off = (col_idx - np.arange(GRID_W)[:, None] + (NA_COLS - 1)).astype(np.int32)
    rpb_cols = rpb[:, :, col_off]

    def one_row(args):
        qr_rot, qr, r, rs = args
        k_rows = lax.dynamic_slice_in_dim(k_g, rs, kr, axis=1)
        v_rows = lax.dynamic_slice_in_dim(v_g, rs, kr, axis=1)
        kw = k_rows[:, :, col_idx]
        vw = v_rows[:, :, col_idx]
        row_off = rs + jnp.arange(kr) - r + (NA_ROWS - 1)
        bias = rpb_cols[:, row_off].transpose(0, 2, 1, 3)
        s_win = jnp.einsum('bqhd,biqjhd->bhqij', qr_rot, kw).astype(jnp.float32) * scale
        s_win = (s_win + bias.astype(jnp.float32)[None]).reshape(b, h, GRID_W, kr * NA_COLS)
        s_ctx = jnp.einsum('bqhd,bchd->bhqc', qr, k_ctx).astype(jnp.float32) * scale
        p = jax.nn.softmax(jnp.concatenate([s_win, s_ctx], axis=-1), axis=-1).astype(v.dtype)
        p_win = p[..., :kr * NA_COLS].reshape(b, h, GRID_W, kr, NA_COLS)
        p_ctx = p[..., kr * NA_COLS:]
        return (jnp.einsum('bhqij,biqjhd->bqhd', p_win, vw)
                + jnp.einsum('bhqc,bchd->bqhd', p_ctx, v_ctx))

    out = lax.map(one_row, (q_rot_g, q_g, jnp.arange(rows, dtype=jnp.int32), jnp.asarray(row_start)))
    return out.transpose(1, 0, 2, 3, 4).reshape(b, l, h * dh)

def first_inputs(seed: int = 0) -> dict:
    key = jax.random.key(seed)
    ks = jax.random.split(key, 18)
    n = jax.random.normal
    return {
        'x': n(ks[0], (BATCH, SEQ, D_MODEL), jnp.float32),
        'c': n(ks[1], (BATCH, D_MODEL), jnp.float32),
        'ctx': n(ks[2], (BATCH, CTX_LEN, D_MODEL), jnp.float32),
        'c_ctx': n(ks[3], (D_MODEL,), jnp.float32),
        'w_ada': n(ks[4], (DEPTH, D_MODEL, N_MOD * D_MODEL), jnp.float32) * (0.5 * D_MODEL ** -0.5),
        'b_ada': 0.02 * n(ks[5], (DEPTH, N_MOD * D_MODEL), jnp.float32),
        'norm1_g': 1.0 + 0.02 * n(ks[6], (DEPTH, D_MODEL), jnp.float32),
        'norm2_g': 1.0 + 0.02 * n(ks[7], (DEPTH, D_MODEL), jnp.float32),
        'w_in': n(ks[8], (DEPTH, D_MODEL, IN_PROJ_DIM), jnp.float32) * D_MODEL ** -0.5,
        'dw_kernel': n(ks[9], (DEPTH, CONV_WIDTH, CONV_DIM), jnp.float32) * CONV_WIDTH ** -0.5,
        'dw_bias': 0.02 * n(ks[10], (DEPTH, CONV_DIM), jnp.float32),
        'conv_ln_g': 1.0 + 0.02 * n(ks[11], (DEPTH, CONV_DIM), jnp.float32),
        'conv_ln_b': 0.02 * n(ks[12], (DEPTH, CONV_DIM), jnp.float32),
        'rpb': 0.5 * n(ks[13], (DEPTH, N_HEADS, 2 * NA_ROWS - 1, 2 * NA_COLS - 1), jnp.float32),
        'w_out': n(ks[14], (DEPTH, MIX_DIM, D_MODEL), jnp.float32) * MIX_DIM ** -0.5,
        'w_mlp1': n(ks[15], (DEPTH, D_MODEL, D_FF), jnp.float32) * D_MODEL ** -0.5,
        'w_mlp2': n(ks[16], (DEPTH, D_FF, D_MODEL), jnp.float32) * D_FF ** -0.5,
        'final_g': 1.0 + 0.02 * n(ks[17], (D_MODEL,), jnp.float32),
    }

def first_block(x, c, ctx, c_ctx, w_ada, b_ada, norm1_g, norm2_g, w_in, dw_kernel, dw_bias,
              conv_ln_g, conv_ln_b, rpb, w_out, w_mlp1, w_mlp2, final_g):
    l = x.shape[1]
    t = jnp.arange(l, dtype=jnp.int32)
    row_pos = t // GRID_W
    col_pos = t % GRID_W
    silu_c = jax.nn.silu(c)
    silu_cc = jax.nn.silu(c_ctx)[None]
    for i in range(DEPTH):
        last = i == DEPTH - 1
        mod_x = (silu_c @ w_ada[i] + b_ada[i])[:, None, :]
        mod_c = (silu_cc @ w_ada[i] + b_ada[i])[:, None, :]
        sh1, sc1, g1, sh2, sc2, g2 = jnp.split(mod_x, N_MOD, axis=-1)
        csh1, csc1, cg1, csh2, csc2, cg2 = jnp.split(mod_c, N_MOD, axis=-1)

        hx = modulate(rms_norm(x, norm1_g[i]), sh1, sc1)
        hc = modulate(rms_norm(ctx, norm1_g[i]), csh1, csc1)
        qx, kx, vx, ux = split_proj(hx @ w_in[i])
        if last:
            kvc = hc @ w_in[i][:, ATT_DIM:3 * ATT_DIM]
            kc, vc = split_heads(kvc[..., :ATT_DIM]), split_heads(kvc[..., ATT_DIM:])
        else:
            qc, kc, vc, uc = split_proj(hc @ w_in[i])

        qx_rot = axial_rope(qx, row_pos, col_pos)
        kx_rot = axial_rope(kx, row_pos, col_pos)
        attn_x = neighbourhood_attention(qx_rot, qx, kx_rot, vx, kc, vc, rpb[i])
        conv_x = conformer_conv(ux, dw_kernel[i], dw_bias[i], conv_ln_g[i], conv_ln_b[i])
        x_new = x + g1 * (jnp.concatenate([attn_x, conv_x], axis=-1) @ w_out[i])

        hx2 = modulate(rms_norm(x_new, norm2_g[i]), sh2, sc2)
        x_new = x_new + g2 * sq_relu_mlp(hx2, w_mlp1[i], w_mlp2[i])

        if not last:
            attn_c = context_attention(qc, kc, vc)
            conv_c = conformer_conv(uc, dw_kernel[i], dw_bias[i], conv_ln_g[i], conv_ln_b[i])
            ctx = ctx + cg1 * (jnp.concatenate([attn_c, conv_c], axis=-1) @ w_out[i])
            hc2 = modulate(rms_norm(ctx, norm2_g[i]), csh2, csc2)
            ctx = ctx + cg2 * sq_relu_mlp(hc2, w_mlp1[i], w_mlp2[i])
        x = x_new
    return rms_norm(x, final_g)


A_HEADS = 8
B_HEADS = 8
IDX_HEADS = 8
IDX_DIM = 64
DILATED_PATTERNS = ((128, 1), (512, 4), (2048, 16))
TOPK_MAX = 256
D_A = A_HEADS * HEAD_DIM
D_B = B_HEADS * HEAD_DIM
D_FF_2 = ((8 * D_MODEL + 767) // 768) * 256
ROPE_THETA = 10000.0
RMS_EPS = 1e-6
BLOCK = 128
ATTN_SCALE = HEAD_DIM ** -0.5
IDX_SCALE = (IDX_DIM ** -0.5) * (IDX_HEADS ** -0.5)
IN_SPLITS = (D_A, D_A, D_A, D_B, HEAD_DIM, HEAD_DIM, IDX_HEADS * IDX_DIM, IDX_DIM, IDX_HEADS, D_MODEL, D_MODEL)
IN_OFFSETS = tuple(int(o) for o in np.cumsum(IN_SPLITS)[:-1])
D_IN = int(sum(IN_SPLITS))


def rmsnorm(x, g):
    x32 = x.astype(jnp.float32)
    y = x32 * lax.rsqrt(jnp.mean(x32 * x32, axis=-1, keepdims=True) + RMS_EPS)
    return (y * g.astype(jnp.float32)).astype(x.dtype)

def rope(z, pos):
    half = z.shape[-1] // 2
    inv_freq = ROPE_THETA ** (-jnp.arange(half, dtype=jnp.float32) / half)
    ang = pos.astype(jnp.float32)[:, None] * inv_freq[None, :]
    cos = jnp.cos(ang)[None, :, None, :]
    sin = jnp.sin(ang)[None, :, None, :]
    z32 = z.astype(jnp.float32)
    z1, z2 = z32[..., :half], z32[..., half:]
    return jnp.concatenate([z1 * cos - z2 * sin, z2 * cos + z1 * sin], axis=-1).astype(z.dtype)

def dilated_window_attention(q, k, v, window, dilation):
    B, T, H, hd = q.shape
    steps = window // dilation
    seg = dilation * BLOCK
    t_pad = -(-T // seg) * seg
    m_len = t_pad // dilation
    nb = m_len // BLOCK

    def to_blocks(z):
        z = jnp.pad(z, ((0, 0), (0, t_pad - T), (0, 0), (0, 0)))
        z = z.reshape(B, m_len, dilation, H, hd).transpose(0, 2, 3, 1, 4)
        return z.reshape(B, dilation, H, nb, BLOCK, hd)

    qb, kb, vb = to_blocks(q), to_blocks(k), to_blocks(v)

    def with_prev(z):
        prev = jnp.pad(z[:, :, :, :-1], ((0, 0), (0, 0), (0, 0), (1, 0), (0, 0), (0, 0)))
        return jnp.concatenate([prev, z], axis=4)

    k2, v2 = with_prev(kb), with_prev(vb)
    s = jnp.einsum('brhnqd,brhnkd->brhnqk', qb, k2).astype(jnp.float32) * ATTN_SCALE
    qi = jnp.arange(BLOCK)[:, None]
    kj = jnp.arange(2 * BLOCK)[None, :]
    dist = qi + BLOCK - kj
    band = (dist >= 0) & (dist <= steps)
    has_prev = (jnp.arange(nb)[:, None, None] > 0) | (kj >= BLOCK)[None]
    mask = band[None] & has_prev
    s = jnp.where(mask, s, -jnp.inf)
    m = jnp.max(s, axis=-1, keepdims=True)
    p = jnp.exp(s - m)
    den = jnp.sum(p, axis=-1, keepdims=True)
    o = jnp.einsum('brhnqk,brhnkd->brhnqd', p.astype(v.dtype), v2).astype(jnp.float32) / den
    lse = (m + jnp.log(den))[..., 0]
    o = o.reshape(B, dilation, H, m_len, hd).transpose(0, 3, 1, 2, 4).reshape(B, t_pad, H, hd)[:, :T]
    lse = lse.reshape(B, dilation, H, m_len).transpose(0, 3, 1, 2).reshape(B, t_pad, H)[:, :T]
    return o, lse

def dilated_mixture(q, k, v):
    outs, lses = [], []
    for window, dilation in DILATED_PATTERNS:
        o, l = dilated_window_attention(q, k, v, window, dilation)
        outs.append(o)
        lses.append(l)
    w = jax.nn.softmax(jnp.stack(lses, axis=0), axis=0)
    return jnp.sum(w[..., None] * jnp.stack(outs, axis=0), axis=0)

def indexed_sparse_attention(q, k, v, qi, ki, wi):
    B, T, H, hd = q.shape
    topk = min(TOPK_MAX, T // 4)
    nb = T // BLOCK
    key_pos = jnp.arange(T)

    def blocks(z):
        return jnp.moveaxis(z.reshape((B, nb, BLOCK) + z.shape[2:]), 1, 0)

    def one_block(args):
        q_blk, qi_blk, wi_blk, start = args
        q_pos = start + jnp.arange(BLOCK)
        causal = key_pos[None, :] <= q_pos[:, None]
        dots = jnp.einsum('bqhd,bsd->bqhs', qi_blk, ki).astype(jnp.float32)
        score = jnp.einsum('bqh,bqhs->bqs', wi_blk.astype(jnp.float32), jax.nn.relu(dots)) * IDX_SCALE
        score = jnp.where(causal[None], score, -jnp.inf)
        _, sel = lax.top_k(score, topk)
        valid = sel <= q_pos[None, :, None]
        k_sel = jax.vmap(lambda kk, ii: kk[ii])(k, sel)
        v_sel = jax.vmap(lambda vv, ii: vv[ii])(v, sel)
        s = jnp.einsum('bqhd,bqkd->bhqk', q_blk, k_sel).astype(jnp.float32) * ATTN_SCALE
        s = jnp.where(valid[:, None], s, -jnp.inf)
        p = jax.nn.softmax(s, axis=-1)
        return jnp.einsum('bhqk,bqkd->bqhd', p.astype(v.dtype), v_sel)

    starts = jnp.arange(nb, dtype=jnp.int32) * BLOCK
    out = lax.map(one_block, (blocks(q), blocks(qi), blocks(wi), starts))
    return jnp.moveaxis(out, 0, 1).reshape(B, T, H, hd)

def second_inputs(seed: int = 0) -> dict:
    key = jax.random.key(seed)
    ks = jax.random.split(key, 12)
    f32 = jnp.float32

    def dense(k, shape, fan_in):
        return jax.random.normal(k, shape, f32) * fan_in ** -0.5

    def gain(k, shape):
        return 1.0 + 0.02 * jax.random.normal(k, shape, f32)

    return {
        'x': jax.random.normal(ks[0], (BATCH, SEQ, D_MODEL), f32),
        'norm_mix': gain(ks[1], (DEPTH, D_MODEL)),
        'w_in': dense(ks[2], (DEPTH, D_MODEL, D_IN), D_MODEL),
        'w_up_a': dense(ks[3], (DEPTH, D_A, D_MODEL), D_A),
        'w_up_b': dense(ks[4], (DEPTH, D_B, D_MODEL), D_B),
        'w_out': dense(ks[5], (DEPTH, D_MODEL, D_MODEL), D_MODEL),
        'norm_ffn': gain(ks[6], (DEPTH, D_MODEL)),
        'w_gate': dense(ks[7], (DEPTH, D_MODEL, D_FF_2), D_MODEL),
        'w_up': dense(ks[8], (DEPTH, D_MODEL, D_FF_2), D_MODEL),
        'w_down': dense(ks[9], (DEPTH, D_FF_2, D_MODEL), D_FF_2),
        'norm_final': gain(ks[10], (D_MODEL,)),
    }

def second_block(x, norm_mix, w_in, w_up_a, w_up_b, w_out, norm_ffn, w_gate, w_up, w_down, norm_final):
    B, T, _ = x.shape
    pos = jnp.arange(T, dtype=jnp.int32)
    for layer in range(DEPTH):
        h = rmsnorm(x, norm_mix[layer])
        proj = h @ w_in[layer]
        qa, ka, va, qb, kb, vb, qi, ki, wi, ga, gb = jnp.split(proj, IN_OFFSETS, axis=-1)
        qa = rope(qa.reshape(B, T, A_HEADS, HEAD_DIM), pos)
        ka = rope(ka.reshape(B, T, A_HEADS, HEAD_DIM), pos)
        va = va.reshape(B, T, A_HEADS, HEAD_DIM)
        y_a = dilated_mixture(qa, ka, va).astype(x.dtype).reshape(B, T, D_A)
        qb = rope(qb.reshape(B, T, B_HEADS, HEAD_DIM), pos)
        kb = rope(kb[:, :, None], pos)[:, :, 0]
        qi = rope(qi.reshape(B, T, IDX_HEADS, IDX_DIM), pos)
        ki = rope(ki[:, :, None], pos)[:, :, 0]
        y_b = indexed_sparse_attention(qb, kb, vb, qi, ki, wi).reshape(B, T, D_B)
        merged = jax.nn.sigmoid(ga) * (y_a @ w_up_a[layer]) + jax.nn.sigmoid(gb) * (y_b @ w_up_b[layer])
        x = x + merged @ w_out[layer]
        h = rmsnorm(x, norm_ffn[layer])
        x = x + (jax.nn.silu(h @ w_gate[layer]) * (h @ w_up[layer])) @ w_down[layer]
    return rmsnorm(x, norm_final)


def setup_inputs(seed=0):
    out = dict(first_inputs(seed))
    for name, value in second_inputs(seed + 1).items():
        if name != "x":
            out[name + "_2"] = value
    return out


def reference(
    x, c, ctx, c_ctx, w_ada, b_ada, norm1_g, norm2_g, w_in, dw_kernel, dw_bias, conv_ln_g,
    conv_ln_b, rpb, w_out, w_mlp1, w_mlp2, final_g, norm_mix_2, w_in_2, w_up_a_2, w_up_b_2,
    w_out_2, norm_ffn_2, w_gate_2, w_up_2, w_down_2, norm_final_2,
):
    x = first_block(
        x, c, ctx, c_ctx, w_ada, b_ada, norm1_g, norm2_g, w_in, dw_kernel, dw_bias, conv_ln_g,
        conv_ln_b, rpb, w_out, w_mlp1, w_mlp2, final_g,
    )
    return second_block(
        x, norm_mix_2, w_in_2, w_up_a_2, w_up_b_2, w_out_2, norm_ffn_2, w_gate_2, w_up_2,
        w_down_2, norm_final_2,
    )


_drawn_inputs = setup_inputs


def setup_inputs(seed=0):
    import zlib

    import numpy as np

    out = dict(_drawn_inputs(seed))
    spreads = {}
    factors = {'norm1_g': 8.0,
     'norm2_g': 3.726,
     'dw_bias': 6.118,
     'conv_ln_g': 7.318,
     'conv_ln_b': 8.0,
     'rpb': 5.531,
     'norm_mix_2': 3.421,
     'norm_ffn_2': 4.065,
     'norm_final_2': 2.88}
    for name, (base, spread) in spreads.items():
        noise = np.random.default_rng([zlib.crc32(name.encode()), seed]).standard_normal(out[name].shape)
        drawn = base * np.exp(spread * noise) if base else spread * noise
        out[name] = __import__('jax').numpy.asarray(drawn.astype(out[name].dtype))
    for name, factor in factors.items():
        out[name] = (out[name] * factor).astype(out[name].dtype)
    return out
```

```python
import numpy as np
import concourse.bass as bass
from concourse import mybir
from contextlib import ExitStack

F32 = mybir.dt.float32
F32R = mybir.dt.float32r
ALU = mybir.AluOpType
ACT = mybir.ActivationFunctionType
AX = mybir.AxisListType

D = 1024
T = 256
NH = 8
EPS = 1e-6
NEG = -1e30
SENT = -3e38
IDX_SCALE = (64 ** -0.5) * (8 ** -0.5)
FF2 = 2816

KB = 1024
RW = 6
RH = 3
AHEAD = 2
UB = 8 * KB


def build_program(nc, d, out):
    ctx = ExitStack()
    with ctx:
        base = 16512

        def at(name, off_kb, shape, dt=F32):
            return nc.alloc_sbuf_tensor_at(name, shape, dt, offset=base + int(off_kb * KB))

        W32 = [at(f"W32_{i}", 8 * i, [128, 2048]) for i in range(RW)]
        WH = [at(f"WH_{i}", 48 + 8 * i, [128, 2048], F32R) for i in range(RH)]
        WL = [at(f"WL_{i}", 72 + 8 * i, [128, 2048], F32R) for i in range(RH)]
        X = at("X", 96, [128, 2, D])
        o = 104
        g1b = at("g1b", o, [128, D])
        g2b = at("g2b", o + 4, [128, D])
        lnC = at("lnC", o + 8, [128, 384])
        caus = at("caus", o + 9.5, [128, 384])
        rope1 = at("rope1", o + 11, [128, 2, 2, 64])
        rope2 = at("rope2", o + 12, [128, 2, 2, 64])
        ident = at("ident", o + 13, [128, 128])
        ones = at("ones", o + 13.5, [128, 128])
        vec = at("vec", o + 14, [128, 224])
        cs = at("cs", o + 15, [128, 16])
        mod1 = at("mod1", o + 15.125, [128, 16, 2])
        mod2 = at("mod2", o + 15.25, [128, 16, 2])
        A1 = at("A1", o + 15.375, [128, 2, 8])
        A2 = at("A2", o + 15.4375, [128, 8])
        stat = at("stat", o + 15.5, [128, 32])
        mneg = at("mneg", o + 15.625, [128, 64])
        lsum = at("lsum", o + 15.875, [128, 64])
        rl = at("rl", o + 16.125, [128, 64])
        best = at("best", o + 16.375, [128, 2, 8])
        ewi = at("wi", o + 16.5, [128, 2, 8])
        csb = at("csb", o + 16.6875, [128, 8, 32])
        m0 = 121.75

        def M(name, off, shape, dt=F32):
            return at(name, m0 + off, shape, dt)

        S1 = M("S1", 0, [128, 2, D])
        S2 = M("S2", 8, [128, 2048])
        AH = M("AH", 16, [128, 8, 256], F32R)
        AL = M("AL", 24, [128, 8, 256], F32R)
        CH = M("CH", 32, [128, 8, 256], F32R)
        CL = M("CL", 40, [128, 8, 256], F32R)
        rows1 = [M(f"rows1_{i}", 32 + 2 * i, [2, 512]) for i in range(4)]
        XC = M("XC", 48, [128, 2, D])
        Q = M("Q", 48, [128, 2, 512])
        Kt = M("Kt", 52, [128, 2, 512])
        V = M("V", 56, [128, 2, 512])
        KC = M("KC", 60, [128, 2, 512])
        VC = M("VC", 64, [128, 2, 512])
        U = M("U", 68, [128, 2, 512])
        G = M("G", 72, [128, 2, 512])
        cacc = M("cacc", 72, [128, 4, 256])
        ccen = M("ccen", 68, [128, 4, 256])
        hp = M("hp", 76, [128, 4, 288])
        csq = M("csq", 76, [128, 4, 256])
        tmp = M("tmp", 80.5, [128, 512])
        QR = M("QR", 0, [128, 2, 512])
        KR = M("KR", 4, [128, 2, 512])
        qrT = M("qrT", 32, [128, 4, 256])
        qT = M("qT", 36, [128, 4, 256])
        kT = M("kT", 40, [128, 4, 256])
        kcT = M("kcT", 44, [128, 4, 256])
        bias = [M(f"bias{i}", 8 + 2 * i, [128, 2, 256]) for i in range(4)]
        O1 = M("O1", 0, [128, 2, 512])
        rows2 = [M(f"rows2_{i}", 4 + 2 * i, [2, 512]) for i in range(2)]
        P1 = [M(f"P1_{i}", 48 + 2 * i, [128, 512]) for i in range(2)]
        PT1 = [M(f"PT1_{i}", 52 + 2 * i, [128, 512]) for i in range(2)]
        s1 = [M(f"s1_{i}", 60 + i, [128, 256]) for i in range(2)]
        crs = M("crs", 62, [128, 256])
        hid = [M(f"hid{i}", 32 + 4 * i, [128, 2, 512]) for i in range(2)]
        HH = [M(f"HH{i}", 40 + 4 * i, [128, 4, 256], F32R) for i in range(2)]
        HL = [M(f"HL{i}", 48 + 4 * i, [128, 4, 256], F32R) for i in range(2)]
        rel = [M(f"rel{i}", 56 + 2 * i, [128, 512]) for i in range(2)]
        raw = [M(f"raw{i}", 32 + 4 * i, [128, 2, 512]) for i in range(2)]
        rr = [M(f"rr{i}", 40 + 4 * i, [128, 2, 512]) for i in range(2)]
        qiT = M("qiT", 48, [128, 4, 256])
        qbT = M("qbT", 52, [128, 4, 256])
        qaT = M("qaT", 56, [128, 4, 256])
        kaT = M("kaT", 60, [128, 4, 256])
        va = M("va", 64, [128, 2, 512])
        kiT = M("kiT", 68, [128, 256])
        kbT = M("kbT", 69, [128, 256])
        small = M("small", 70, [128, 2, 200])
        skk = [M(f"skk{i}", 72 + i, [128, 2, 128]) for i in range(2)]
        Ob = M("Ob", 74, [128, 2, 512])
        mB = M("mB", 78, [128, 384])
        P2 = [M(f"P2_{i}", 1.5 * i, [128, 384]) for i in range(2)]
        PT2 = [M(f"PT2_{i}", 3 + 1.5 * i, [128, 384]) for i in range(2)]
        s2 = [M(f"s2_{i}", 6 + 1.5 * i, [128, 384]) for i in range(2)]
        rlu = [M(f"rlu{i}", 9 + 1.5 * i, [128, 384]) for i in range(2)]
        Oa = M("Oa", 12, [128, 2, 512])
        sco = M("sco", 74, [128, 384])
        ga = M("ga", 32, [128, 2, D])
        gb = M("gb", 40, [128, 2, D])
        YH = [M(f"YH{i}", 48 + 8 * i, [128, 4, 256], F32R) for i in range(2)]
        YL = [M(f"YL{i}", 52 + 8 * i, [128, 4, 256], F32R) for i in range(2)]
        mrg = M("mrg", 0, [128, 2, D])
        mt = [M(f"mt{i}", 64 + 2 * i, [128, 512]) for i in range(2)]

        bank = [ctx.enter_context(nc.psum_tensor(f"bank{i}", [128, 512], F32)) for i in range(8)]
        bfree = [[] for _ in range(8)]

        prog = {e: [] for e in ("pe", "act", "dve", "pool", "sp")}
        value = {}
        seen = {e: {} for e in prog}

        def waits_of(e, toks):
            need = {}
            todo = list(toks)
            while todo:
                t = todo.pop()
                if t is None:
                    continue
                if isinstance(t, list):
                    todo.extend(t)
                    continue
                need[t[0]] = max(need.get(t[0], 0), t[1])
            outw = []
            for s, v in need.items():
                if seen[e].get(s, 0) < v:
                    seen[e][s] = v
                    outw.append((s, v))
            return outw

        def op(e, fn, *toks, inc=True):
            w = waits_of(e, toks)
            if inc:
                value[e] = value.get(e, 0) + 1
            prog[e].append((w, fn, e if inc else None, 1))
            return (e, value.get(e, 0)) if inc else None

        def dma(e, dst, src, sem, *toks):
            w = waits_of(e, toks)
            value[sem] = value.get(sem, 0) + 16
            prog[e].append((w, lambda q, dst=dst, src=src: q.dma_start(dst, src), sem, 16))
            return (sem, value[sem])

        def pe(fn, *t, inc=True):
            return op("pe", fn, *t, inc=inc)

        def act(fn, *t):
            return op("act", fn, *t)

        def dve(fn, *t):
            return op("dve", fn, *t)

        def mm(o_, l, r, start, stop, *t, inc=False):
            return pe(lambda e: e.matmul(o_, l, r, start=start, stop=stop), *t, inc=inc)

        def copy(e, o_, i_, *t):
            if e == "act":
                return act(lambda q: q.activation(o_, i_, ACT.Copy), *t)
            return dve(lambda q: q.tensor_copy(o_, i_), *t)

        def tt(o_, a, b, alu, *t):
            return dve(lambda q: q.tensor_tensor(o_, a, b, alu), *t)

        def tsc(o_, a, s1_, s2_, a0, a1, *t):
            if a1 is None:
                return dve(lambda q: q.tensor_scalar(o_, a, s1_, None, a0), *t)
            return dve(lambda q: q.tensor_scalar(o_, a, s1_, s2_, a0, a1), *t)

        def stt(o_, a, s, b, a0, a1, *t):
            return dve(lambda q: q.scalar_tensor_tensor(o_, a, s, b, a0, a1), *t)

        units = []

        def add_unit(parts, raw_=False):
            units.append((parts, raw_))
            return len(units) - 1

        def unit_of(w, k0, nk, cols, raw_=False):
            wid = sum(c[1] for c in cols)
            parts, c0 = [], 0
            for n0, cw in cols:
                src = w[k0 * 128:(k0 + nk) * 128, n0:n0 + cw].rearrange("(k p) n -> p k n", p=128)
                parts.append((c0, cw, src))
                c0 += cw
            return add_unit((nk, wid, parts), raw_)

        rel_w32 = {}
        rel_hl = []
        unit_dma = {}
        unit_tok = {}
        unit_slot = {}
        state = {"l": 0, "s": 0}

        def w32_view(u):
            nk, wid, _ = units[u][0]
            return W32[u % RW][:, 0:nk * wid].rearrange("p (k n) -> p k n", k=nk)

        def pump(u):
            moved = True
            while moved:
                moved = False
                n = state["l"]
                if n < len(units) and (n < RW or (n - RW) in rel_w32):
                    (nk, wid, parts), _ = units[n]
                    v = w32_view(n)
                    for c0, cw, src in parts:
                        tk = dma("sp", v[:, :, c0:c0 + cw], src, f"w{n % RW}", rel_w32.get(n - RW))
                    unit_dma[n] = tk
                    state["l"] += 1
                    moved = True
                n = state["s"]
                if n < len(units) and n <= u + AHEAD and n in unit_dma:
                    if units[n][1]:
                        unit_tok[n] = [unit_dma[n]]
                        state["s"] += 1
                        moved = True
                        continue
                    k = len(unit_slot)
                    if k >= RH and len(rel_hl) <= k - RH:
                        continue
                    free = rel_hl[k - RH] if k >= RH else None
                    nk, wid, _ = units[n][0]
                    sl = k % RH
                    w, h, l = (x[:, 0:nk * wid] for x in (W32[n % RW], WH[sl], WL[sl]))
                    a = act(lambda q, h=h, w=w: q.activation(h, w, ACT.Copy), unit_dma[n], free)
                    b = tt(l, w, h.bitcast(F32), ALU.subtract, a, unit_dma[n], free)
                    unit_slot[n] = sl
                    unit_tok[n] = [a, b]
                    rel_w32[n] = [a, b]
                    state["s"] += 1
                    moved = True

        def unit(u, targets, after=None):
            pump(u)
            nk, wid, _ = units[u][0]
            sl = unit_slot[u]
            wh = WH[sl][:, 0:nk * wid].rearrange("p (k n) -> p k n", k=nk)
            wl = WL[sl][:, 0:nk * wid].rearrange("p (k n) -> p k n", k=nk)
            done = []
            for H, L, k0, tb, bk, (c0, cw), first, last, tk in targets:
                w = [unit_tok[u], tk] + ([bfree[bk]] if first else [])
                for k in range(nk):
                    hs = H[:, k0 + k, tb * 128:tb * 128 + 128]
                    ls = L[:, k0 + k, tb * 128:tb * 128 + 128]
                    po = bank[bk][:, 0:cw]
                    f = first and k == 0
                    e = last and k == nk - 1
                    mm(po, hs, wh[:, k, c0:c0 + cw], f, False, w)
                    mm(po, hs, wl[:, k, c0:c0 + cw], False, False)
                    tok = mm(po, ls, wh[:, k, c0:c0 + cw], False, e, inc=(k == nk - 1))
                    w = []
                if first:
                    bfree[bk] = []
                done.append(tok)
            rel_hl.append(done[-1])
            if after:
                after()
            return done

        wada, win, wout, wm1, wm2 = (d[n] for n in ("w_ada", "w_in", "w_out", "w_mlp1", "w_mlp2"))
        win2, wua, wub, wout2, wg, wu, wd = (d[n] for n in (
            "w_in_2", "w_up_a_2", "w_up_b_2", "w_out_2", "w_gate_2", "w_up_2", "w_down_2"))

        def col_units(w, cols, kt=8, raw_=False):
            return [unit_of(w, k0, 4, cols, raw_) for k0 in range(0, kt, 4)]

        u_ada1 = [col_units(wada, [(512 * n, 512)], raw_=True) for n in range(4)]
        u_in = {}
        for nm, c0 in (("a", 1536), ("b", 2048), ("k", 512), ("q", 0), ("v", 1024)):
            u_in[nm] = col_units(win, [(c0, 512)])
        u_ada2 = [(nm, n, col_units(wada, [(c0 + 512 * n, 512)], raw_=True))
                  for nm, c0 in (("sh", 3072), ("sc", 4096), ("g1", 2048), ("g2", 5120)) for n in range(2)]
        u_out = [col_units(wout, [(512 * n, 512)]) for n in range(2)]
        u_m1, u_m2 = [], []
        for c in range(8):
            u_m1.append(col_units(wm1, [(512 * c, 512)]))
            if c:
                u_m2.append([unit_of(wm2, 4 * (c - 1) + 2 * j, 2, [(0, 1024)]) for j in range(2)])
        u_m2.append([unit_of(wm2, 28 + 2 * j, 2, [(0, 1024)]) for j in range(2)])
        u_in2 = {}
        for nm, cols in (("s", [(2048, 128), (2688, 72)]), ("qi", [(2176, 512)]), ("qb", [(1536, 512)]),
                         ("qa", [(0, 512)]), ("ka", [(512, 512)]), ("va", [(1024, 512)]),
                         ("ga0", [(2760, 512)]), ("ga1", [(3272, 512)]), ("gb0", [(3784, 512)]),
                         ("gb1", [(4296, 512)])):
            u_in2[nm] = col_units(win2, cols)
        u_upa = [unit_of(wua, 0, 4, [(512 * n, 512)]) for n in range(2)]
        u_upb = [unit_of(wub, 0, 4, [(512 * n, 512)]) for n in range(2)]
        u_out2 = [col_units(wout2, [(512 * n, 512)]) for n in range(2)]
        u_gu, u_dn = [], []
        for c in range(11):
            u_gu.append(None)
            u_dn.append(None)
        for c in range(12):
            if c < 11:
                u_gu[c] = []
                for k0 in (0, 4):
                    sg = wg[k0 * 128:(k0 + 4) * 128, 256 * c:256 * c + 256].rearrange("(k p) n -> p k n", p=128)
                    su = wu[k0 * 128:(k0 + 4) * 128, 256 * c:256 * c + 256].rearrange("(k p) n -> p k n", p=128)
                    u_gu[c].append(add_unit((4, 512, [(0, 256, sg), (256, 256, su)])))
            if c:
                u_dn[c - 1] = [unit_of(wd, 2 * (c - 1), 2, [(0, 1024)])]

        def tokmaj(ap):
            return ap.rearrange("(t p) n -> p t n", p=128)

        t_vec = dma("pool", vec[:, :], d["vec"], "d_vec")
        t_cs = dma("pool", cs[:, :], d["cs"], "d_cs")
        t_x = dma("pool", X[:, :, :], tokmaj(d["x"]), "d_x")
        t_ident = dma("pool", ident[:, :], d["ident"], "d_id")
        t_xc = dma("pool", XC[:, :, :], tokmaj(d["ctx"]), "d_xc")
        t_rope1 = dma("pool", rope1[:, :, :, :], d["rope1"], "d_r1")
        t_rope2 = dma("pool", rope2[:, :, :, :], d["rope2"], "d_r2")
        t_lnC = dma("pool", lnC[:, :], d["lnC"], "d_lc")
        t_caus = dma("pool", caus[:, :], d["caus"], "d_ca")
        bada = d["b_ada"]
        t_g1 = dma("pool", g1b[:, :], bada[0:1, 2048:3072].to_broadcast([128, D]), "d_g1")
        t_g2 = dma("pool", g2b[:, :], bada[0:1, 5120:6144].to_broadcast([128, D]), "d_g2")
        t_ones = op("pool", lambda q: q.memset(ones[:, :], 1.0))
        t_onesm = t_ones
        v_n1, v_n2, v_b1, v_b2 = vec[:, 0:8], vec[:, 8:16], vec[:, 16:32], vec[:, 32:48]
        v_dw = vec[:, 48:172].rearrange("p (c j) -> p c j", c=4)
        v_dwb, v_lng, v_lnb = vec[:, 172:176], vec[:, 176:180], vec[:, 180:184]
        v_mix, v_ffn = vec[:, 184:192], vec[:, 192:200]
        t_eps = dve(lambda q: q.memset(stat[:, 30:31], -0.5))
        t_eps2 = dve(lambda q: q.memset(stat[:, 31:32], EPS))

        t_cs = act(lambda q: q.activation(cs[:, :], cs[:, :], ACT.Silu), t_cs)
        csv = cs[:, :].rearrange("p (k r) -> p k r", r=2)

        tq = {"n": 0}

        def tbank():
            b = 6 + tq["n"] % 2
            tq["n"] += 1
            w = bfree[b]
            bfree[b] = []
            return b, w

        def transposes(blocks, *toks):
            b, w = tbank()
            for i, (c, src) in enumerate(blocks):
                dst = bank[b][:, c * 128:c * 128 + 128]
                tk = pe(lambda e, dst=dst, src=src: e.transpose(dst, src, ident[:, :]),
                        w, list(toks), t_ident, inc=(i == len(blocks) - 1))
            return b, tk

        def to_features(src, nj, dst, eng, *toks):
            outt, pet = [], []
            for j in range(0, nj, 2):
                n = min(2, nj - j)
                b, tk = transposes([(2 * i + tb, src[:, tb, (j + i) * 128:(j + i) * 128 + 128])
                                    for i in range(n) for tb in range(2)], *toks)
                pv = bank[b][:, 0:n * 256].rearrange("p (j n) -> p j n", j=n)
                t = copy(eng[(j // 2) % len(eng)], dst[:, j:j + n, :], pv, tk)
                bfree[b] = [t]
                outt.append(t)
                pet.append(tk)
            return outt, pet

        def split_bank(b, tk, H, L, n, *toks):
            pv = bank[b][:, 0:n]
            a = act(lambda q: q.activation(H, pv, ACT.Copy), tk, list(toks))
            c = tt(L, pv, H.bitcast(F32), ALU.subtract, a, tk, list(toks))
            bfree[b] = [c]
            return [a, c]

        def flat(ap):
            return ap.rearrange("p a b -> p (a b)")

        def to_split(src, nj, H, L, k0, *toks):
            outt, pet = [], []
            for j in range(0, nj, 2):
                b, tk = transposes([(2 * i + tb, src[:, tb, (j + i) * 128:(j + i) * 128 + 128])
                                    for i in range(2) for tb in range(2)], *toks)
                outt += [split_bank(b, tk, flat(H[:, k0 + j:k0 + j + 2, :]), flat(L[:, k0 + j:k0 + j + 2, :]), 512)] * 2
                pet.append(tk)
            return outt, pet

        nstat = {"n": 0}

        def rstd(src, ready, junk, *free):
            res = []
            for tb in range(2):
                c = nstat["n"]
                nstat["n"] = (c + 1) % 14
                a = act(lambda q, tb=tb, c=c: q.activation(junk[:, tb, :], src[:, tb, :], ACT.Square,
                                                          accum_out=stat[:, 2 * c:2 * c + 1]),
                        ready[tb], list(free))
                m = tsc(stat[:, 2 * c + 1:2 * c + 2], stat[:, 2 * c:2 * c + 1], 1.0 / D, EPS, ALU.mult, ALU.add, a)
                p = op("pool", lambda q, c=c: q.tensor_tensor(stat[:, 2 * c:2 * c + 1], stat[:, 2 * c + 1:2 * c + 2],
                                                              stat[:, 30:31], ALU.pow), m, t_eps)
                res.append((stat[:, 2 * c:2 * c + 1], p))
            return res

        s2v = S2[:, :].rearrange("p (a b) -> p a b", a=2)
        hTv = S2[:, :].rearrange("p (k t) -> p k t", k=8)

        def norm(src, ready, H, L, Av, Bv, *free):
            rs = rstd(src, ready, s2v, *free)
            tx = [tsc(S1[:, tb, :], src[:, tb, :], rs[tb][0], None, ALU.mult, None, rs[tb][1], list(free))
                  for tb in range(2)]
            toks = []
            for i in range(4):
                b, tk = transposes([(2 * j + tb, S1[:, tb, (2 * i + j) * 128:(2 * i + j) * 128 + 128])
                                    for j in range(2) for tb in range(2)], tx)
                ev = []
                for j in range(2):
                    kt = 2 * i + j
                    o_, p_ = hTv[:, kt, :], bank[b][:, j * 256:j * 256 + 256]
                    A_ = Av[:, kt:kt + 1]
                    B_ = Bv[:, kt:kt + 1] if Bv is not None else 0.0
                    if i % 2 == 0:
                        ev.append(act(lambda q, o_=o_, p_=p_, A_=A_, B_=B_: q.activation(
                            o_, p_, ACT.Identity, bias=B_, scale=A_), tk, list(free)))
                    elif Bv is not None:
                        ev.append(tsc(o_, p_, A_, B_, ALU.mult, ALU.add, tk, list(free)))
                    else:
                        ev.append(tsc(o_, p_, A_, None, ALU.mult, None, tk, list(free)))
                bfree[b] = ev
                hv, lv = flat(H[:, 2 * i:2 * i + 2, :]), flat(L[:, 2 * i:2 * i + 2, :])
                sv = flat(hTv[:, 2 * i:2 * i + 2, :])
                a = copy("act" if i % 2 else "dve", hv, sv, ev, list(free))
                c = tt(lv, sv, hv.bitcast(F32), ALU.subtract, a, ev, list(free))
                toks += [[a, c]] * 2
            return toks, tx

        def pairs(ktoks, k0, n):
            return [ktoks[k] for k in range(k0, k0 + n)]

        def chunk(us, stats, width=512, after=None):
            for i, u in enumerate(us):
                nk = units[u][0][0]
                targets = [(H, L, nk * i, tb, bk[tb], (0, width), i == 0, i == len(us) - 1,
                            pairs(kt, nk * i, nk))
                           for H, L, kt, bk in stats for tb in range(2)]
                res = unit(u, targets, after)
            return res

        def raw_unit(u, lhs_of, bk, rows, first, last, *toks):
            pump(u)
            v = w32_view(u)
            w = [unit_tok[u], list(toks)] + ([bfree[bk]] if first else [])
            if first:
                bfree[bk] = []
            nk = units[u][0][0]
            for k in range(nk):
                tk = mm(bank[bk][0:rows, :], lhs_of(k), v[:, k, :], first and k == 0, last and k == nk - 1,
                        w, inc=(k == nk - 1))
                w = []
            rel_w32[u] = [tk]
            return tk

        rt = []
        for n in range(4):
            for i in range(2):
                tk = raw_unit(u_ada1[n][i], lambda k, i=i: csv[:, 4 * i + k, :], n, 2, i == 0, i == 1, t_cs)
            t = copy("act" if n % 2 else "dve", rows1[n][:, :], bank[n][0:2, :], tk)
            bfree[n] = [t]
            rt.append(t)
        b, w = tbank()
        for n in range(4):
            for j in range(4):
                c = (4 * n + j) * 2
                tk = mm(bank[b][:, c:c + 2], rows1[n][:, j * 128:j * 128 + 128], ident[0:2, 0:2], True, True,
                        rt[n], t_ident, w, inc=(n == 3 and j == 3))
        t_mod1 = tt(mod1[:, :, :], bank[b][:, 0:32].rearrange("p (k r) -> p k r", r=2),
                    v_b1.unsqueeze(2).to_broadcast([128, 16, 2]), ALU.add, tk, t_vec)
        bfree[b] = [t_mod1]
        B1 = []
        t_A1 = []
        for r in range(2):
            t_A1.append(stt(A1[:, r, :], mod1[:, 8:16, r], 1.0, v_n1, ALU.add, ALU.mult, t_mod1, t_vec))
            B1.append(mod1[:, :, r])
        modB = at("modB", 104 + 17.6875, [128, 2, 8])
        t_B = [dve(lambda q, r=r: q.tensor_copy(modB[:, r, :], mod1[:, 0:8, r]), t_mod1) for r in range(2)]

        kx, tx_x = norm(X, [[t_x], [t_x]], AH, AL, A1[:, 0, :], modB[:, 0, :], t_A1, t_B)
        ra = chunk(u_in["a"], [(AH, AL, kx, (0, 1))])
        kc, tx_c = norm(XC, [[t_xc], [t_xc]], CH, CL, A1[:, 1, :], modB[:, 1, :], t_A1, t_B,
                        kx, rt, ("pe", value["pe"]))
        rb = chunk(u_in["b"], [(AH, AL, kx, (2, 3))])
        tu = []
        for tb in range(2):
            s = act(lambda q, tb=tb: q.activation(G[:, tb, :], bank[2 + tb][:, :], ACT.Sigmoid), rb[tb])
            bfree[2 + tb] = [s]
            t = tt(U[:, tb, :], bank[tb][:, :], G[:, tb, :], ALU.mult, s, ra[tb])
            bfree[tb] = [t]
            tu.append(t)
        t_z = op("pool", lambda q: q.memset(hp[:, :, 0:15], 0.0))
        t_z = op("pool", lambda q: q.memset(hp[:, :, 271:288], 0.0), t_z)
        t_hp = []
        for j in range(0, 4, 2):
            b, tk = transposes([(2 * i + tb, U[:, tb, (j + i) * 128:(j + i) * 128 + 128])
                                for i in range(2) for tb in range(2)], tu)
            t = copy("act", hp[:, j:j + 2, 15:271], bank[b][:, :].rearrange("p (j n) -> p j n", j=2), tk)
            bfree[b] = [t]
            t_hp.append(t)

        conv_last = [None] * 4

        def conv():
            for j in range(31):
                for c in range(4):
                    src = hp[:, c, j:j + 256]
                    if j == 0:
                        conv_last[c] = tsc(cacc[:, c, :], src, v_dw[:, c, 0:1], v_dwb[:, c:c + 1], ALU.mult, ALU.add,
                                           t_hp, t_z, tu, t_vec)
                    else:
                        conv_last[c] = stt(cacc[:, c, :], src, v_dw[:, c, j:j + 1], cacc[:, c, :],
                                           ALU.mult, ALU.add, conv_last[c])
                    yield

        bg = [conv()]

        def background(n):
            def go():
                for _ in range(n):
                    while bg:
                        try:
                            next(bg[0])
                            break
                        except StopIteration:
                            bg.pop(0)
            return go

        def tm(b_, o_, e, scale, tk, *toks):
            pv, = (bank[b_][:, :],)
            if e == "act":
                t = act(lambda q: q.activation(o_, pv, ACT.Copy, scale=scale), tk, list(toks))
            elif scale == 1.0:
                t = dve(lambda q: q.tensor_copy(o_, pv), tk, list(toks))
            else:
                t = tsc(o_, pv, scale, None, ALU.mult, None, tk, list(toks))
            bfree[b_] = [t]
            return t

        def rope(dst, src, nh, tab, s, tb, ready, *free):
            cosv = tab[:, tb, 0, :].unsqueeze(1).to_broadcast([128, nh, 64])
            sv = src.rearrange("p (h e) -> p h e", e=64) if nh > 2 else src
            dv = dst.rearrange("p (h e) -> p h e", e=64)
            t1 = tt(dv, sv, cosv, ALU.mult, ready, list(free))
            tv = tmp[:, 0:nh * 64].rearrange("p (h e) -> p h e", e=64)
            t2 = []
            for lo in range(0, 64, 2 * s):
                for x, y in ((lo, lo + s), (lo + s, lo)):
                    snv = tab[:, tb, 1, x:x + s].unsqueeze(1).to_broadcast([128, nh, s])
                    t2.append(tt(tv[:, :, x:x + s], sv[:, :, y:y + s], snv, ALU.mult, ready, list(free)))
            return tt(dv, dv, tv, ALU.add, t1, t2)

        rk = chunk(u_in["k"], [(AH, AL, kx, (0, 1)), (CH, CL, kc, (4, 5))], after=background(16))
        cdone = [tx_c, ("pe", value["pe"])]
        tk_ = [tm(tb, Kt[:, tb, :], "act", 1.0, rk[tb], tx_c) for tb in range(2)]
        tkc = [tm(4 + tb, KC[:, tb, :], "act", 1.0, rk[2 + tb]) for tb in range(2)]
        rq = chunk(u_in["q"], [(AH, AL, kx, (2, 3))], after=background(12))
        tq_ = [tm(2 + tb, Q[:, tb, :], "act", 0.125, rq[tb], tx_c) for tb in range(2)]
        tkr = []
        prev = None
        for tb in range(2):
            prev = rope(KR[:, tb, :], Kt[:, tb, :], 8, rope1, 16, tb, [tk_[tb], t_rope1], prev, kc, tx_c,
                        ("pe", value["pe"]))
            tkr.append(prev)
        rv = chunk(u_in["v"], [(AH, AL, kx, (0, 1)), (CH, CL, kc, (4, 5))], after=background(18))
        tv_ = [tm(tb, V[:, tb, :], "act", 1.0, rv[tb], tx_c) for tb in range(2)]
        tvc = [tm(4 + tb, VC[:, tb, :], "dve", 1.0, rv[2 + tb]) for tb in range(2)]
        gdone = ("pe", value["pe"])
        tqr = []
        for tb in range(2):
            prev = rope(QR[:, tb, :], Q[:, tb, :], 8, rope1, 16, tb, [tq_[tb], t_rope1], prev)
            tqr.append(prev)
        background(200)()

        ada2 = []

        def ada_steps():
            for i8, (nm, n, us) in enumerate(u_ada2):
                bk = 4 + i8 % 2
                for i in range(2):
                    if nm in ("sh", "sc"):
                        tk = raw_unit(us[i], lambda k, i=i: csv[:, 4 * i + k, :], bk, 2, i == 0, i == 1, t_cs)
                    else:
                        tk = raw_unit(us[i], lambda k, i=i: csv[:, 4 * i + k, 0:1].to_broadcast([128, 128]), bk, 128,
                                      i == 0, i == 1, t_cs)
                    if i == 0:
                        yield
                if nm in ("sh", "sc"):
                    r2 = rows2[n]
                    t = copy("act", r2[:, :], bank[bk][0:2, :], tk, rows2_free[n])
                    bfree[bk] = [t]
                    b, w = tbank()
                    for j in range(4):
                        tk = mm(bank[b][:, 2 * j:2 * j + 2], r2[:, j * 128:j * 128 + 128], ident[0:2, 0:2],
                                True, True, t, w, inc=(j == 3))
                    rows2_free[n] = [tk]
                    k0 = (0 if nm == "sh" else 8) + 4 * n
                    t = tt(mod2[:, k0:k0 + 4, :], bank[b][:, 0:8].rearrange("p (k r) -> p k r", r=2),
                           v_b2[:, k0:k0 + 4].unsqueeze(2).to_broadcast([128, 4, 2]), ALU.add, tk)
                    bfree[b] = [t]
                    ada2.append(t)
                else:
                    gt, tg = (g1b, t_g1) if nm == "g1" else (g2b, t_g2)
                    gv = gt[:, 512 * n:512 * n + 512]
                    t = tt(gv, bank[bk][:, :], gv, ALU.add, tk, tg)
                    bfree[bk] = [t]
                    ada2.append(t)
                yield

        rows2_free = [[tkr, tqr], [tkr, tqr]]
        ada = ada_steps()

        def fill(n=1):
            for _ in range(n):
                next(ada, None)

        e1, p1 = to_features(KR, 4, kT, ["act", "dve"], tkr, gdone)
        e2, p2 = to_features(KC, 4, kcT, ["act", "dve"], tkc, gdone)
        e3, p3 = to_features(Q, 4, qT, ["act", "dve"], tq_, gdone)
        e4, p4 = to_features(QR, 4, qrT, ["act", "dve"], tqr, gdone)
        rows2_free[0] = rows2_free[1] = [p1]
        t_qk = [e1, e2, e3, e4]
        t_pqk = [p1, p2, p3, p4]

        fill(1)
        b, w = tbank()
        for c in range(4):
            tk = mm(bank[b][:, 0:256], ones[:, :], cacc[:, c, :], c == 0, c == 3, w, conv_last, t_ones, inc=(c == 3))
        mu = bank[b]
        t = []
        for c in range(4):
            t.append(stt(ccen[:, c, :], mu[:, 0:256], -1.0 / 512, cacc[:, c, :], ALU.mult, ALU.add, tk, conv_last,
                         tu, t_hp))
        bfree[b] = t
        t_cc = t
        tsq = act(lambda q: q.activation(csq[:, :, :], ccen[:, :, :], ACT.Square), t_cc, conv_last)
        fill(1)
        b, w = tbank()
        for c in range(4):
            tk = mm(bank[b][:, 0:256], ones[:, :], csq[:, c, :], c == 0, c == 3, w, tsq, inc=(c == 3))
        var = bank[b]
        t = act(lambda q: q.activation(crs[:, :], var[:, 0:256], ACT.Sqrt, bias=stat[:, 31:32], scale=1.0 / 512),
                tk, t_eps2, p2)
        bfree[b] = [t]
        t = dve(lambda q: q.reciprocal(crs[:, :], crs[:, :]), t)
        t = tt(ccen[:, :, :], ccen[:, :, :], crs[:, :].unsqueeze(1).to_broadcast([128, 4, 256]), ALU.mult, t, tsq)
        tn = [act(lambda q, c=c: q.activation(cacc[:, c, :], ccen[:, c, :], ACT.Silu, bias=v_lnb[:, c:c + 1],
                                              scale=v_lng[:, c:c + 1]), t) for c in range(4)]
        ch = act(lambda q: q.activation(flat(AH[:, 4:8, :]), flat(cacc[:, :, :]), ACT.Copy), tn, gdone)
        cl = tt(flat(AL[:, 4:8, :]), flat(cacc[:, :, :]), flat(AH[:, 4:8, :]).bitcast(F32), ALU.subtract, ch, tn, gdone)
        k_conv = [[ch, cl]] * 4

        bias_free = [[prev, tkr, kc]] * 4
        bias_tok = {}

        def load_bias(h):
            if h < NH:
                bias_tok[h] = dma("pool", bias[h % 4][:, :, :], tokmaj(d["rpb"][h]), f"d_b{h % 4}", bias_free[h % 4])

        for h in range(4):
            load_bias(h)
        its = [(h, tb) for h in range(NH) for tb in range(2)]
        st = {}

        def scores1(n):
            h, tb = its[n]
            b = n % 2
            r = slice(64 * (h % 2), 64 * (h % 2) + 64)
            w = bfree[b]
            bfree[b] = []
            mm(bank[b][:, 0:256], qrT[r, h // 2, tb * 128:tb * 128 + 128], kT[r, h // 2, :], True, True, w, t_qk)
            st["s", n] = mm(bank[b][:, 256:512], qT[r, h // 2, tb * 128:tb * 128 + 128], kcT[r, h // 2, :],
                            True, True, inc=True)

        pv_tok = {}
        pe_tr = {}
        obank = (2, 3)

        def soft1(n):
            h, tb = its[n]
            b = n % 2
            m1, m2, mg = mneg[:, 2 * n:2 * n + 1], mneg[:, 2 * n + 1:2 * n + 2], rl[:, 16 + n:17 + n]
            a = dve(lambda q: q.reduce_max(m1, bank[b][:, 256:512], AX.X), st["s", n])
            bt = bias[h % 4][:, tb, :]
            a = dve(lambda q: q.tensor_tensor_reduce(out=s1[b][:, :], in0=bank[b][:, 0:256], in1=bt, scale=1.0,
                                                     scalar=m1, op0=ALU.add, op1=ALU.max, accum_out=m2),
                    a, bias_tok[h], t_pqk, st.get(("e", n - 2)))
            bias_free[h % 4] = [a]
            g = tsc(mg, m2, -1.0, None, ALU.mult, None, a)
            e1_ = act(lambda q: q.activation(P1[b][:, 0:256], s1[b][:, :], ACT.Exp, bias=mg,
                                             accum_out=lsum[:, 2 * n:2 * n + 1]), g, t_pqk, pe_tr.get(n - 2))
            e2_ = act(lambda q: q.activation(P1[b][:, 256:512], bank[b][:, 256:512], ACT.Exp, bias=mg,
                                             accum_out=lsum[:, 2 * n + 1:2 * n + 2]), g, pe_tr.get(n - 2))
            bfree[b] = [a, e2_]
            st["e", n] = [e1_, e2_]

        def turn1(n):
            b, tk = transposes([(i, P1[n % 2][:, i * 128:i * 128 + 128]) for i in range(4)], st["e", n])
            pe_tr[n] = tk
            t = copy("act" if n % 2 else "dve", PT1[n % 2][:, :], bank[b][:, :], tk, pv_tok.get(n - 2), t_pqk)
            bfree[b] = [t]
            st["t", n] = t

        def pv1(n):
            h, tb = its[n]
            ob = obank[tb]
            w = [st["t", n], tv_, tvc]
            if h == 0:
                w.append(bfree[ob])
                bfree[ob] = []
            for i in range(4):
                vv = (V if i < 2 else VC)[:, i % 2, h * 64:h * 64 + 64]
                tk = mm(bank[ob][:, h * 64:h * 64 + 64], PT1[n % 2][:, i * 128:i * 128 + 128], vv, i == 0, i == 3,
                        w, inc=(i == 3))
            pv_tok[n] = tk

        scores1(0)
        for n in range(16):
            soft1(n)
            if n + 1 < 16:
                scores1(n + 1)
            fill(1)
            if n:
                pv1(n - 1)
            turn1(n)
            if n % 2 == 1:
                load_bias(n // 2 + 4)
        pump(u_out[0][0] - AHEAD)
        pv1(15)
        fill(20)
        n16 = lsum[:, 0:32].rearrange("p (n r) -> p n r", r=2)
        t = tt(rl[:, 32:48], n16[:, :, 0], n16[:, :, 1], ALU.add, st["e", 15])
        t_rl = dve(lambda q: q.reciprocal(rl[:, 48:64], rl[:, 32:48]), t)
        rlv = rl[:, 48:64].rearrange("p (h t) -> p h t", t=2)

        def o_out(O_, ob, tb, rv_, *toks):
            t = tt(O_[:, tb, :].rearrange("p (h e) -> p h e", e=64),
                   bank[ob][:, :].rearrange("p (h e) -> p h e", e=64),
                   rv_.unsqueeze(2).to_broadcast([128, 8, 64]), ALU.mult, list(toks))
            bfree[ob] = [t]
            return t

        t_o = [o_out(O1, 2 + tb, tb, rlv[:, :, tb], t_rl, pv_tok[14 + tb], t_pqk) for tb in range(2)]
        t_A2 = stt(A2[:, :], mod2[:, 8:16, 0], 1.0, v_n2, ALU.add, ALU.mult, ada2)
        t_B2 = dve(lambda q: q.tensor_copy(modB[:, 0, :], mod2[:, 0:8, 0]), ada2, kx)

        k_att, _ = to_split(O1, 4, AH, AL, 0, t_o, gdone)
        k_a2 = k_att + k_conv
        ready = [[t_x], [t_x]]
        for n in range(2):
            r = []
            for i in (1, 0):
                pass
            r = chunk(u_out[n], [(AH, AL, k_a2, (2 * n, 2 * n + 1))])
            for tb in range(2):
                xv = X[:, tb, 512 * n:512 * n + 512]
                yv = S1[:, tb, 512 * n:512 * n + 512]
                t = tt(yv, bank[2 * n + tb][:, :], g1b[:, 512 * n:512 * n + 512], ALU.mult, r[tb], ada2, t_o, k_att)
                bfree[2 * n + tb] = [t]
                t = tt(xv, xv, yv, ALU.add, t, tx_x)
                ready[tb] = ready[tb] + [t]
        wo_pe = ("pe", value["pe"])
        t_fg = dma("pool", g1b[:, :], d["final_g"].to_broadcast([128, D]), "d_fg", ready)

        kh, tx_h = norm(X, ready, AH, AL, A2[:, :], modB[:, 0, :], t_A2, t_B2, wo_pe, ready)
        hfree = [[wo_pe, t_qk, st["e", 15], pv_tok], [wo_pe]]
        hid_free = [[wo_pe], [wo_pe]]
        hh_free = [[wo_pe], [wo_pe]]
        attn_done = [pv_tok[15], pv_tok[14], p4]
        hh_tok = {}

        def up1(c):
            r = chunk(u_m1[c], [(AH, AL, kh, (4, 5))])
            ts = []
            for tb in range(2):
                rv_ = rel[tb][:, :]
                a = act(lambda q, rv_=rv_, tb=tb: q.activation(rv_, bank[4 + tb][:, :], ACT.Relu), r[tb],
                        st.get(("sq", tb)), attn_done)
                bfree[4 + tb] = [a]
                s = act(lambda q, rv_=rv_, tb=tb, c=c: q.activation(hid[c % 2][:, tb, :], rv_, ACT.Square), a,
                        hid_free[c % 2], attn_done)
                st["sq", tb] = s
                ts.append(s)
            st["hid", c] = ts

        def turn_hid(c, nj):
            hh_tok[c], pet = to_split(hid[c % 2], nj, HH[c % 2], HL[c % 2], 0, st["hid", c], hh_free[c % 2], attn_done)
            hid_free[c % 2] = pet

        def down(us, c, first, last):
            for j, u in enumerate(us):
                targets = [(HH[c % 2], HL[c % 2], 2 * j, tb, 2 * n + tb, (512 * n, 512), first and j == 0,
                            last and j == len(us) - 1, pairs(hh_tok[c], 2 * j, 2))
                           for n in range(2) for tb in range(2)]
                r = unit(u, targets)
            hh_free[c % 2] = [r[-1]]
            return r

        for c in range(8):
            up1(c)
            if c:
                down(u_m2[c - 1], c - 1, c == 1, False)
            turn_hid(c, 4)
        r = down(u_m2[7], 7, False, True)
        xr = [[], []]
        for n in range(2):
            for tb in range(2):
                xv = X[:, tb, 512 * n:512 * n + 512]
                yv = S1[:, tb, 512 * n:512 * n + 512]
                t = tt(yv, bank[2 * n + tb][:, :], g2b[:, 512 * n:512 * n + 512], ALU.mult, r[2 * n + tb], ada2, kh)
                bfree[2 * n + tb] = [t]
                xr[tb].append(tt(xv, xv, yv, ALU.add, t, ready[tb], tx_h))
        t_nf = dma("pool", g2b[:, :], d["norm_final"].to_broadcast([128, D]), "d_nf", xr)
        gdone2 = ("pe", value["pe"])
        rs = rstd(X, xr, s2v, kh)
        xr = [[stt(X[:, tb, :], X[:, tb, :], rs[tb][0], g1b[:, :], ALU.mult, ALU.mult, rs[tb][1], t_fg)]
              for tb in range(2)]

        k2, tx_2 = norm(X, xr, AH, AL, v_mix, None, gdone2, xr, kh)
        hfin = [hh_tok[7], hh_tok[6], gdone2]

        r = chunk(u_in2["s"], [(AH, AL, k2, (0, 1))], width=200)
        t_sm = []
        for tb in range(2):
            t = act(lambda q, tb=tb: q.activation(small[:, tb, :], bank[tb][:, 0:200], ACT.Copy), r[tb], hfin)
            bfree[tb] = [t]
            t_sm.append(t)
        prev = None
        t_kk = []
        for i, c0 in ((0, 0), (1, 128)):
            for tb in range(2):
                src = small[:, tb, c0:c0 + 64].unsqueeze(1).to_broadcast([128, 2, 64])
                prev = rope(skk[i][:, tb, :], src, 2, rope2, 32, tb, [t_sm, t_rope2], prev)
                t_kk.append(prev)
        t_kiT = []
        for i, dst in ((1, kiT), (0, kbT)):
            b, tk = transposes([(tb, skk[i][:, tb, :]) for tb in range(2)], t_kk)
            t = copy("act", dst[:, :], bank[b][:, 0:256], tk, hfin)
            bfree[b] = [t]
            t_kiT.append(t)
        rawf = [[hfin], [hfin]]
        rrf = [[hfin], [hfin]]
        cnt = {"n": 0}

        def project(nm, dst, scale, after=None):
            nonlocal prev
            i = cnt["n"] % 2
            cnt["n"] += 1
            bk = (0, 1) if i else (2, 3)
            r = chunk(u_in2[nm], [(AH, AL, k2, bk)], after=after)
            ts = []
            for tb in range(2):
                t = tm(bk[tb], raw[i][:, tb, :], "act", scale, r[tb], rawf[i])
                prev = rope(rr[i][:, tb, :], raw[i][:, tb, :], 8, rope2, 32, tb, [t], prev, rrf[i])
                ts.append(prev)
            rawf[i] = ts
            return i, ts

        def turn_proj(it, dst):
            i, ts = it
            e_, p_ = to_features(rr[i], 4, dst, ["act", "dve"], ts, hfin)
            rrf[i] = p_
            return e_

        it_qi = project("qi", qiT, 1.0)
        it_qb = project("qb", qbT, 0.125)
        t_qi = turn_proj(it_qi, qiT)

        def dots():
            acc = [None, None]
            for h in range(NH):
                b = 4 + h % 2
                rws = slice(64 * (h % 2), 64 * (h % 2) + 64)
                w = bfree[b]
                bfree[b] = []
                mm(bank[b][:, 128:256], qiT[rws, h // 2, 0:128], kiT[rws, 0:128], True, True, w, t_qi, t_kiT)
                tk = mm(bank[b][:, 256:512], qiT[rws, h // 2, 128:256], kiT[rws, :], True, True, inc=True)
                rv_ = rlu[h % 2]
                a = act(lambda q, rv_=rv_, b=b: q.activation(rv_[:, :], bank[b][:, 128:512], ACT.Relu), tk,
                        st.get(("rf", h % 2)), k2)
                bfree[b] = [a]
                yield
                new = []
                for tb in range(2):
                    cc = slice(0, 128) if tb == 0 else slice(128, 384)
                    wv = small[:, tb, 192 + h:193 + h]
                    if h == 0:
                        acc[tb] = tsc(sco[:, cc], rv_[:, cc], wv, None, ALU.mult, None, a, prev)
                    else:
                        acc[tb] = stt(sco[:, cc], rv_[:, cc], wv, sco[:, cc], ALU.mult, ALU.add, a, acc[tb])
                    new.append(acc[tb])
                st["rf", h % 2] = new
                yield
            t = stt(sco[:, :], sco[:, :], IDX_SCALE, caus[:, :], ALU.mult, ALU.add, acc, t_caus)
            lt = [t, t]
            for _ in range(8):
                for tb in range(2):
                    cc = slice(0, 128) if tb == 0 else slice(128, 384)
                    lt[tb] = dve(lambda q, tb=tb, cc=cc: q.max(best[:, tb, :], sco[:, cc]), lt[tb])
                    yield
                for tb in range(2):
                    cc = slice(0, 128) if tb == 0 else slice(128, 384)
                    lt[tb] = dve(lambda q, tb=tb, cc=cc: q.match_replace(sco[:, cc], best[:, tb, :], sco[:, cc], SENT),
                                 lt[tb])
                    yield
            t = tsc(mB[:, :], sco[:, :], SENT, None, ALU.is_equal, None, lt, hfin)
            t = tsc(mB[:, :], mB[:, :], -1.0, -NEG, ALU.add, ALU.mult, t)
            st["mB"] = tt(mB[:, :], mB[:, :], caus[:, :], ALU.add, t)
            yield

        it_qa = project("qa", qaT, 0.125)
        bg.append(dots())
        t_qb = turn_proj(it_qb, qbT)
        it_ka = project("ka", kaT, 1.0, background(8))
        t_qa = turn_proj(it_qa, qaT)
        bk = (0, 1) if cnt["n"] % 2 else (2, 3)
        r = chunk(u_in2["va"], [(AH, AL, k2, bk)], after=background(10))
        t_va = [tm(bk[tb], va[:, tb, :], "act", 1.0, r[tb], hfin) for tb in range(2)]
        t_ka = turn_proj(it_ka, kaT)
        cnt["n"] += 1
        ring = {"n": 0}

        gsteps = []

        def gates():
            for nm, dst, n in (("ga0", ga, 0), ("ga1", ga, 1), ("gb0", gb, 0), ("gb1", gb, 1)):
                us = u_in2[nm]
                for i, u in enumerate(us):
                    targets = [(AH, AL, 4 * i, tb, 4 + tb, (0, 512), i == 0, i == 1, pairs(k2, 4 * i, 4))
                               for tb in range(2)]
                    r = unit(u, targets)
                    if i == 0:
                        yield
                for tb in range(2):
                    o_ = dst[:, tb, 512 * n:512 * n + 512]
                    t = tm(4 + tb, o_, "act", 1.0, r[tb], t_ka, t_qa, t_qb, rrf, rawf)
                    gsteps.append(t)
                yield

        gs = gates()

        def gfill():
            next(gs, None)

        def attend(name, qT_, kTs, vs, bias_, O_, btok, col, obs, extra):
            S, E, TR, PTt, PVt = {}, {}, {}, {}, {}

            def scores(h):
                b = h % 2
                r_ = slice(64 * (h % 2), 64 * (h % 2) + 64)
                w = bfree[b]
                bfree[b] = []
                kk = kTs(h)
                mm(bank[b][:, 128:256], qT_[r_, h // 2, 0:128], kk[r_, 0:128], True, True, w, extra)
                S[h] = mm(bank[b][:, 256:512], qT_[r_, h // 2, 128:256], kk[r_, :], True, True, inc=True)

            def soft(h):
                b = h % 2
                es = []
                fr = []
                for tb in range(2):
                    cc = slice(0, 128) if tb == 0 else slice(128, 384)
                    pc = slice(128, 256) if tb == 0 else slice(256, 512)
                    i = col + 2 * h + tb
                    m1 = mneg[:, i:i + 1]
                    mg = rl[:, i:i + 1]
                    a = dve(lambda q, cc=cc, pc=pc, m1=m1: q.tensor_tensor_reduce(
                        out=s2[b][:, cc], in0=bank[b][:, pc], in1=bias_[:, cc], scale=1.0, scalar=SENT,
                        op0=ALU.add, op1=ALU.max, accum_out=m1), S[h], btok, E.get(h - 2))
                    fr.append(a)
                    g = tsc(mg, m1, -1.0, None, ALU.mult, None, a)
                    es.append(act(lambda q, cc=cc, mg=mg, i=i: q.activation(
                        P2[b][:, cc], s2[b][:, cc], ACT.Exp, bias=mg, accum_out=lsum[:, i:i + 1]), g, TR.get(h - 2)))
                bfree[b] = fr
                E[h] = es

            def turn(h):
                b, tk = transposes([(i, P2[h % 2][:, i * 128:i * 128 + 128]) for i in range(3)], E[h])
                TR[h] = tk
                t = copy("act" if h % 2 else "dve", PT2[h % 2][:, :], bank[b][:, 0:384], tk, PVt.get(h - 2))
                bfree[b] = [t]
                PTt[h] = t

            def pv(h):
                w = [PTt[h], extra]
                if h == 0:
                    w += [bfree[obs[0]], bfree[obs[1]]]
                    bfree[obs[0]] = bfree[obs[1]] = []
                v = vs(h)
                hc = slice(h * 64, h * 64 + 64)
                mm(bank[obs[0]][:, hc], PT2[h % 2][:, 0:128], v[0], True, True, w)
                mm(bank[obs[1]][:, hc], PT2[h % 2][:, 128:256], v[0], True, False)
                PVt[h] = mm(bank[obs[1]][:, hc], PT2[h % 2][:, 256:384], v[1], False, True, inc=True)

            scores(0)
            for h in range(NH):
                soft(h)
                if h + 1 < NH:
                    scores(h + 1)
                if h % 2 == 0:
                    gfill()
                background(6)()
                if h:
                    pv(h - 1)
                turn(h)
            pv(NH - 1)
            t = dve(lambda q: q.reciprocal(rl[:, 32 + col:48 + col], lsum[:, col:col + 16]), E[NH - 1])
            rv_ = rl[:, 32 + col:48 + col].rearrange("p (h t) -> p h t", t=2)
            return [o_out(O_, obs[tb], tb, rv_[:, :, tb], t, PVt[NH - 1]) for tb in range(2)], E[NH - 1]

        t_oa, _ = attend("a", qaT, lambda h: kaT[:, h // 2, :],
                         lambda h: [va[:, i, h * 64:h * 64 + 64] for i in range(2)], lnC, Oa, t_lnC, 0, (2, 3),
                         [t_qa, t_ka, t_va, k2, tx_2])
        background(500)()
        t_ob, last_e = attend("b", qbT, lambda h: kbT[:, :],
                              lambda h: [small[:, i, 64:128] for i in range(2)], mB, Ob, st["mB"], 16, (2, 3),
                              [t_qb, t_kiT, k2, tx_2])
        for _ in range(20):
            gfill()
        att_pe = ("pe", value["pe"])
        t_ga = act(lambda q: q.activation(flat(ga[:, :, :]), flat(ga[:, :, :]), ACT.Sigmoid), gsteps)
        t_gb = act(lambda q: q.activation(flat(gb[:, :, :]), flat(gb[:, :, :]), ACT.Sigmoid), gsteps)

        ky = []
        for i, (O_, t_) in enumerate(((Oa, t_oa), (Ob, t_ob))):
            kk_, _ = to_split(O_, 4, YH[i], YL[i], 0, t_, att_pe)
            ky.append(kk_)
        ypt = ("pe", value["pe"])
        t_m = {}
        for i, us in ((0, u_upa), (1, u_upb)):
            for n in range(2):
                r = unit(us[n], [(YH[i], YL[i], 0, tb, 2 * n + tb, (0, 512), True, True, ky[i]) for tb in range(2)])
                for tb in range(2):
                    gv = (ga if i == 0 else gb)[:, tb, 512 * n:512 * n + 512]
                    mv = mrg[:, tb, 512 * n:512 * n + 512]
                    if i == 0:
                        t = tt(mv, bank[2 * n + tb][:, :], gv, ALU.mult, r[tb], t_ga, ypt)
                        bfree[2 * n + tb] = [t]
                        t_m[n, tb] = t
                    else:
                        t = tt(mt[tb][:, :], bank[2 * n + tb][:, :], gv, ALU.mult, r[tb], t_gb, t_m.get(("f", tb)), ypt)
                        bfree[2 * n + tb] = [t]
                        t_m[n, tb] = tt(mv, mv, mt[tb][:, :], ALU.add, t, t_m[n, tb])
                        t_m["f", tb] = t_m[n, tb]
        allm = [t_m[n, tb] for n in range(2) for tb in range(2)]
        km, mpe = to_split(mrg, 8, AH, AL, 0, allm, att_pe)
        ready = [[], []]
        for n in range(2):
            r = chunk(u_out2[n], [(AH, AL, km, (2 * n, 2 * n + 1))])
            for tb in range(2):
                xv = X[:, tb, 512 * n:512 * n + 512]
                t = tt(xv, bank[2 * n + tb][:, :], xv, ALU.add, r[tb], xr, tx_2)
                bfree[2 * n + tb] = [t]
                ready[tb].append(t)
        wo_pe = ("pe", value["pe"])
        kf, tx_f = norm(X, ready, AH, AL, v_ffn, None, wo_pe, ready)
        attn_done = [wo_pe, allm]
        hid_free = [[wo_pe, allm], [wo_pe, allm]]
        hh_free = [[wo_pe, allm], [wo_pe, allm]]
        hh_tok.clear()

        def upg(c):
            r = chunk(u_gu[c], [(AH, AL, kf, (4, 5))])
            ts = []
            for tb in range(2):
                rv_ = rel[tb][:, 0:256]
                a = act(lambda q, rv_=rv_, tb=tb: q.activation(rv_, bank[4 + tb][:, 0:256], ACT.Silu), r[tb],
                        st.get(("sq2", tb)), attn_done)
                s = tt(hid[c % 2][:, tb, 0:256], bank[4 + tb][:, 256:512], rv_, ALU.mult, a, hid_free[c % 2])
                bfree[4 + tb] = [s]
                st["sq2", tb] = s
                ts.append(s)
            st["hid", c] = ts

        for c in range(11):
            upg(c)
            if c:
                down(u_dn[c - 1], c - 1, c == 1, False)
            turn_hid(c, 2)
        r = down(u_dn[10], 10, False, True)
        xr = [[], []]
        for n in range(2):
            for tb in range(2):
                xv = X[:, tb, 512 * n:512 * n + 512]
                t = tt(xv, bank[2 * n + tb][:, :], xv, ALU.add, r[2 * n + tb], ready, tx_f)
                xr[tb].append(t)
        rs = rstd(X, xr, s2v, kf)
        t_out = []
        for tb in range(2):
            t = stt(S1[:, tb, :], X[:, tb, :], rs[tb][0], g2b[:, :], ALU.mult, ALU.mult, rs[tb][1], t_nf, kf)
            t_out.append(dma("sp", out[tb * 128:tb * 128 + 128, :], S1[:, tb, :], f"d_o{tb}", t))
        prog["sp"].append((t_out, None, None, 0))
        assert state["l"] == len(units) and state["s"] == len(units)

        sems = {s: ctx.enter_context(nc.semaphore(f"s_{s}")) for s in value}
        block = ctx.enter_context(nc.Block())

        def emit(name):
            def run(eng):
                for waits, fn, sem, by in prog[name]:
                    for s, v in waits:
                        eng.wait_ge(sems[s], v)
                    if fn is not None:
                        ins = fn(eng)
                        if sem is not None:
                            ins.then_inc(sems[sem], by)
            return run

        block.sync(emit("sp"))
        block.gpsimd(emit("pool"))
        block.scalar(emit("act"))
        block.vector(emit("dve"))
        block.tensor(emit("pe"))


def rope_tables(pos_of, width):
    n = width // 2
    t = np.arange(T)
    inv = np.float32(10000.0) ** (-np.arange(n, dtype=np.float32) / np.float32(n))
    cols_c, cols_s = [], []
    for pos in pos_of(t):
        ang = pos.astype(np.float32)[:, None] * inv[None, :].astype(np.float32)
        c, s = np.cos(ang.astype(np.float32)), np.sin(ang.astype(np.float32))
        cols_c += [c, c]
        cols_s += [-s, s]
    tab = np.stack([np.concatenate(cols_c, 1), np.concatenate(cols_s, 1)], 1).astype(np.float32)
    return np.ascontiguousarray(tab.reshape(2, 128, 2, 64).transpose(1, 0, 2, 3))


def packed(m):
    return np.ascontiguousarray(np.concatenate([m[:128, :128], m[128:, :]], 1).astype(np.float32))


def kernel(**inputs):
    import concourse.bacc as bacc
    from concourse.bass_utils import run_bass_kernel_spmd

    a = {k: np.asarray(v) for k, v in inputs.items()}

    def fm(v):
        v = v.reshape(-1)
        return v.reshape(-1, 128).T

    bada = a["b_ada"].reshape(-1)
    vec = np.concatenate([
        fm(a["norm1_g"]), fm(a["norm2_g"]), fm(bada[0:2048]), fm(bada[3072:5120]),
        a["dw_kernel"][0].reshape(31, 4, 128).transpose(2, 1, 0).reshape(128, 124),
        fm(a["dw_bias"]), fm(a["conv_ln_g"]), fm(a["conv_ln_b"]), fm(a["norm_mix_2"]), fm(a["norm_ffn_2"]),
        np.zeros((128, 24), np.float32)], 1)
    cs = np.stack([a["c"].reshape(8, 128), a["c_ctx"].reshape(8, 128)], -1).transpose(1, 0, 2).reshape(128, 16)

    t = np.arange(T)
    row, col = t // 64, t % 64
    start = np.clip(col - 8, 0, 48)
    roff = np.clip(row[None, :] - row[:, None] + 7, 0, 14)
    coff = col[None, :] - col[:, None] + 15
    inside = (col[None, :] >= start[:, None]) & (col[None, :] < start[:, None] + 16)
    rpb = a["rpb"][0]
    rb = np.where(inside[None], rpb[:, roff, np.clip(coff, 0, 30)], np.float32(NEG)).astype(np.float32)

    q, k = t[:, None], t[None, :]
    count = ((q - k >= 0) & (q - k <= 128)).astype(int) + ((q >= k) & ((q - k) % 4 == 0)) + ((q >= k) & ((q - k) % 16 == 0))
    lnC = np.where(count > 0, np.log(np.maximum(count, 1).astype(np.float32)), np.float32(NEG))
    caus = np.where(q >= k, np.float32(0), np.float32(NEG))

    arrays = {
        "vec": vec, "cs": cs, "x": a["x"][0], "ctx": a["ctx"][0], "ident": np.eye(128, dtype=np.float32),
        "rope1": rope_tables(lambda t: (t // 64, t % 64), 32), "rope2": rope_tables(lambda t: (t,), 64),
        "lnC": packed(lnC), "caus": packed(caus), "b_ada": bada.reshape(1, -1),
        "rpb": rb, "final_g": a["final_g"].reshape(1, -1), "norm_final": a["norm_final_2"].reshape(1, -1),
    }
    for n in ("w_ada", "w_in", "w_out", "w_mlp1", "w_mlp2", "w_in_2", "w_up_a_2", "w_up_b_2", "w_out_2",
              "w_gate_2", "w_up_2", "w_down_2"):
        arrays[n] = a[n][0]
    arrays = {f"in_{k}": np.ascontiguousarray(v) for k, v in arrays.items()}
    nc = bacc.Bacc("TRN2", target_bir_lowering=False, num_devices=1)
    d = {k[3:]: nc.dram_tensor(k, v.shape, mybir.dt.from_np(v.dtype), kind="ExternalInput").ap()
         for k, v in arrays.items()}
    out = nc.dram_tensor("out", (T, D), F32, kind="ExternalOutput").ap()
    build_program(nc, d, out)
    res = run_bass_kernel_spmd(nc, [arrays], core_ids=[0])
    return res.results[0]["out"].reshape(1, T, D)
```

```python
import numpy as np
import concourse.bass as bass
from concourse import mybir
from contextlib import ExitStack

F32 = mybir.dt.float32
F32R = mybir.dt.float32r
ALU = mybir.AluOpType
ACT = mybir.ActivationFunctionType
AX = mybir.AxisListType

D = 1024
T = 256
NH = 8
EPS = 1e-6
NEG = -1e30
SENT = -3e38
IDX_SCALE = (64 ** -0.5) * (8 ** -0.5)
FF2 = 2816

KB = 1024
RW = 4
RH = 4
AHEAD = 3
AHEAD_ADA = 1
UB = 8 * KB


def build_program(nc, d, out):
    ctx = ExitStack()
    with ctx:
        base = 16512

        def at(name, off_kb, shape, dt=F32):
            return nc.alloc_sbuf_tensor_at(name, shape, dt, offset=base + int(off_kb * KB))

        W32 = [at(f"W32_{i}", 8 * i, [128, 2048]) for i in range(RW)]
        WH = [at(f"WH_{i}", 32 + 8 * i, [128, 2048], F32R) for i in range(RH)]
        WL = [at(f"WL_{i}", 64 + 8 * i, [128, 2048], F32R) for i in range(RH)]
        X = at("X", 96, [128, 2, D])
        o = 104
        g1b = at("g1b", o, [128, D])
        g2b = at("g2b", o + 4, [128, D])
        lnC = at("lnC", o + 8, [128, 384])
        caus = at("caus", o + 9.5, [128, 384])
        rope1 = at("rope1", o + 11, [128, 2, 2, 64])
        rope2 = at("rope2", o + 12, [128, 2, 2, 64])
        ident = at("ident", o + 13, [128, 128])
        ones = at("ones", o + 13.5, [128, 128])
        vec = at("vec", o + 14, [128, 224])
        csx = at("csx", o + 14.875, [128, 8, 4], F32R)
        cs = at("cs", o + 15, [128, 16])
        mod1 = at("mod1", o + 15.125, [128, 16, 2])
        mod2 = at("mod2", o + 15.25, [128, 16, 2])
        A1 = at("A1", o + 15.375, [128, 2, 8])
        A2 = at("A2", o + 15.4375, [128, 8])
        stat = at("stat", o + 16.6875, [128, 96])
        mneg = at("mneg", o + 15.625, [128, 64])
        lsum = at("lsum", o + 15.875, [128, 64])
        rl = at("rl", o + 16.125, [128, 64])
        best = at("best", o + 16.375, [128, 2, 8])
        m0 = 121.75

        def M(name, off, shape, dt=F32):
            return at(name, m0 + off, shape, dt)

        S1 = M("S1", 0, [128, 2, D])
        S2 = M("S2", 8, [128, 2048])
        AH = M("AH", 16, [128, 8, 256], F32R)
        AL = M("AL", 24, [128, 8, 256], F32R)
        CH = M("CH", 32, [128, 8, 256], F32R)
        CL = M("CL", 40, [128, 8, 256], F32R)
        rows1 = [M(f"rows1_{i}", 32 + 2 * i, [4, 512]) for i in range(4)]
        XC = M("XC", 48, [128, 2, D])
        XC2 = M("XC2", 56, [128, 2, D])
        hTc = M("hTc", 0, [128, 8, 256])
        Q = M("Q", 48, [128, 2, 512])
        Kt = M("Kt", 52, [128, 2, 512])
        V = M("V", 56, [128, 2, 512])
        KC = M("KC", 60, [128, 2, 512])
        VC = M("VC", 64, [128, 2, 512])
        U = M("U", 68, [128, 2, 512])
        G = M("G", 72, [128, 2, 512])
        cacc = M("cacc", 72, [128, 4, 256])
        ccen = M("ccen", 68, [128, 4, 256])
        hp = M("hp", 76, [128, 4, 288])
        csq = M("csq", 76, [128, 4, 256])
        tmp = M("tmp", 80.5, [128, 512])
        QR = M("QR", 0, [128, 2, 512])
        KR = M("KR", 4, [128, 2, 512])
        qrT = M("qrT", 32, [128, 4, 256])
        qT = M("qT", 36, [128, 4, 256])
        kT = M("kT", 40, [128, 4, 256])
        kcT = M("kcT", 44, [128, 4, 256])
        bias = [M(f"bias{i}", 8 + 2 * i, [128, 2, 256]) for i in range(4)]
        O1 = M("O1", 0, [128, 2, 512])
        rows2 = [M(f"rows2_{i}", 4 + 2 * i, [4, 512]) for i in range(2)]
        P1 = [M(f"P1_{i}", 48 + 2 * i, [128, 512]) for i in range(2)]
        PT1 = [M(f"PT1_{i}", 52 + 2 * i, [128, 512]) for i in range(2)]
        s1 = [M(f"s1_{i}", 60 + i, [128, 256]) for i in range(2)]
        crs = M("crs", 62, [128, 256])
        hid = [M(f"hid{i}", 32 + 4 * i, [128, 2, 512]) for i in range(2)]
        HH = [M(f"HH{i}", 40 + 4 * i, [128, 4, 256], F32R) for i in range(2)]
        HL = [M(f"HL{i}", 48 + 4 * i, [128, 4, 256], F32R) for i in range(2)]
        rel = [M(f"rel{i}", 56 + 2 * i, [128, 512]) for i in range(2)]
        raw = [M(f"raw{i}", 32 + 4 * i, [128, 2, 512]) for i in range(2)]
        rr = [M(f"rr{i}", 40 + 4 * i, [128, 2, 512]) for i in range(2)]
        qiT = M("qiT", 48, [128, 4, 256])
        qbT = M("qbT", 52, [128, 4, 256])
        qaT = M("qaT", 56, [128, 4, 256])
        kaT = M("kaT", 60, [128, 4, 256])
        va = M("va", 64, [128, 2, 512])
        kiT = M("kiT", 68, [128, 256])
        kbT = M("kbT", 69, [128, 256])
        small = M("small", 70, [128, 2, 200])
        skk = [M(f"skk{i}", 72 + i, [128, 2, 128]) for i in range(2)]
        Ob = M("Ob", 74, [128, 2, 512])
        mB = M("mB", 78, [128, 384])
        P2 = [M(f"P2_{i}", 1.5 * i, [128, 384]) for i in range(2)]
        PT2 = [M(f"PT2_{i}", 3 + 1.5 * i, [128, 384]) for i in range(2)]
        s2 = [M(f"s2_{i}", 6 + 1.5 * i, [128, 384]) for i in range(2)]
        rlu = [M(f"rlu{i}", 9 + 1.5 * i, [128, 384]) for i in range(2)]
        Oa = M("Oa", 12, [128, 2, 512])
        sco = M("sco", 74, [128, 384])
        ga = M("ga", 32, [128, 2, D])
        gb = M("gb", 40, [128, 2, D])
        YH = [M(f"YH{i}", 48 + 8 * i, [128, 4, 256], F32R) for i in range(2)]
        YL = [M(f"YL{i}", 52 + 8 * i, [128, 4, 256], F32R) for i in range(2)]
        mrg = M("mrg", 0, [128, 2, D])
        mt = [M(f"mt{i}", 64 + 2 * i, [128, 512]) for i in range(2)]

        bank = [ctx.enter_context(nc.psum_tensor(f"bank{i}", [128, 512], F32)) for i in range(8)]
        bfree = [[] for _ in range(8)]

        prog = {e: [] for e in ("pe", "act", "dve", "pool", "sp")}
        value = {}
        seen = {e: {} for e in prog}

        def waits_of(e, toks):
            need = {}
            todo = list(toks)
            while todo:
                t = todo.pop()
                if t is None:
                    continue
                if isinstance(t, list):
                    todo.extend(t)
                    continue
                need[t[0]] = max(need.get(t[0], 0), t[1])
            outw = []
            for s, v in need.items():
                if seen[e].get(s, 0) < v:
                    seen[e][s] = v
                    outw.append((s, v))
            return outw

        def op(e, fn, *toks, inc=True):
            w = waits_of(e, toks)
            if inc:
                value[e] = value.get(e, 0) + 1
            prog[e].append((w, fn, e if inc else None, 1))
            return (e, value.get(e, 0)) if inc else None

        def dma(e, dst, src, sem, *toks):
            w = waits_of(e, toks)
            value[sem] = value.get(sem, 0) + 16
            prog[e].append((w, lambda q, dst=dst, src=src: q.dma_start(dst, src), sem, 16))
            return (sem, value[sem])

        def pe(fn, *t, inc=True):
            return op("pe", fn, *t, inc=inc)

        def act(fn, *t):
            return op("act", fn, *t)

        def dve(fn, *t):
            return op("dve", fn, *t)

        def mm(o_, l, r, start, stop, *t, inc=False):
            return pe(lambda e: e.matmul(o_, l, r, start=start, stop=stop), *t, inc=inc)

        def copy(e, o_, i_, *t):
            if e == "act":
                return act(lambda q: q.activation(o_, i_, ACT.Copy), *t)
            return dve(lambda q: q.tensor_copy(o_, i_), *t)

        def tt(o_, a, b, alu, *t):
            return dve(lambda q: q.tensor_tensor(o_, a, b, alu), *t)

        def tsc(o_, a, s1_, s2_, a0, a1, *t):
            if a1 is None:
                return dve(lambda q: q.tensor_scalar(o_, a, s1_, None, a0), *t)
            return dve(lambda q: q.tensor_scalar(o_, a, s1_, s2_, a0, a1), *t)

        def stt(o_, a, s, b, a0, a1, *t):
            return dve(lambda q: q.scalar_tensor_tensor(o_, a, s, b, a0, a1), *t)

        units = []

        def add_unit(parts, lo="dve"):
            units.append((parts, lo))
            return len(units) - 1

        def unit_of(w, k0, nk, cols, lo="dve"):
            wid = sum(c[1] for c in cols)
            parts, c0 = [], 0
            for n0, cw in cols:
                src = w[k0 * 128:(k0 + nk) * 128, n0:n0 + cw].rearrange("(k p) n -> p k n", p=128)
                parts.append((c0, cw, src))
                c0 += cw
            return add_unit((nk, wid, parts), lo)

        rel_w32 = {}
        rel_hl = []
        unit_dma = {}
        unit_tok = {}
        unit_slot = {}
        state = {"l": 0, "s": 0, "ahead": AHEAD_ADA}

        def w32_view(u):
            nk, wid, _ = units[u][0]
            return W32[u % RW][:, 0:nk * wid].rearrange("p (k n) -> p k n", k=nk)

        def pump(u):
            moved = True
            while moved:
                moved = False
                n = state["l"]
                if n < len(units) and (n < RW or (n - RW) in rel_w32):
                    (nk, wid, parts), _ = units[n]
                    v = w32_view(n)
                    for c0, cw, src in parts:
                        tk = dma("sp", v[:, :, c0:c0 + cw], src, f"w{n % RW}", rel_w32.get(n - RW))
                    unit_dma[n] = tk
                    state["l"] += 1
                    moved = True
                n = state["s"]
                if n < len(units) and n <= u + state["ahead"] and n in unit_dma:
                    k = len(unit_slot)
                    if k >= RH and len(rel_hl) <= k - RH:
                        continue
                    free = rel_hl[k - RH] if k >= RH else None
                    nk, wid, _ = units[n][0]
                    sl = k % RH
                    w, h, l = W32[n % RW], WH[sl], WL[sl]
                    ts = []
                    for p in range(0, nk, nk // 2):
                        c = slice(p * wid, (p + nk // 2) * wid)
                        a = act(lambda q, h=h, w=w, c=c: q.activation(h[:, c], w[:, c], ACT.Copy), unit_dma[n], free)
                        b = op(units[n][1], lambda q, l=l, w=w, h=h, c=c: q.tensor_tensor(
                            l[:, c], w[:, c], h[:, c].bitcast(F32), ALU.subtract), a, unit_dma[n], free)
                        ts += [[a, b]] * (nk // 2)
                    unit_slot[n] = sl
                    unit_tok[n] = ts
                    rel_w32[n] = ts
                    state["s"] += 1
                    moved = True

        def part(u, target, last_use):
            H, L, k0, tb, bk, (c0, cw), first, last, tk = target
            nk, wid, _ = units[u][0]
            sl = unit_slot[u]
            wh = WH[sl][:, 0:nk * wid].rearrange("p (k n) -> p k n", k=nk)
            wl = WL[sl][:, 0:nk * wid].rearrange("p (k n) -> p k n", k=nk)
            w = [tk] + ([bfree[bk]] if first else [])
            if first:
                bfree[bk] = []
            po = bank[bk][:, 0:cw]
            for k in range(nk):
                hs = H[:, k0 + k, tb * 128:tb * 128 + 128]
                ls = L[:, k0 + k, tb * 128:tb * 128 + 128]
                mm(po, hs, wh[:, k, c0:c0 + cw], first and k == 0, False, w, unit_tok[u][k])
                mm(po, hs, wl[:, k, c0:c0 + cw], False, False)
                tok = mm(po, ls, wh[:, k, c0:c0 + cw], False, last and k == nk - 1, inc=(k == nk - 1))
                w = []
            if last_use:
                rel_hl.append(tok)
            return tok

        wada, win, wout, wm1, wm2 = (d[n] for n in ("w_ada", "w_in", "w_out", "w_mlp1", "w_mlp2"))
        win2, wua, wub, wout2, wg, wu, wd = (d[n] for n in (
            "w_in_2", "w_up_a_2", "w_up_b_2", "w_out_2", "w_gate_2", "w_up_2", "w_down_2"))

        def col_units(w, cols, kt=8, lo="dve"):
            return [unit_of(w, k0, 4, cols, lo) for k0 in range(0, kt, 4)]

        u_ada1 = [col_units(wada, [(512 * n, 512)]) for n in range(4)]
        u_in = {}
        for nm, c0 in (("a", 1536), ("b", 2048), ("k", 512), ("q", 0), ("v", 1024)):
            u_in[nm] = col_units(win, [(c0, 512)], lo="dve" if nm in "ab" else "pool")
        u_ada2 = [(nm, n, [unit_of(wada, k0, 4, [(c0 + 512 * n, 512)], "dve" if (n + k0 // 2) % 3 == 2 else "pool")
                           for k0 in (0, 4)])
                  for nm, c0 in (("sh", 3072), ("sc", 4096), ("g1", 2048), ("g2", 5120)) for n in range(2)]
        u_out = [unit_of(wout, k0, 4, [(512 * n, 512)]) for k0 in (4, 0) for n in range(2)]
        u_m1, u_m2 = [], []
        for c in range(8):
            u_m1.append(col_units(wm1, [(512 * c, 512)]))
            if c:
                u_m2.append([unit_of(wm2, 4 * (c - 1) + 2 * j, 2, [(0, 1024)]) for j in range(2)])
        u_m2.append([unit_of(wm2, 28 + 2 * j, 2, [(0, 1024)]) for j in range(2)])
        u_in2 = {}
        for nm, cols in (("qi", [(2176, 512)]), ("s", [(2048, 128), (2688, 72)]), ("qb", [(1536, 512)]),
                         ("qa", [(0, 512)]), ("ka", [(512, 512)]), ("va", [(1024, 512)]),
                         ("ga0", [(2760, 512)]), ("ga1", [(3272, 512)]), ("gb0", [(3784, 512)]),
                         ("gb1", [(4296, 512)])):
            u_in2[nm] = col_units(win2, cols)
        u_upa = [unit_of(wua, 0, 4, [(512 * n, 512)]) for n in range(2)]
        u_upb = [unit_of(wub, 0, 4, [(512 * n, 512)]) for n in range(2)]
        u_out2 = [[None, None], [None, None]]
        for i in range(2):
            for n in range(2):
                u_out2[n][i] = unit_of(wout2, 4 * i, 4, [(512 * n, 512)])
        u_gu, u_dn = [], []
        for c in range(11):
            u_gu.append(None)
            u_dn.append(None)
        for c in range(12):
            if c < 11:
                u_gu[c] = []
                for k0 in (0, 4):
                    sg = wg[k0 * 128:(k0 + 4) * 128, 256 * c:256 * c + 256].rearrange("(k p) n -> p k n", p=128)
                    su = wu[k0 * 128:(k0 + 4) * 128, 256 * c:256 * c + 256].rearrange("(k p) n -> p k n", p=128)
                    u_gu[c].append(add_unit((4, 512, [(0, 256, sg), (256, 256, su)])))
            if c:
                u_dn[c - 1] = [unit_of(wd, 2 * (c - 1), 2, [(0, 1024)])]

        def tokmaj(ap):
            return ap.rearrange("(t p) n -> p t n", p=128)

        t_cs = dma("act", cs[:, :], d["cs"], "d_cs")
        pump(-AHEAD - 1)
        t_x = dma("act", X[:, :, :], tokmaj(d["x"]), "d_x")
        t_vec = dma("pool", vec[:, :], d["vec"], "d_vec")
        t_ident = dma("pool", ident[:, :], d["ident"], "d_id")
        t_xc = dma("sp", XC[:, :, :], tokmaj(d["ctx"]), "d_xc")
        bada = d["b_ada"]
        t_ones = op("pool", lambda q: q.memset(ones[:, :], 1.0))
        v_n1, v_n2, v_b1, v_b2 = vec[:, 0:8], vec[:, 8:16], vec[:, 16:32], vec[:, 32:48]
        v_dw = vec[:, 48:172].rearrange("p (c j) -> p c j", c=4)
        v_dwb, v_lng, v_lnb = vec[:, 172:176], vec[:, 176:180], vec[:, 180:184]
        v_mix, v_ffn = vec[:, 184:192], vec[:, 192:200]
        t_eps = dve(lambda q: q.memset(stat[:, 94:95], -0.5))
        t_eps2 = dve(lambda q: q.memset(stat[:, 95:96], EPS))

        t_cs = act(lambda q: q.activation(cs[:, :], cs[:, :], ACT.Silu), t_cs)
        csv = cs[:, :].rearrange("p (k r) -> p k r", r=2)
        t_ch = dve(lambda q: q.tensor_copy(csx[:, :, 0:2], csv), t_cs)
        t_csx = [t_ch, tt(csx[:, :, 2:4], csv, csx[:, :, 0:2].bitcast(F32), ALU.subtract, t_ch)]
        comb = vec[0:4, 200:202]

        tq = {"n": 0}

        def tbank():
            b = 6 + tq["n"] % 2
            tq["n"] += 1
            w = bfree[b]
            bfree[b] = []
            return b, w

        def transposes(blocks, *toks):
            b, w = tbank()
            for i, (c, src) in enumerate(blocks):
                dst = bank[b][:, c * 128:c * 128 + 128]
                tk = pe(lambda e, dst=dst, src=src: e.transpose(dst, src, ident[:, :]),
                        w, list(toks), t_ident, inc=(i == len(blocks) - 1))
            return b, tk

        def to_features(src, nj, dst, eng, *toks):
            outt, pet = [], []
            for j in range(0, nj, 2):
                n = min(2, nj - j)
                b, tk = transposes([(2 * i + tb, src[:, tb, (j + i) * 128:(j + i) * 128 + 128])
                                    for i in range(n) for tb in range(2)], *toks)
                pv = bank[b][:, 0:n * 256].rearrange("p (j n) -> p j n", j=n)
                t = copy(eng[(j // 2) % len(eng)], dst[:, j:j + n, :], pv, tk)
                bfree[b] = [t]
                outt.append(t)
                pet.append(tk)
            return outt, pet

        def flat(ap):
            return ap.rearrange("p a b -> p (a b)")

        def split_tb(src, nj, H, L, k0, tb, *toks):
            b, tk = transposes([(i, src[:, tb, i * 128:i * 128 + 128]) for i in range(nj)], *toks)
            pv = bank[b][:, 0:nj * 128].rearrange("p (j n) -> p j n", j=nj)
            hv = H[:, k0:k0 + nj, tb * 128:tb * 128 + 128]
            lv = L[:, k0:k0 + nj, tb * 128:tb * 128 + 128]
            a = act(lambda q: q.activation(hv, pv, ACT.Copy), tk, list(toks))
            c = tt(lv, pv, hv.bitcast(F32), ALU.subtract, a, tk, list(toks))
            bfree[b] = [c]
            return [a, c], tk

        nstat = {"n": 0}

        def col():
            nstat["n"] += 1
            assert nstat["n"] <= 94
            return stat[:, nstat["n"] - 1:nstat["n"]]

        def square(src, junk, *toks):
            c = col()
            return c, act(lambda q: q.activation(junk, src, ACT.Square, scale=1.0 / 32, accum_out=c), *toks)

        def power(src, t):
            c = col()
            return c, op("pool", lambda q: q.tensor_tensor(c, src, stat[:, 94:95], ALU.pow), t, t_eps)

        def rstd(parts):
            c = col()
            s0, t0 = parts[0]
            if len(parts) == 2:
                m = tsc(c, s0, parts[1][0], EPS, ALU.add, ALU.add, t0, parts[1][1])
            else:
                m = tsc(c, s0, EPS, None, ALU.add, None, t0)
            return power(c, m)

        hTv = S2[:, :].rearrange("p (k t) -> p k t", k=8)

        def norm_scale(src, tb, r, rt_, *free):
            return [tsc(S1[:, tb, 0:512], src[:, tb, 0:512], r, None, ALU.mult, None, rt_, list(free)),
                    act(lambda q: q.activation(S1[:, tb, 512:1024], src[:, tb, 512:1024], ACT.Copy, scale=r),
                        rt_, list(free))]

        def norm_turn(tb, tx, H, L, Av, Bv, *free):
            toks = []
            for i in range(2):
                b, tk = transposes([(j, S1[:, tb, (4 * i + j) * 128:(4 * i + j) * 128 + 128]) for j in range(4)], tx[i])
                ts = slice(tb * 128, tb * 128 + 128)
                ks = slice(4 * i, 4 * i + 4)
                sv, hv, lv = hTv[:, ks, ts], H[:, ks, ts], L[:, ks, ts]
                if i == 1:
                    ev = [act(lambda q, j=j: q.activation(
                        hTv[:, 4 + j, ts], bank[b][:, j * 128:j * 128 + 128], ACT.Identity,
                        bias=Bv[:, 4 + j:5 + j] if Bv is not None else 0.0, scale=Av[:, 4 + j:5 + j]), tk, list(free))
                        for j in range(4)]
                    bfree[b] = ev
                else:
                    pv = bank[b][:, :].rearrange("p (j n) -> p j n", j=4)
                    ev = tt(sv, pv, Av[:, ks].unsqueeze(2).to_broadcast([128, 4, 128]), ALU.mult, tk, list(free))
                    bfree[b] = [ev]
                    if Bv is not None:
                        ev = tt(sv, sv, Bv[:, ks].unsqueeze(2).to_broadcast([128, 4, 128]), ALU.add, ev)
                a = copy("act" if i else "dve", hv, sv, ev, list(free))
                c = tt(lv, sv, hv.bitcast(F32), ALU.subtract, a, ev, list(free))
                toks += [[a, c]] * 4
            return toks

        def residual(n, tb, bk, tok, gate, *free):
            xv = X[:, tb, 512 * n:512 * n + 512]
            yv = S1[:, tb, 512 * n:512 * n + 512]
            if gate is None:
                t = tt(xv, bank[bk][:, :], xv, ALU.add, tok, list(free))
                bfree[bk] = [t]
            else:
                t = tt(yv, bank[bk][:, :], gate[:, 512 * n:512 * n + 512], ALU.mult, tok, list(free))
                bfree[bk] = [t]
                t = tt(xv, xv, yv, ALU.add, t)
            return t

        def halves(n):
            return slice(512 * n, 512 * n + 512)

        def pairs(ktoks, k0, n, tb):
            return [ktoks[k][tb] for k in range(k0, k0 + n)]

        def chunk(us, stats, width=512, after=None, mid=None):
            res = []
            goals = [(s_, tb) for s_ in stats for tb in range(2)]
            for g, ((H, L, kt, bk), tb) in enumerate(goals):
                for i, u in enumerate(us):
                    pump(u)
                    nk = units[u][0][0]
                    tok = part(u, (H, L, nk * i, tb, bk[tb], (0, width), i == 0, i == len(us) - 1,
                                   pairs(kt, nk * i, nk, tb)), g == len(goals) - 1)
                    if after:
                        after()
                res.append(tok)
                if mid and g in mid:
                    mid[g]()
            return res

        def ada_unit(u, k0, bk, first, last):
            pump(u)
            sl = unit_slot[u]
            wh, wl = (x[sl][:, :].rearrange("p (k n) -> p k n", k=4) for x in (WH, WL))
            w = [t_csx] + ([bfree[bk]] if first else [])
            if first:
                bfree[bk] = []
            for k in range(4):
                mm(bank[bk][0:4, :], csx[:, k0 + k, :], wh[:, k, :], first and k == 0, False, w, unit_tok[u][k])
                tk = mm(bank[bk][0:2, :], csx[:, k0 + k, 0:2], wl[:, k, :], False, last and k == 3, inc=(k == 3))
                w = []
            rel_hl.append(tk)
            return tk

        def norm_in(src, ready, xh, *free):
            ts = []
            for tb in range(2):
                r, rt_ = rstd([square(src[:, tb, :], xh[:, tb, :], ready, list(free))])
                ts.append(tsc(xh[:, tb, :], src[:, tb, :], r, None, ALU.mult, None, rt_))
            return ts

        def turn_in(xh, hT, ts, *free):
            ev, pt = [], []
            for i in range(4):
                b, tk = transposes([(2 * j + tb, xh[:, tb, (2 * i + j) * 128:(2 * i + j) * 128 + 128])
                                    for j in range(2) for tb in range(2)], ts)
                t = copy("act" if i % 2 else "dve", flat(hT[:, 2 * i:2 * i + 2, :]), bank[b][:, :], tk, list(free))
                bfree[b] = [t]
                ev += [t, t]
                pt.append(tk)
            return ev, pt

        def modulate(hT, ev, H, L, r, *free):
            toks = []
            for i in range(4):
                e = []
                for k in (2 * i, 2 * i + 1):
                    A_, B_, h_ = A1[:, r, k:k + 1], modB[:, r, k:k + 1], hT[:, k, :]
                    if i % 2:
                        e.append(act(lambda q, A_=A_, B_=B_, h_=h_: q.activation(h_, h_, ACT.Identity, bias=B_, scale=A_),
                                     ev[k], t_A1, t_B))
                    else:
                        e.append(tsc(h_, h_, A_, B_, ALU.mult, ALU.add, ev[k], t_A1, t_B))
                hv, lv = flat(H[:, 2 * i:2 * i + 2, :]), flat(L[:, 2 * i:2 * i + 2, :])
                sv = flat(hT[:, 2 * i:2 * i + 2, :])
                a = copy("act" if i % 2 else "dve", hv, sv, e, list(free))
                c = tt(lv, sv, hv.bitcast(F32), ALU.subtract, a, e, list(free))
                toks += [[[a, c], [a, c]]] * 2
            return toks

        rt = []
        for n in range(4):
            if n == 1:
                tx_x = norm_in(X, t_x, S1)
            if n == 2:
                tx_c = norm_in(XC, t_xc, XC2)
            for i in range(2):
                tk = ada_unit(u_ada1[n][i], 4 * i, n, i == 0, i == 1)
            t = copy("act" if n % 2 else "dve", rows1[n][:, :], bank[n][0:4, :], tk)
            bfree[n] = [t]
            rt.append(t)
            if n == 1:
                ev_x, px = turn_in(S1, hTv, tx_x)
            if n == 2:
                ev_c, pc = turn_in(XC2, hTc, tx_c, px)
        b, w = tbank()
        for n in range(4):
            for j in range(4):
                c = (4 * n + j) * 2
                tk = mm(bank[b][:, c:c + 2], rows1[n][:, j * 128:j * 128 + 128], comb, True, True,
                        rt[n], t_vec, w, inc=(n == 3 and j == 3))
        state["ahead"] = AHEAD
        t_mod1 = tt(mod1[:, :, :], bank[b][:, 0:32].rearrange("p (k r) -> p k r", r=2),
                    v_b1.unsqueeze(2).to_broadcast([128, 16, 2]), ALU.add, tk, t_vec)
        bfree[b] = [t_mod1]
        rows_pe = tk
        B1 = []
        t_A1 = []
        for r in range(2):
            t_A1.append(stt(A1[:, r, :], mod1[:, 8:16, r], 1.0, v_n1, ALU.add, ALU.mult, t_mod1, t_vec))
            B1.append(mod1[:, :, r])
        modB = at("modB", 104 + 17.6875, [128, 2, 8])
        t_B = [dve(lambda q, r=r: q.tensor_copy(modB[:, r, :], mod1[:, 0:8, r]), t_mod1) for r in range(2)]

        kx = modulate(hTv, ev_x, AH, AL, 0)
        t_rope1 = dma("pool", rope1[:, :, :, :], d["rope1"], "d_r1", t_mod1)
        t_rope2 = dma("pool", rope2[:, :, :, :], d["rope2"], "d_r2", t_mod1)
        t_lnC = dma("pool", lnC[:, :], d["lnC"], "d_lc", t_mod1)
        t_caus = dma("pool", caus[:, :], d["caus"], "d_ca", t_mod1)
        t_g1 = dma("pool", g1b[:, :], bada[0:1, 2048:3072].to_broadcast([128, D]), "d_g1", t_mod1)
        t_g2 = dma("pool", g2b[:, :], bada[0:1, 5120:6144].to_broadcast([128, D]), "d_g2", t_mod1)
        ra = chunk(u_in["a"], [(AH, AL, kx, (0, 1))])
        kc = modulate(hTc, ev_c, CH, CL, 1, rows_pe)
        rb = chunk(u_in["b"], [(AH, AL, kx, (2, 3))])
        tu = []
        for tb in range(2):
            s = act(lambda q, tb=tb: q.activation(G[:, tb, :], bank[2 + tb][:, :], ACT.Sigmoid), rb[tb], pc, tx_c)
            bfree[2 + tb] = [s]
            t = tt(U[:, tb, :], bank[tb][:, :], G[:, tb, :], ALU.mult, s, ra[tb])
            bfree[tb] = [t]
            tu.append(t)
        t_z = op("pool", lambda q: q.memset(hp[:, :, 0:15], 0.0))
        t_z = op("pool", lambda q: q.memset(hp[:, :, 271:288], 0.0), t_z)
        t_hp = []

        def turn_u():
            for j in range(0, 4, 2):
                b, tk = transposes([(2 * i + tb, U[:, tb, (j + i) * 128:(j + i) * 128 + 128])
                                    for i in range(2) for tb in range(2)], tu)
                t = copy("act", hp[:, j:j + 2, 15:271], bank[b][:, :].rearrange("p (j n) -> p j n", j=2), tk)
                bfree[b] = [t]
                t_hp.append(t)
            bg.append(conv())

        bg = []
        conv_last = [None] * 4

        def conv():
            for j in range(31):
                for c in range(4):
                    src = hp[:, c, j:j + 256]
                    if j == 0:
                        conv_last[c] = tsc(cacc[:, c, :], src, v_dw[:, c, 0:1], v_dwb[:, c:c + 1], ALU.mult, ALU.add,
                                           t_hp, t_z, tu, t_vec)
                    else:
                        conv_last[c] = stt(cacc[:, c, :], src, v_dw[:, c, j:j + 1], cacc[:, c, :],
                                           ALU.mult, ALU.add, conv_last[c])
                    yield

        def background(n):
            def go():
                for _ in range(n):
                    while bg:
                        try:
                            next(bg[0])
                            break
                        except StopIteration:
                            bg.pop(0)
            return go

        def tm(b_, o_, e, scale, tk, *toks):
            pv, = (bank[b_][:, :],)
            if e == "act":
                t = act(lambda q: q.activation(o_, pv, ACT.Copy, scale=scale), tk, list(toks))
            elif scale == 1.0:
                t = dve(lambda q: q.tensor_copy(o_, pv), tk, list(toks))
            else:
                t = tsc(o_, pv, scale, None, ALU.mult, None, tk, list(toks))
            bfree[b_] = [t]
            return t

        def rope(dst, src, nh, tab, s, tb, ready, *free):
            cosv = tab[:, tb, 0, :].unsqueeze(1).to_broadcast([128, nh, 64])
            sv = src.rearrange("p (h e) -> p h e", e=64) if nh > 2 else src
            dv = dst.rearrange("p (h e) -> p h e", e=64)
            t1 = tt(dv, sv, cosv, ALU.mult, ready, list(free))
            tv = tmp[:, 0:nh * 64].rearrange("p (h e) -> p h e", e=64)
            t2 = []
            for lo in range(0, 64, 2 * s):
                for x, y in ((lo, lo + s), (lo + s, lo)):
                    snv = tab[:, tb, 1, x:x + s].unsqueeze(1).to_broadcast([128, nh, s])
                    t2.append(tt(tv[:, :, x:x + s], sv[:, :, y:y + s], snv, ALU.mult, ready, list(free)))
            return tt(dv, dv, tv, ALU.add, t1, t2)

        bias_free = [[kx]] * 4
        bias_tok = {}

        def load_bias(h):
            if h < NH:
                bias_tok[h] = dma("pool", bias[h % 4][:, :, :], tokmaj(d["rpb"][h]), f"d_b{h % 4}", bias_free[h % 4])

        for h in range(4):
            load_bias(h)
        rk = chunk(u_in["k"], [(AH, AL, kx, (0, 1)), (CH, CL, kc, (4, 5))], after=background(5),
                   mid={0: turn_u})
        cdone = [tx_c, ("pe", value["pe"])]
        tk_ = [tm(tb, Kt[:, tb, :], "act", 1.0, rk[tb], tx_c) for tb in range(2)]
        tkc = [tm(4 + tb, KC[:, tb, :], "act", 1.0, rk[2 + tb]) for tb in range(2)]
        rq = chunk(u_in["q"], [(AH, AL, kx, (2, 3))], after=background(5))
        tq_ = [tm(2 + tb, Q[:, tb, :], "act", 0.125, rq[tb], tx_c) for tb in range(2)]
        tkr = []
        prev = None
        for tb in range(2):
            prev = rope(KR[:, tb, :], Kt[:, tb, :], 8, rope1, 16, tb, [tk_[tb], t_rope1], prev, kc, tx_c,
                        ("pe", value["pe"]))
            tkr.append(prev)
        tqr = []
        for tb in range(2):
            prev = rope(QR[:, tb, :], Q[:, tb, :], 8, rope1, 16, tb, [tq_[tb], t_rope1], prev)
            tqr.append(prev)
        t_qk, t_pqk = [], []

        def turn_qk(*what):
            for src, dst, ts in what:
                e_, p_ = to_features(src, 4, dst, ["act", "dve"], ts, turn_free)
                t_qk.append(e_)
                t_pqk.append(p_)

        turn_free = []

        def ctx_done():
            turn_free.append(("pe", value["pe"]))

        rv = chunk(u_in["v"], [(CH, CL, kc, (4, 5)), (AH, AL, kx, (0, 1))], after=background(4),
                   mid={1: ctx_done, 2: lambda: turn_qk((KR, kT, tkr), (KC, kcT, tkc))})
        gdone = ("pe", value["pe"])
        tv_ = [tm(tb, V[:, tb, :], "act", 1.0, rv[2 + tb], tx_c) for tb in range(2)]
        tvc = [tm(4 + tb, VC[:, tb, :], "dve", 1.0, rv[tb]) for tb in range(2)]
        turn_qk((Q, qT, tq_), (QR, qrT, tqr))
        p1, p2 = t_pqk[0], t_pqk[1]
        p4 = t_pqk[3]

        ada2 = []

        def ada_tail(nm, n, t):
            r2 = rows2[n]
            b, w = tbank()
            if nm in ("sh", "sc"):
                for j in range(4):
                    tk = mm(bank[b][:, 2 * j:2 * j + 2], r2[:, j * 128:j * 128 + 128], comb,
                            True, True, t, w, inc=(j == 3))
                k0 = (0 if nm == "sh" else 8) + 4 * n
                t = tt(mod2[:, k0:k0 + 4, :], bank[b][:, 0:8].rearrange("p (k r) -> p k r", r=2),
                       v_b2[:, k0:k0 + 4].unsqueeze(2).to_broadcast([128, 4, 2]), ALU.add, tk)
            else:
                gt, tg = (g1b, t_g1) if nm == "g1" else (g2b, t_g2)
                gv = gt[:, 512 * n:512 * n + 512]
                tk = mm(bank[b][:, :], comb[:, 0:1].to_broadcast([4, 128]), r2[:, :], True, True, t, w, inc=True)
                t = tt(gv, bank[b][:, :], gv, ALU.add, tk, tg)
            rows2_free[n] = [tk]
            bfree[b] = [t]
            ada2.append(t)

        def ada_steps():
            tail = None
            for i8, (nm, n, us) in enumerate(u_ada2):
                bk = 4 + i8 % 2
                ada_unit(us[0], 0, bk, True, False)
                if tail:
                    ada_tail(*tail)
                yield
                tk = ada_unit(us[1], 4, bk, False, True)
                t = copy("act", rows2[n][:, :], bank[bk][0:4, :], tk, rows2_free[n])
                bfree[bk] = [t]
                tail = (nm, n, t)
                yield
            ada_tail(*tail)
            yield

        rows2_free = [[tkr, tqr, p1], [tkr, tqr, p1]]
        ada = ada_steps()

        def fill(n=1):
            for _ in range(n):
                next(ada, None)

        def conv_norm():
            b, w = tbank()
            for c in range(4):
                tk = mm(bank[b][:, 0:256], ones[:, :], cacc[:, c, :], c == 0, c == 3, w, conv_last, t_ones, inc=(c == 3))
            mu = bank[b]
            t = []
            for c in range(4):
                t.append(stt(ccen[:, c, :], mu[:, 0:256], -1.0 / 512, cacc[:, c, :], ALU.mult, ALU.add, tk, conv_last,
                             tu, t_hp))
            bfree[b] = t
            t_cc = t
            tsq = act(lambda q: q.activation(csq[:, :, :], ccen[:, :, :], ACT.Square), t_cc, conv_last)
            yield
            b, w = tbank()
            for c in range(4):
                tk = mm(bank[b][:, 0:256], ones[:, :], csq[:, c, :], c == 0, c == 3, w, tsq, inc=(c == 3))
            var = bank[b]
            t = act(lambda q: q.activation(crs[:, :], var[:, 0:256], ACT.Sqrt, bias=stat[:, 95:96], scale=1.0 / 512),
                    tk, t_eps2, p2)
            bfree[b] = [t]
            yield
            t = dve(lambda q: q.reciprocal(crs[:, :], crs[:, :]), t)
            t = tt(ccen[:, :, :], ccen[:, :, :], crs[:, :].unsqueeze(1).to_broadcast([128, 4, 256]), ALU.mult, t, tsq)
            tn = [act(lambda q, c=c: q.activation(cacc[:, c, :], ccen[:, c, :], ACT.Silu, bias=v_lnb[:, c:c + 1],
                                                  scale=v_lng[:, c:c + 1]), t) for c in range(4)]
            yield
            ch = act(lambda q: q.activation(flat(AH[:, 4:8, :]), flat(cacc[:, :, :]), ACT.Copy), tn, gdone)
            cl = tt(flat(AL[:, 4:8, :]), flat(cacc[:, :, :]), flat(AH[:, 4:8, :]).bitcast(F32), ALU.subtract, ch, tn, gdone)
            k_conv.extend([[[ch, cl], [ch, cl]]] * 4)
            yield

        k_conv = []
        cn = conv_norm()

        its = [(h, tb) for h in range(NH) for tb in range(2)]
        st = {}

        def scores1(n):
            h, tb = its[n]
            b = n % 2
            r = slice(64 * (h % 2), 64 * (h % 2) + 64)
            w = bfree[b]
            bfree[b] = []
            mm(bank[b][:, 0:256], qrT[r, h // 2, tb * 128:tb * 128 + 128], kT[r, h // 2, :], True, True, w, t_qk)
            st["s", n] = mm(bank[b][:, 256:512], qT[r, h // 2, tb * 128:tb * 128 + 128], kcT[r, h // 2, :],
                            True, True, inc=True)

        pv_tok = {}
        pe_tr = {}
        obank = (2, 3)

        def soft1(n):
            h, tb = its[n]
            b = n % 2
            m1, m2, mg = mneg[:, 2 * n:2 * n + 1], mneg[:, 2 * n + 1:2 * n + 2], rl[:, 16 + n:17 + n]
            a = dve(lambda q: q.reduce_max(m1, bank[b][:, 256:512], AX.X), st["s", n])
            bt = bias[h % 4][:, tb, :]
            a = dve(lambda q: q.tensor_tensor_reduce(out=s1[b][:, :], in0=bank[b][:, 0:256], in1=bt, scale=1.0,
                                                     scalar=m1, op0=ALU.add, op1=ALU.max, accum_out=m2),
                    a, bias_tok[h], t_pqk, st.get(("e", n - 2)))
            bias_free[h % 4] = [a]
            g = tsc(mg, m2, -1.0, None, ALU.mult, None, a)
            e1_ = act(lambda q: q.activation(P1[b][:, 0:256], s1[b][:, :], ACT.Exp, bias=mg,
                                             accum_out=lsum[:, 2 * n:2 * n + 1]), g, t_pqk, pe_tr.get(n - 2))
            e2_ = act(lambda q: q.activation(P1[b][:, 256:512], bank[b][:, 256:512], ACT.Exp, bias=mg,
                                             accum_out=lsum[:, 2 * n + 1:2 * n + 2]), g, pe_tr.get(n - 2))
            bfree[b] = [a, e2_]
            st["e", n] = [e1_, e2_]

        def turn1(n):
            b, tk = transposes([(i, P1[n % 2][:, i * 128:i * 128 + 128]) for i in range(4)], st["e", n])
            pe_tr[n] = tk
            t = copy("act" if n % 2 else "dve", PT1[n % 2][:, :], bank[b][:, :], tk, pv_tok.get(n - 2), t_pqk)
            bfree[b] = [t]
            st["t", n] = t

        def pv1(n):
            h, tb = its[n]
            ob = obank[tb]
            w = [st["t", n], tv_, tvc]
            if h == 0:
                w.append(bfree[ob])
                bfree[ob] = []
            for i in range(4):
                vv = (V if i < 2 else VC)[:, i % 2, h * 64:h * 64 + 64]
                tk = mm(bank[ob][:, h * 64:h * 64 + 64], PT1[n % 2][:, i * 128:i * 128 + 128], vv, i == 0, i == 3,
                        w, inc=(i == 3))
            pv_tok[n] = tk

        scores1(0)
        for n in range(16):
            soft1(n)
            if n + 1 < 16:
                scores1(n + 1)
            fill(1)
            if n < 11:
                background(5)()
            elif n == 11:
                background(500)()
            else:
                next(cn, None)
            if n:
                pv1(n - 1)
            turn1(n)
            if n % 2 == 1:
                load_bias(n // 2 + 4)
        pv1(15)
        for _ in cn:
            pass
        n16 = lsum[:, 0:32].rearrange("p (n r) -> p n r", r=2)
        t = tt(rl[:, 32:48], n16[:, :, 0], n16[:, :, 1], ALU.add, st["e", 15])
        t_rl = dve(lambda q: q.reciprocal(rl[:, 48:64], rl[:, 32:48]), t)
        rlv = rl[:, 48:64].rearrange("p (h t) -> p h t", t=2)

        def o_out(O_, ob, tb, rv_, *toks):
            t = tt(O_[:, tb, :].rearrange("p (h e) -> p h e", e=64),
                   bank[ob][:, :].rearrange("p (h e) -> p h e", e=64),
                   rv_.unsqueeze(2).to_broadcast([128, 8, 64]), ALU.mult, list(toks))
            bfree[ob] = [t]
            return t

        t_o = [o_out(O1, 2 + tb, tb, rlv[:, :, tb], t_rl, pv_tok[14 + tb], t_pqk) for tb in range(2)]
        t_A2 = stt(A2[:, :], mod2[:, 8:16, 0], 1.0, v_n2, ALU.add, ALU.mult, ada2)
        t_B2 = dve(lambda q: q.tensor_copy(modB[:, 0, :], mod2[:, 0:8, 0]), ada2, kx)

        fill(20)
        ready = [[], []]
        sq = [[], []]

        def out_parts(us, tb, ktoks, after):
            for u, n, k0, first, last in us:
                pump(u)
                tok = part(u, (AH, AL, k0, tb, 2 * n + tb, (0, 512), first, last, pairs(ktoks[k0 // 4], 0, 4, tb)), tb == 1)
                if last:
                    after(n, tb, tok)

        def out1(n, tb, tok):
            t = residual(n, tb, 2 * n + tb, tok, g1b, t_x, tx_x, ada2, t_o, kk_out[0])
            ready[tb].append(t)
            sq[tb].append(square(X[:, tb, halves(n)], S1[:, tb, halves(n)], t))

        kk_out = [None, k_conv]
        us_out = [(u_out[0], 0, 4, True, False), (u_out[1], 1, 4, True, False),
                  (u_out[2], 0, 0, False, True), (u_out[3], 1, 0, False, True)]
        out_parts(us_out[0:2], 0, kk_out, out1)
        sp_ = [split_tb(O1, 4, AH, AL, 0, tb, t_o[tb], gdone) for tb in range(2)]
        kk_out[0] = [[sp_[0][0], sp_[1][0]]] * 4
        out_parts(us_out[2:4], 0, kk_out, out1)
        r_, rt_ = rstd(sq[0])
        wo0 = ("pe", value["pe"])
        tx0 = norm_scale(X, 0, r_, rt_)
        out_parts(us_out[0:2], 1, kk_out, out1)
        kh0 = norm_turn(0, tx0, AH, AL, A2, modB[:, 0, :], t_A2, t_B2, wo0)
        out_parts(us_out[2:4], 1, kk_out, out1)
        wo_pe = ("pe", value["pe"])
        t_fg = dma("pool", g1b[:, :], d["final_g"].to_broadcast([128, D]), "d_fg", ready)
        kh = [[kh0[k], None] for k in range(8)]
        tx_h = [tx0]

        r_, rt_ = rstd(sq[1])
        tx_h.append(norm_scale(X, 1, r_, rt_))

        def turn_late(kt, tx, *args):
            for k, t in enumerate(norm_turn(1, tx, *args)):
                kt[k][1] = t

        hfree = [[wo_pe, t_qk, st["e", 15], pv_tok], [wo_pe]]
        hid_free = [[wo_pe], [wo_pe]]
        hh_free = [[wo_pe], [wo_pe]]
        attn_done = [pv_tok[15], pv_tok[14], p4]
        hh_tok = {}

        def half_chunk(us, kt, tb, bk):
            for i, u in enumerate(us):
                pump(u)
                tok = part(u, (AH, AL, 4 * i, tb, bk, (0, 512), i == 0, i == 1, pairs(kt, 4 * i, 4, tb)), tb == 1)
            return tok

        def up1(c, tb, bk=None):
            bk = bk or 4 + tb
            r = half_chunk(u_m1[c], kh, tb, bk)
            rv_ = rel[tb][:, :]
            a = act(lambda q: q.activation(rv_, bank[bk][:, :], ACT.Relu), r, st.get(("sq", tb)), attn_done)
            bfree[bk] = [a]
            s = act(lambda q: q.activation(hid[c % 2][:, tb, :], rv_, ACT.Square), a, hid_free[c % 2], attn_done)
            st["sq", tb] = s
            st["hid", c, tb] = s

        def turn_hid(c, nj, tb):
            tk, p_ = split_tb(hid[c % 2], nj, HH[c % 2], HL[c % 2], 0, tb, st["hid", c, tb], hh_free[c % 2], attn_done)
            hh_tok.setdefault(c, [[None, None] for _ in range(nj)])
            for k in range(nj):
                hh_tok[c][k][tb] = tk
            if tb == 0:
                hid_free[c % 2] = []
            hid_free[c % 2] = hid_free[c % 2] + [p_]

        def down(us, c, tb, first, last):
            r = []
            for n in range(2):
                for j, u in enumerate(us):
                    pump(u)
                    tok = part(u, (HH[c % 2], HL[c % 2], 2 * j, tb, 2 * n + tb, (512 * n, 512),
                                   first and j == 0, last and j == len(us) - 1,
                                   pairs(hh_tok[c], 2 * j, 2, tb)), False)
                    if tb == 1 and n == 1:
                        rel_hl.append(tok)
                r.append(tok)
            if tb == 1:
                hh_free[c % 2] = [tok]
            return r

        def feed_forward(nc_, nj, up, dn, early):
            up(0, 0)
            early()
            if True:
                up(0, 1)
            turn_hid(0, nj, 0)
            turn_hid(0, nj, 1)
            for c in range(1, nc_):
                up(c, 0)
                if c == nc_ - 1:
                    down(dn[c - 1], c - 1, 0, c == 1, False)
                    up(c, 1)
                    turn_hid(c, nj, 0)
                    r0 = down(dn[c], c, 0, False, True)
                    yield r0, 0
                    down(dn[c - 1], c - 1, 1, False, False)
                    turn_hid(c, nj, 1)
                    yield down(dn[c], c, 1, False, True), 1
                else:
                    up(c, 1)
                    for tb in range(2):
                        down(dn[c - 1], c - 1, tb, c == 1, False)
                    for tb in range(2):
                        turn_hid(c, nj, tb)

        ff = feed_forward(8, 4, up1, u_m2,
                          lambda: turn_late(kh, tx_h[1], AH, AL, A2, modB[:, 0, :], t_A2, t_B2, wo_pe))
        r_, _ = next(ff)
        kh_pe = ("pe", value["pe"])
        xr = [[], []]
        k2 = [[None, None] for _ in range(8)]
        tx_2 = []

        def between_norms(tb, r):
            zs = []
            for n in range(2):
                t = residual(n, tb, 2 * n + tb, r[n], g2b, ada2, kh, ready[tb], tx_h)
                s1_ = square(X[:, tb, halves(n)], S1[:, tb, halves(n)], t)
                xv = X[:, tb, halves(n)]
                t = tt(xv, xv, g1b[:, halves(n)], ALU.mult, t, s1_[1], t_fg)
                zs.append((s1_, square(xv, S1[:, tb, halves(n)], t, s1_[1]), t))
            r1, t1 = rstd([z[0] for z in zs])
            cz, cr, c2 = col(), col(), col()
            tz = tsc(cz, zs[0][1][0], zs[1][1][0], None, ALU.add, None, zs[0][1][1], zs[1][1][1])
            t2 = tsc(cr, cz, r1, r1, ALU.mult, ALU.mult, tz, t1)
            r2, t2 = rstd([(cr, t2)])
            t2 = tsc(c2, r2, r1, None, ALU.mult, None, t2, t1)
            tx_ = norm_scale(X, tb, c2, t2, [z[2] for z in zs], [z[1][1] for z in zs])
            tx_2.append(tx_)
            xr[tb] = [tsc(X[:, tb, :], X[:, tb, :], r1, None, ALU.mult, None, t1, tx_)]

        def between_turn(tb):
            for k, t in enumerate(norm_turn(tb, tx_2[tb], AH, AL, v_mix, None, kh_pe)):
                k2[k][tb] = t

        between_norms(0, r_)
        r_, _ = next(ff)
        gdone2 = ("pe", value["pe"])
        between_turn(0)
        between_norms(1, r_)


        hfin = [hh_tok[7], hh_tok[6], gdone2]
        rawf = [[hfin], [hfin]]
        rrf = [[hfin], [hfin]]
        cnt = {"n": 0}
        prev = None

        def project(nm, scale, after=None, r=None):
            nonlocal prev
            i = cnt["n"] % 2
            cnt["n"] += 1
            bk = (0, 1) if i else (2, 3)
            if r is None:
                r = chunk(u_in2[nm], [(AH, AL, k2, bk)], after=after)
            else:
                bk = (4, 5)
            ts = []
            for tb in range(2):
                t = tm(bk[tb], raw[i][:, tb, :], "act", scale, r[tb], rawf[i])
                prev = rope(rr[i][:, tb, :], raw[i][:, tb, :], 8, rope2, 32, tb, [t, t_rope2], prev, rrf[i])
                ts.append(prev)
            rawf[i] = ts
            return i, ts

        def small_part(tb):
            for i, u in enumerate(u_in2["s"]):
                pump(u)
                tok = part(u, (AH, AL, 4 * i, tb, tb, (0, 200), i == 0, i == 1, pairs(k2, 4 * i, 4, tb)), tb == 1)
            return tok

        r_qi = [half_chunk(u_in2["qi"], k2, 0, 4)]
        r = [small_part(0)]
        between_turn(1)
        r_qi.append(half_chunk(u_in2["qi"], k2, 1, 5))
        r.append(small_part(1))
        it_qi = project("qi", 1.0, r=r_qi)
        t_nf = dma("pool", g2b[:, :], d["norm_final"].to_broadcast([128, D]), "d_nf", xr)
        t_sm = []
        for tb in range(2):
            t = act(lambda q, tb=tb: q.activation(small[:, tb, :], bank[tb][:, 0:200], ACT.Copy), r[tb], hfin)
            bfree[tb] = [t]
            t_sm.append(t)
        t_kk = []
        for i, c0 in ((0, 0), (1, 128)):
            for tb in range(2):
                src = small[:, tb, c0:c0 + 64].unsqueeze(1).to_broadcast([128, 2, 64])
                prev = rope(skk[i][:, tb, :], src, 2, rope2, 32, tb, [t_sm, t_rope2], prev)
                t_kk.append(prev)
        it_qb = project("qb", 0.125)
        t_kiT = []
        for i, dst in ((1, kiT), (0, kbT)):
            b, tk = transposes([(tb, skk[i][:, tb, :]) for tb in range(2)], t_kk)
            t = copy("act", dst[:, :], bank[b][:, 0:256], tk, hfin)
            bfree[b] = [t]
            t_kiT.append(t)
        def turn_proj(it, dst):
            i, ts = it
            e_, p_ = to_features(rr[i], 4, dst, ["act", "dve"], ts, hfin)
            rrf[i] = p_
            return e_

        t_qi = turn_proj(it_qi, qiT)

        def dots():
            acc = [None, None]
            for h in range(NH):
                b = 4 + h % 2
                rws = slice(64 * (h % 2), 64 * (h % 2) + 64)
                w = bfree[b]
                bfree[b] = []
                mm(bank[b][:, 128:256], qiT[rws, h // 2, 0:128], kiT[rws, 0:128], True, True, w, t_qi, t_kiT)
                tk = mm(bank[b][:, 256:512], qiT[rws, h // 2, 128:256], kiT[rws, :], True, True, inc=True)
                rv_ = rlu[h % 2]
                a = act(lambda q, rv_=rv_, b=b: q.activation(rv_[:, :], bank[b][:, 128:512], ACT.Relu), tk,
                        st.get(("rf", h % 2)), k2)
                bfree[b] = [a]
                yield
                new = []
                for tb in range(2):
                    cc = slice(0, 128) if tb == 0 else slice(128, 384)
                    wv = small[:, tb, 192 + h:193 + h]
                    if h == 0:
                        acc[tb] = tsc(sco[:, cc], rv_[:, cc], wv, None, ALU.mult, None, a, prev)
                    else:
                        acc[tb] = stt(sco[:, cc], rv_[:, cc], wv, sco[:, cc], ALU.mult, ALU.add, a, acc[tb])
                    new.append(acc[tb])
                st["rf", h % 2] = new
                yield
            t = stt(sco[:, :], sco[:, :], IDX_SCALE, caus[:, :], ALU.mult, ALU.add, acc, t_caus)
            lt = [t, t]
            for _ in range(8):
                for tb in range(2):
                    cc = slice(0, 128) if tb == 0 else slice(128, 384)
                    lt[tb] = dve(lambda q, tb=tb, cc=cc: q.max(best[:, tb, :], sco[:, cc]), lt[tb])
                    yield
                for tb in range(2):
                    cc = slice(0, 128) if tb == 0 else slice(128, 384)
                    lt[tb] = dve(lambda q, tb=tb, cc=cc: q.match_replace(sco[:, cc], best[:, tb, :], sco[:, cc], SENT),
                                 lt[tb])
                    yield
            t = tsc(mB[:, :], sco[:, :], SENT, None, ALU.is_equal, None, lt, hfin)
            t = tsc(mB[:, :], mB[:, :], -1.0, -NEG, ALU.add, ALU.mult, t)
            st["mB"] = tt(mB[:, :], mB[:, :], caus[:, :], ALU.add, t)
            yield

        it_qa = project("qa", 0.125)
        bg.append(dots())
        t_qb = turn_proj(it_qb, qbT)
        it_ka = project("ka", 1.0, background(5))
        t_qa = turn_proj(it_qa, qaT)
        bk = (0, 1) if cnt["n"] % 2 else (2, 3)
        r = chunk(u_in2["va"], [(AH, AL, k2, bk)], after=background(5))
        t_va = [tm(bk[tb], va[:, tb, :], "act", 1.0, r[tb], hfin) for tb in range(2)]
        t_ka = turn_proj(it_ka, kaT)
        cnt["n"] += 1
        ring = {"n": 0}

        gsteps = []

        def gates():
            for nm, dst, n in (("ga0", ga, 0), ("ga1", ga, 1), ("gb0", gb, 0), ("gb1", gb, 1)):
                us = u_in2[nm]
                for tb in range(2):
                    for i, u in enumerate(us):
                        pump(u)
                        tok = part(u, (AH, AL, 4 * i, tb, 4 + tb, (0, 512), i == 0, i == 1, pairs(k2, 4 * i, 4, tb)),
                                   tb == 1)
                        if i == 0:
                            yield
                    o_ = dst[:, tb, 512 * n:512 * n + 512]
                    gsteps.append(tm(4 + tb, o_, "act", 1.0, tok, t_ka, t_qa, t_qb, rrf, rawf))
                    yield

        gs = gates()

        def gfill():
            next(gs, None)

        def attend(name, qT_, kTs, vs, bias_, O_, btok, col, obs, extra):
            S, E, TR, PTt, PVt = {}, {}, {}, {}, {}

            def scores(h):
                b = h % 2
                r_ = slice(64 * (h % 2), 64 * (h % 2) + 64)
                w = bfree[b]
                bfree[b] = []
                kk = kTs(h)
                mm(bank[b][:, 128:256], qT_[r_, h // 2, 0:128], kk[r_, 0:128], True, True, w, extra)
                S[h] = mm(bank[b][:, 256:512], qT_[r_, h // 2, 128:256], kk[r_, :], True, True, inc=True)

            def soft(h):
                b = h % 2
                es = []
                fr = []
                for tb in range(2):
                    cc = slice(0, 128) if tb == 0 else slice(128, 384)
                    pc = slice(128, 256) if tb == 0 else slice(256, 512)
                    i = col + 2 * h + tb
                    m1 = mneg[:, i:i + 1]
                    mg = rl[:, i:i + 1]
                    a = dve(lambda q, cc=cc, pc=pc, m1=m1: q.tensor_tensor_reduce(
                        out=s2[b][:, cc], in0=bank[b][:, pc], in1=bias_[:, cc], scale=1.0, scalar=SENT,
                        op0=ALU.add, op1=ALU.max, accum_out=m1), S[h], btok, E.get(h - 2))
                    fr.append(a)
                    g = tsc(mg, m1, -1.0, None, ALU.mult, None, a)
                    es.append(act(lambda q, cc=cc, mg=mg, i=i: q.activation(
                        P2[b][:, cc], s2[b][:, cc], ACT.Exp, bias=mg, accum_out=lsum[:, i:i + 1]), g, TR.get(h - 2)))
                bfree[b] = fr
                E[h] = es

            def turn(h):
                b, tk = transposes([(i, P2[h % 2][:, i * 128:i * 128 + 128]) for i in range(3)], E[h])
                TR[h] = tk
                t = copy("act" if h % 2 else "dve", PT2[h % 2][:, :], bank[b][:, 0:384], tk, PVt.get(h - 2))
                bfree[b] = [t]
                PTt[h] = t

            def pv(h):
                w = [PTt[h], extra]
                if h == 0:
                    w += [bfree[obs[0]], bfree[obs[1]]]
                    bfree[obs[0]] = bfree[obs[1]] = []
                v = vs(h)
                hc = slice(h * 64, h * 64 + 64)
                mm(bank[obs[0]][:, hc], PT2[h % 2][:, 0:128], v[0], True, True, w)
                mm(bank[obs[1]][:, hc], PT2[h % 2][:, 128:256], v[0], True, False)
                PVt[h] = mm(bank[obs[1]][:, hc], PT2[h % 2][:, 256:384], v[1], False, True, inc=True)

            scores(0)
            for h in range(NH):
                soft(h)
                if h + 1 < NH:
                    scores(h + 1)
                gfill()
                background(6)()
                if h:
                    pv(h - 1)
                turn(h)
            pv(NH - 1)
            t = dve(lambda q: q.reciprocal(rl[:, 32 + col:48 + col], lsum[:, col:col + 16]), E[NH - 1])
            rv_ = rl[:, 32 + col:48 + col].rearrange("p (h t) -> p h t", t=2)
            return [o_out(O_, obs[tb], tb, rv_[:, :, tb], t, PVt[NH - 1]) for tb in range(2)], E[NH - 1]

        gfill()
        t_oa, _ = attend("a", qaT, lambda h: kaT[:, h // 2, :],
                         lambda h: [va[:, i, h * 64:h * 64 + 64] for i in range(2)], lnC, Oa, t_lnC, 0, (2, 3),
                         [t_qa, t_ka, t_va, k2, tx_2])
        background(500)()
        gfill()
        t_ob, last_e = attend("b", qbT, lambda h: kbT[:, :],
                              lambda h: [small[:, i, 64:128] for i in range(2)], mB, Ob, st["mB"], 16, (2, 3),
                              [t_qb, t_kiT, k2, tx_2])
        for _ in range(20):
            gfill()
        t_ga = act(lambda q: q.activation(flat(ga[:, :, :]), flat(ga[:, :, :]), ACT.Sigmoid), gsteps)
        t_gb = act(lambda q: q.activation(flat(gb[:, :, :]), flat(gb[:, :, :]), ACT.Sigmoid), gsteps)

        ky = []
        att_pe = ("pe", value["pe"])
        for i, (O_, t_) in enumerate(((Oa, t_oa), (Ob, t_ob))):
            sp_ = [split_tb(O_, 4, YH[i], YL[i], 0, tb, t_[tb], att_pe) for tb in range(2)]
            ky.append([[sp_[0][0], sp_[1][0]]] * 4)
        ypt = ("pe", value["pe"])
        t_m = {}
        for i, us in ((0, u_upa), (1, u_upb)):
            for tb in range(2):
                for n in range(2):
                    pump(us[n])
                    r = part(us[n], (YH[i], YL[i], 0, tb, 2 * n + tb, (0, 512), True, True, pairs(ky[i], 0, 4, tb)),
                             tb == 1)
                    gv = (ga if i == 0 else gb)[:, tb, 512 * n:512 * n + 512]
                    mv = mrg[:, tb, 512 * n:512 * n + 512]
                    if i == 0:
                        t = tt(mv, bank[2 * n + tb][:, :], gv, ALU.mult, r, t_ga, ypt)
                        bfree[2 * n + tb] = [t]
                        t_m[n, tb] = t
                    else:
                        t = tt(mt[tb][:, :], bank[2 * n + tb][:, :], gv, ALU.mult, r, t_gb, t_m.get(("f", tb)), ypt)
                        bfree[2 * n + tb] = [t]
                        t_m[n, tb] = tt(mv, mv, mt[tb][:, :], ALU.add, t, t_m[n, tb])
                        t_m["f", tb] = t_m[n, tb]
        allm = [t_m[n, tb] for n in range(2) for tb in range(2)]
        km = [[None, None] for _ in range(8)]
        for tb in range(2):
            for i in range(2):
                tk, _ = split_tb(mrg[:, :, 512 * i:512 * i + 512], 4, AH, AL, 4 * i, tb, t_m[0, tb], t_m[1, tb], att_pe)
                for k in range(4):
                    km[4 * i + k][tb] = tk
        ready = [[], []]
        sq = [[], []]

        def out2(n, tb, tok):
            t = residual(n, tb, 2 * n + tb, tok, None, xr, tx_2)
            ready[tb].append(t)
            sq[tb].append(square(X[:, tb, halves(n)], S1[:, tb, halves(n)], t, allm, km))

        us_out = [(u_out2[n][i], n, 4 * i, i == 0, i == 1) for i in range(2) for n in range(2)]
        kk_out = [km[0:4], km[4:8]]
        out_parts(us_out, 0, kk_out, out2)
        wo0 = ("pe", value["pe"])
        r_, rt_ = rstd(sq[0])
        tx_f = [norm_scale(X, 0, r_, rt_)]
        out_parts(us_out[0:2], 1, kk_out, out2)
        kf = [[t, None] for t in norm_turn(0, tx_f[0], AH, AL, v_ffn, None, wo0)]
        out_parts(us_out[2:4], 1, kk_out, out2)
        wo_pe = ("pe", value["pe"])
        r_, rt_ = rstd(sq[1])
        tx_f.append(norm_scale(X, 1, r_, rt_))
        attn_done = [wo_pe, allm]
        hid_free = [[wo_pe, allm], [wo_pe, allm]]
        hh_free = [[wo_pe, allm], [wo_pe, allm]]
        hh_tok.clear()

        def upg(c, tb):
            bk = 4 + tb
            r = half_chunk(u_gu[c], kf, tb, bk)
            rv_ = rel[tb][:, 0:256]
            a = act(lambda q: q.activation(rv_, bank[bk][:, 0:256], ACT.Silu), r, st.get(("sq2", tb)), attn_done)
            s = tt(hid[c % 2][:, tb, 0:256], bank[bk][:, 256:512], rv_, ALU.mult, a, hid_free[c % 2])
            bfree[bk] = [s]
            st["sq2", tb] = s
            st["hid", c, tb] = s

        ff = feed_forward(11, 2, upg, u_dn, lambda: turn_late(kf, tx_f[1], AH, AL, v_ffn, None, wo_pe))
        t_out = []
        for r_, tb in ff:
            sq_ = []
            for n in range(2):
                t = residual(n, tb, 2 * n + tb, r_[n], None, ready, tx_f)
                sq_.append(square(X[:, tb, halves(n)], S1[:, tb, halves(n)], t, kf))
            r_, rt_ = rstd(sq_)
            t = stt(S1[:, tb, :], X[:, tb, :], r_, g2b[:, :], ALU.mult, ALU.mult, rt_, t_nf, kf)
            t_out.append(dma("sp", out[tb * 128:tb * 128 + 128, :], S1[:, tb, :], f"d_o{tb}", t))
        prog["sp"].append((t_out, None, None, 0))
        assert state["l"] == len(units) and state["s"] == len(units)

        sems = {s: ctx.enter_context(nc.semaphore(f"s_{s}")) for s in value}
        block = ctx.enter_context(nc.Block())

        def emit(name):
            def run(eng):
                for waits, fn, sem, by in prog[name]:
                    for s, v in waits:
                        eng.wait_ge(sems[s], v)
                    if fn is not None:
                        ins = fn(eng)
                        if sem is not None:
                            ins.then_inc(sems[sem], by)
            return run

        block.sync(emit("sp"))
        block.gpsimd(emit("pool"))
        block.scalar(emit("act"))
        block.vector(emit("dve"))
        block.tensor(emit("pe"))


def rope_tables(pos_of, width):
    n = width // 2
    t = np.arange(T)
    inv = np.float32(10000.0) ** (-np.arange(n, dtype=np.float32) / np.float32(n))
    cols_c, cols_s = [], []
    for pos in pos_of(t):
        ang = pos.astype(np.float32)[:, None] * inv[None, :].astype(np.float32)
        c, s = np.cos(ang.astype(np.float32)), np.sin(ang.astype(np.float32))
        cols_c += [c, c]
        cols_s += [-s, s]
    tab = np.stack([np.concatenate(cols_c, 1), np.concatenate(cols_s, 1)], 1).astype(np.float32)
    return np.ascontiguousarray(tab.reshape(2, 128, 2, 64).transpose(1, 0, 2, 3))


def packed(m):
    return np.ascontiguousarray(np.concatenate([m[:128, :128], m[128:, :]], 1).astype(np.float32))


def kernel(**inputs):
    import concourse.bacc as bacc
    from concourse.bass_utils import run_bass_kernel_spmd

    a = {k: np.asarray(v) for k, v in inputs.items()}

    def fm(v):
        v = v.reshape(-1)
        return v.reshape(-1, 128).T

    bada = a["b_ada"].reshape(-1)
    comb = np.zeros((128, 2), np.float32)
    comb[[0, 1, 2, 3], [0, 1, 0, 1]] = 1.0
    vec = np.concatenate([
        fm(a["norm1_g"]), fm(a["norm2_g"]), fm(bada[0:2048]), fm(bada[3072:5120]),
        a["dw_kernel"][0].reshape(31, 4, 128).transpose(2, 1, 0).reshape(128, 124),
        fm(a["dw_bias"]), fm(a["conv_ln_g"]), fm(a["conv_ln_b"]), fm(a["norm_mix_2"]), fm(a["norm_ffn_2"]),
        np.concatenate([comb, np.zeros((128, 22), np.float32)], 1)], 1)
    cs = np.stack([a["c"].reshape(8, 128), a["c_ctx"].reshape(8, 128)], -1).transpose(1, 0, 2).reshape(128, 16)

    t = np.arange(T)
    row, col = t // 64, t % 64
    start = np.clip(col - 8, 0, 48)
    roff = np.clip(row[None, :] - row[:, None] + 7, 0, 14)
    coff = col[None, :] - col[:, None] + 15
    inside = (col[None, :] >= start[:, None]) & (col[None, :] < start[:, None] + 16)
    rpb = a["rpb"][0]
    rb = np.where(inside[None], rpb[:, roff, np.clip(coff, 0, 30)], np.float32(NEG)).astype(np.float32)

    q, k = t[:, None], t[None, :]
    count = ((q - k >= 0) & (q - k <= 128)).astype(int) + ((q >= k) & ((q - k) % 4 == 0)) + ((q >= k) & ((q - k) % 16 == 0))
    lnC = np.where(count > 0, np.log(np.maximum(count, 1).astype(np.float32)), np.float32(NEG))
    caus = np.where(q >= k, np.float32(0), np.float32(NEG))

    arrays = {
        "vec": vec, "cs": cs, "x": a["x"][0], "ctx": a["ctx"][0], "ident": np.eye(128, dtype=np.float32),
        "rope1": rope_tables(lambda t: (t // 64, t % 64), 32), "rope2": rope_tables(lambda t: (t,), 64),
        "lnC": packed(lnC), "caus": packed(caus), "b_ada": bada.reshape(1, -1),
        "rpb": rb, "final_g": a["final_g"].reshape(1, -1), "norm_final": a["norm_final_2"].reshape(1, -1),
    }
    for n in ("w_ada", "w_in", "w_out", "w_mlp1", "w_mlp2", "w_in_2", "w_up_a_2", "w_up_b_2", "w_out_2",
              "w_gate_2", "w_up_2", "w_down_2"):
        arrays[n] = a[n][0]
    arrays = {f"in_{k}": np.ascontiguousarray(v) for k, v in arrays.items()}
    nc = bacc.Bacc("TRN2", target_bir_lowering=False, num_devices=1)
    d = {k[3:]: nc.dram_tensor(k, v.shape, mybir.dt.from_np(v.dtype), kind="ExternalInput").ap()
         for k, v in arrays.items()}
    out = nc.dram_tensor("out", (T, D), F32, kind="ExternalOutput").ap()
    build_program(nc, d, out)
    res = run_bass_kernel_spmd(nc, [arrays], core_ids=[0])
    return res.results[0]["out"].reshape(1, T, D)
```

```python
import numpy as np
import concourse.bass as bass
from concourse import mybir
from contextlib import ExitStack

F32 = mybir.dt.float32
F32R = mybir.dt.float32r
ALU = mybir.AluOpType
ACT = mybir.ActivationFunctionType
AX = mybir.AxisListType

D = 1024
T = 256
NH = 8
EPS = 1e-6
NEG = -1e30
SENT = -3e38
IDX_SCALE = (64 ** -0.5) * (8 ** -0.5)
FF2 = 2816

KB = 1024
RW = 4
RH = 4
AHEAD = 3
AHEAD_ADA = 1
AHEAD_FIRST = 3
UB = 8 * KB


def build_program(nc, d, out):
    ctx = ExitStack()
    with ctx:
        base = 16512

        def at(name, off_kb, shape, dt=F32):
            return nc.alloc_sbuf_tensor_at(name, shape, dt, offset=base + int(off_kb * KB))

        W32 = [at(f"W32_{i}", 8 * i, [128, 2048]) for i in range(RW)]
        WH = [at(f"WH_{i}", 32 + 8 * i, [128, 2048], F32R) for i in range(RH)]
        WL = [at(f"WL_{i}", 64 + 8 * i, [128, 2048], F32R) for i in range(RH)]
        X = at("X", 96, [128, 2, D])
        o = 104
        g1b = at("g1b", o, [128, D])
        g2b = at("g2b", o + 4, [128, D])
        lnC = at("lnC", o + 8, [128, 384])
        caus = at("caus", o + 9.5, [128, 384])
        rope1 = at("rope1", o + 11, [128, 2, 2, 64])
        rope2 = at("rope2", o + 12, [128, 2, 2, 64])
        ident = at("ident", o + 13, [128, 128])
        ones = at("ones", o + 13.5, [128, 128])
        vec = at("vec", o + 14, [128, 224])
        csx = at("csx", o + 14.875, [128, 8, 4], F32R)
        cs = at("cs", o + 15, [128, 16])
        mod1 = at("mod1", o + 15.125, [128, 16, 2])
        mod2 = at("mod2", o + 15.25, [128, 16, 2])
        A1 = at("A1", o + 15.375, [128, 2, 8])
        A2 = at("A2", o + 15.4375, [128, 8])
        stat = at("stat", o + 16.6875, [128, 96])
        mneg = at("mneg", o + 15.625, [128, 64])
        lsum = at("lsum", o + 15.875, [128, 64])
        rl = at("rl", o + 16.125, [128, 64])
        best = at("best", o + 16.375, [128, 2, 8])
        m0 = 121.75

        def M(name, off, shape, dt=F32):
            return at(name, m0 + off, shape, dt)

        S1 = M("S1", 0, [128, 2, D])
        S2 = M("S2", 8, [128, 2048])
        AH = M("AH", 16, [128, 8, 256], F32R)
        AL = M("AL", 24, [128, 8, 256], F32R)
        CH = M("CH", 32, [128, 8, 256], F32R)
        CL = M("CL", 40, [128, 8, 256], F32R)
        rows1 = [M(f"rows1_{i}", 32 + 2 * i, [4, 512]) for i in range(4)]
        XC = M("XC", 48, [128, 2, D])
        XC2 = M("XC2", 56, [128, 2, D])
        hTc = M("hTc", 0, [128, 8, 256])
        Q = M("Q", 48, [128, 2, 512])
        Kt = M("Kt", 52, [128, 2, 512])
        V = M("V", 56, [128, 2, 512])
        KC = M("KC", 60, [128, 2, 512])
        VC = M("VC", 64, [128, 2, 512])
        U = M("U", 68, [128, 2, 512])
        G = M("G", 72, [128, 2, 512])
        cacc = M("cacc", 72, [128, 4, 256])
        ccen = M("ccen", 68, [128, 4, 256])
        hp = M("hp", 76, [128, 4, 288])
        csq = M("csq", 76, [128, 4, 256])
        tmp = M("tmp", 80.5, [128, 512])
        QR = M("QR", 0, [128, 2, 512])
        KR = M("KR", 4, [128, 2, 512])
        qrT = M("qrT", 32, [128, 4, 256])
        qT = M("qT", 36, [128, 4, 256])
        kT = M("kT", 40, [128, 4, 256])
        kcT = M("kcT", 44, [128, 4, 256])
        bias = [M(f"bias{i}", 8 + 2 * i, [128, 2, 256]) for i in range(4)]
        O1 = M("O1", 0, [128, 2, 512])
        rows2 = [M(f"rows2_{i}", 4 + 2 * i, [4, 512]) for i in range(2)]
        P1 = [M(f"P1_{i}", 48 + 2 * i, [128, 512]) for i in range(2)]
        PT1 = [M(f"PT1_{i}", (52, 54, 83)[i], [128, 512]) for i in range(3)]
        s1 = [M(f"s1_{i}", 60 + i, [128, 256]) for i in range(2)]
        crs = M("crs", 62, [128, 256])
        hid = [M(f"hid{i}", 32 + 4 * i, [128, 2, 512]) for i in range(2)]
        HH = [M(f"HH{i}", 40 + 4 * i, [128, 4, 256], F32R) for i in range(2)]
        HL = [M(f"HL{i}", 48 + 4 * i, [128, 4, 256], F32R) for i in range(2)]
        rel = [M(f"rel{i}", 56 + 2 * i, [128, 512]) for i in range(2)]
        raw = [M(f"raw{i}", 32 + 4 * i, [128, 2, 512]) for i in range(2)]
        rr = [M(f"rr{i}", 40 + 4 * i, [128, 2, 512]) for i in range(2)]
        qiT = M("qiT", 48, [128, 4, 256])
        qbT = M("qbT", 52, [128, 4, 256])
        qaT = M("qaT", 56, [128, 4, 256])
        kaT = M("kaT", 60, [128, 4, 256])
        va = M("va", 64, [128, 2, 512])
        kiT = M("kiT", 68, [128, 256])
        kbT = M("kbT", 69, [128, 256])
        small = M("small", 70, [128, 2, 200])
        skk = [M(f"skk{i}", 72 + i, [128, 2, 128]) for i in range(2)]
        Ob = M("Ob", 74, [128, 2, 512])
        mB = M("mB", 78, [128, 384])
        P2 = [M(f"P2_{i}", 1.5 * i, [128, 384]) for i in range(2)]
        PT2 = [M(f"PT2_{i}", (3, 4.5, 83)[i], [128, 384]) for i in range(3)]
        s2 = [M(f"s2_{i}", 6 + 1.5 * i, [128, 384]) for i in range(2)]
        rlu = [M(f"rlu{i}", 9 + 1.5 * i, [128, 384]) for i in range(2)]
        Oa = M("Oa", 12, [128, 2, 512])
        sco = M("sco", 74, [128, 384])
        ga = M("ga", 32, [128, 2, D])
        gb = M("gb", 40, [128, 2, D])
        YH = [M(f"YH{i}", 56 - 8 * i, [128, 4, 256], F32R) for i in range(2)]
        YL = [M(f"YL{i}", 60 - 8 * i, [128, 4, 256], F32R) for i in range(2)]
        mrg = M("mrg", 0, [128, 2, D])
        mt = [M(f"mt{i}", 64 + 2 * i, [128, 512]) for i in range(2)]

        bank = [ctx.enter_context(nc.psum_tensor(f"bank{i}", [128, 512], F32)) for i in range(8)]
        bfree = [[] for _ in range(8)]

        prog = {e: [] for e in ("pe", "act", "dve", "pool", "sp")}
        value = {}
        seen = {e: {} for e in prog}

        def waits_of(e, toks):
            need = {}
            todo = list(toks)
            while todo:
                t = todo.pop()
                if t is None:
                    continue
                if isinstance(t, list):
                    todo.extend(t)
                    continue
                need[t[0]] = max(need.get(t[0], 0), t[1])
            outw = []
            for s, v in need.items():
                if seen[e].get(s, 0) < v:
                    seen[e][s] = v
                    outw.append((s, v))
            return outw

        def op(e, fn, *toks, inc=True):
            w = waits_of(e, toks)
            if inc:
                value[e] = value.get(e, 0) + 1
            prog[e].append((w, fn, e if inc else None, 1))
            return (e, value.get(e, 0)) if inc else None

        def dma(e, dst, src, sem, *toks):
            w = waits_of(e, toks)
            value[sem] = value.get(sem, 0) + 16
            prog[e].append((w, lambda q, dst=dst, src=src: q.dma_start(dst, src), sem, 16))
            return (sem, value[sem])

        def pe(fn, *t, inc=True):
            return op("pe", fn, *t, inc=inc)

        def act(fn, *t):
            return op("act", fn, *t)

        def dve(fn, *t):
            return op("dve", fn, *t)

        def mm(o_, l, r, start, stop, *t, inc=False):
            return pe(lambda e: e.matmul(o_, l, r, start=start, stop=stop), *t, inc=inc)

        def copy(e, o_, i_, *t):
            if e == "act":
                return act(lambda q: q.activation(o_, i_, ACT.Copy), *t)
            return dve(lambda q: q.tensor_copy(o_, i_), *t)

        def tt(o_, a, b, alu, *t):
            return dve(lambda q: q.tensor_tensor(o_, a, b, alu), *t)

        def tsc(o_, a, s1_, s2_, a0, a1, *t):
            if a1 is None:
                return dve(lambda q: q.tensor_scalar(o_, a, s1_, None, a0), *t)
            return dve(lambda q: q.tensor_scalar(o_, a, s1_, s2_, a0, a1), *t)

        def stt(o_, a, s, b, a0, a1, *t):
            return dve(lambda q: q.scalar_tensor_tensor(o_, a, s, b, a0, a1), *t)

        units = []

        def add_unit(parts, lo="dve"):
            units.append((parts, lo))
            return len(units) - 1

        def unit_of(w, k0, nk, cols, lo="dve"):
            wid = sum(c[1] for c in cols)
            parts, c0 = [], 0
            for n0, cw in cols:
                src = w[k0 * 128:(k0 + nk) * 128, n0:n0 + cw].rearrange("(k p) n -> p k n", p=128)
                parts.append((c0, cw, src))
                c0 += cw
            return add_unit((nk, wid, parts), lo)

        rel_w32 = {}
        rel_hl = []
        unit_dma = {}
        unit_tok = {}
        unit_slot = {}
        state = {"l": 0, "s": 0, "ahead": AHEAD_ADA}

        def w32_view(u):
            nk, wid, _ = units[u][0]
            return W32[u % RW][:, 0:nk * wid].rearrange("p (k n) -> p k n", k=nk)

        def pump(u):
            moved = True
            while moved:
                moved = False
                n = state["l"]
                if n < len(units) and (n < RW or (n - RW) in rel_w32):
                    (nk, wid, parts), _ = units[n]
                    v = w32_view(n)
                    for c0, cw, src in parts:
                        tk = dma("sp", v[:, :, c0:c0 + cw], src, f"w{n % RW}", rel_w32.get(n - RW))
                    unit_dma[n] = tk
                    state["l"] += 1
                    moved = True
                n = state["s"]
                if n < len(units) and n <= u + state["ahead"] and n in unit_dma:
                    k = len(unit_slot)
                    if k >= RH and len(rel_hl) <= k - RH:
                        continue
                    free = rel_hl[k - RH] if k >= RH else None
                    nk, wid, _ = units[n][0]
                    sl = k % RH
                    w, h, l = W32[n % RW], WH[sl], WL[sl]
                    ts = []
                    for p in range(0, nk, nk // 2):
                        c = slice(p * wid, (p + nk // 2) * wid)
                        a = act(lambda q, h=h, w=w, c=c: q.activation(h[:, c], w[:, c], ACT.Copy), unit_dma[n], free)
                        b = op(units[n][1], lambda q, l=l, w=w, h=h, c=c: q.tensor_tensor(
                            l[:, c], w[:, c], h[:, c].bitcast(F32), ALU.subtract), a, unit_dma[n], free)
                        ts += [[a, b]] * (nk // 2)
                    unit_slot[n] = sl
                    unit_tok[n] = ts
                    rel_w32[n] = ts
                    state["s"] += 1
                    moved = True

        def part(u, target, last_use):
            H, L, k0, tb, bk, (c0, cw), first, last, tk = target
            nk, wid, _ = units[u][0]
            sl = unit_slot[u]
            wh = WH[sl][:, 0:nk * wid].rearrange("p (k n) -> p k n", k=nk)
            wl = WL[sl][:, 0:nk * wid].rearrange("p (k n) -> p k n", k=nk)
            w = [tk] + ([bfree[bk]] if first else [])
            if first:
                bfree[bk] = []
            po = bank[bk][:, 0:cw]
            for k in range(nk):
                hs = H[:, k0 + k, tb * 128:tb * 128 + 128]
                ls = L[:, k0 + k, tb * 128:tb * 128 + 128]
                mm(po, hs, wh[:, k, c0:c0 + cw], first and k == 0, False, w, unit_tok[u][k])
                mm(po, hs, wl[:, k, c0:c0 + cw], False, False)
                tok = mm(po, ls, wh[:, k, c0:c0 + cw], False, last and k == nk - 1, inc=(k == nk - 1))
                w = []
            if last_use:
                rel_hl.append(tok)
            return tok

        wada, win, wout, wm1, wm2 = (d[n] for n in ("w_ada", "w_in", "w_out", "w_mlp1", "w_mlp2"))
        win2, wua, wub, wout2, wg, wu, wd = (d[n] for n in (
            "w_in_2", "w_up_a_2", "w_up_b_2", "w_out_2", "w_gate_2", "w_up_2", "w_down_2"))

        def col_units(w, cols, kt=8, lo="dve"):
            return [unit_of(w, k0, 4, cols, lo) for k0 in range(0, kt, 4)]

        def lo_first(u):
            return "pool" if u in (4,9) else "dve"

        u_ada1, u_in = {}, {"a": [], "b": []}
        for nm, h in (("ada", 0), ("a", 0), ("ada", 1), ("b", 0), ("a", 1), ("b", 1)):
            if nm == "ada":
                for n in (h, 2 + h):
                    u_ada1[n] = [unit_of(wada, k0, 4, [(512 * n, 512)], lo_first(len(units))) for k0 in (0, 4)]
            else:
                u_in[nm].append(unit_of(win, 4 * h, 4, [({"a": 1536, "b": 2048}[nm], 512)], lo_first(len(units))))
        for nm, c0 in (("k", 512), ("q", 0), ("v", 1024)):
            u_in[nm] = col_units(win, [(c0, 512)], lo="pool")
        u_ada2 = [(nm, n, [unit_of(wada, k0, 4, [(c0 + 512 * n, 512)], "pool")
                           for k0 in (0, 4)])
                  for nm, c0 in (("sh", 3072), ("sc", 4096), ("g1", 2048), ("g2", 5120)) for n in range(2)]
        u_out = [unit_of(wout, k0, 4, [(512 * n, 512)], "pool") for k0 in (4, 0) for n in range(2)]
        u_m1, u_m2 = [], []
        for c in range(8):
            u_m1.append(col_units(wm1, [(512 * c, 512)], lo="dve" if c else "pool"))
            if c:
                u_m2.append([unit_of(wm2, 4 * (c - 1) + 2 * j, 2, [(0, 1024)]) for j in range(2)])
        u_m2.append([unit_of(wm2, 28 + 2 * j, 2, [(0, 1024)]) for j in range(2)])
        u_in2 = {}
        for nm, cols in (("qi", [(2176, 512)]), ("s", [(2048, 128), (2688, 72)]), ("qb", [(1536, 512)]),
                         ("qa", [(0, 512)]), ("ka", [(512, 512)]), ("va", [(1024, 512)]),
                         ("ga0", [(2760, 512)]), ("ga1", [(3272, 512)]), ("gb0", [(3784, 512)]),
                         ("gb1", [(4296, 512)])):
            lo = "pool" if nm in ("s", "qb", "qa", "ka", "va", "ga0", "ga1", "gb0", "gb1") else "dve"
            u_in2[nm] = [unit_of(win2, k0, 4, cols, "pool" if nm == "qi" else lo) for k0 in (0, 4)]
        u_upa = [unit_of(wua, 0, 4, [(512 * n, 512)], "pool") for n in range(2)]
        u_upb = [unit_of(wub, 0, 4, [(512 * n, 512)], "pool") for n in range(2)]
        u_out2 = [[None, None], [None, None]]
        for i in range(2):
            for n in range(2):
                u_out2[n][i] = unit_of(wout2, 4 * i, 4, [(512 * n, 512)], "pool")
        u_gu, u_dn = [], []
        for c in range(11):
            u_gu.append(None)
            u_dn.append(None)
        for c in range(12):
            if c < 11:
                u_gu[c] = []
                for k0 in (0, 4):
                    sg = wg[k0 * 128:(k0 + 4) * 128, 256 * c:256 * c + 256].rearrange("(k p) n -> p k n", p=128)
                    su = wu[k0 * 128:(k0 + 4) * 128, 256 * c:256 * c + 256].rearrange("(k p) n -> p k n", p=128)
                    u_gu[c].append(add_unit((4, 512, [(0, 256, sg), (256, 256, su)]), "dve" if c else "pool"))
            if c:
                u_dn[c - 1] = [unit_of(wd, 2 * (c - 1), 2, [(0, 1024)])]

        def tokmaj(ap):
            return ap.rearrange("(t p) n -> p t n", p=128)

        t_cs = dma("act", cs[:, :], d["cs"], "d_cs")
        pump(-AHEAD - 1)
        t_x = dma("act", X[:, :, :], tokmaj(d["x"]), "d_x")
        t_vec = dma("pool", vec[:, :], d["vec"], "d_vec")
        t_ident = dma("pool", ident[:, :], d["ident"], "d_id")
        bada = d["b_ada"]
        t_ones = op("pool", lambda q: q.memset(ones[:, :], 1.0))
        v_n1, v_n2, v_b1, v_b2 = vec[:, 0:8], vec[:, 8:16], vec[:, 16:32], vec[:, 32:48]
        v_dw = vec[:, 48:172].rearrange("p (c j) -> p c j", c=4)
        v_dwb, v_lng, v_lnb = vec[:, 172:176], vec[:, 176:180], vec[:, 180:184]
        v_mix, v_ffn = vec[:, 184:192], vec[:, 192:200]
        t_eps = dve(lambda q: q.memset(stat[:, 94:95], -0.5))
        t_eps2 = dve(lambda q: q.memset(stat[:, 95:96], EPS))

        t_cs = act(lambda q: q.activation(cs[:, :], cs[:, :], ACT.Silu), t_cs)
        csv = cs[:, :].rearrange("p (k r) -> p k r", r=2)
        t_ch = dve(lambda q: q.tensor_copy(csx[:, :, 0:2], csv), t_cs)
        t_csx = [t_ch, tt(csx[:, :, 2:4], csv, csx[:, :, 0:2].bitcast(F32), ALU.subtract, t_ch)]
        comb = vec[0:4, 200:202]

        tq = {"n": 0}

        def tbank():
            b = 6 + tq["n"] % 2
            tq["n"] += 1
            w = bfree[b]
            bfree[b] = []
            return b, w

        def transposes(blocks, *toks):
            b, w = tbank()
            for i, (c, src) in enumerate(blocks):
                dst = bank[b][:, c * 128:c * 128 + 128]
                tk = pe(lambda e, dst=dst, src=src: e.transpose(dst, src, ident[:, :]),
                        w, list(toks), t_ident, inc=(i == len(blocks) - 1))
            return b, tk

        def to_features(src, nj, dst, eng, *toks):
            outt, pet = [], []
            for j in range(0, nj, 2):
                n = min(2, nj - j)
                b, tk = transposes([(2 * i + tb, src[:, tb, (j + i) * 128:(j + i) * 128 + 128])
                                    for i in range(n) for tb in range(2)], *toks)
                pv = bank[b][:, 0:n * 256].rearrange("p (j n) -> p j n", j=n)
                t = copy(eng[(j // 2) % len(eng)], dst[:, j:j + n, :], pv, tk)
                bfree[b] = [t]
                outt.append(t)
                pet.append(tk)
            return outt, pet

        def flat(ap):
            return ap.rearrange("p a b -> p (a b)")

        def split_tb(src, nj, H, L, k0, tb, *toks):
            b, tk = transposes([(i, src[:, tb, i * 128:i * 128 + 128]) for i in range(nj)], *toks)
            pv = bank[b][:, 0:nj * 128].rearrange("p (j n) -> p j n", j=nj)
            hv = H[:, k0:k0 + nj, tb * 128:tb * 128 + 128]
            lv = L[:, k0:k0 + nj, tb * 128:tb * 128 + 128]
            a = act(lambda q: q.activation(hv, pv, ACT.Copy), tk, list(toks))
            c = tt(lv, pv, hv.bitcast(F32), ALU.subtract, a, tk, list(toks))
            bfree[b] = [c]
            return [a, c], tk

        nstat = {"n": 0}

        def col():
            nstat["n"] += 1
            assert nstat["n"] <= 94
            return stat[:, nstat["n"] - 1:nstat["n"]]

        def square(src, junk, *toks):
            c = col()
            return c, act(lambda q: q.activation(junk, src, ACT.Square, scale=1.0 / 32, accum_out=c), *toks)

        def power(src, t):
            c = col()
            return c, op("pool", lambda q: q.tensor_tensor(c, src, stat[:, 94:95], ALU.pow), t, t_eps)

        def rstd(parts):
            c = col()
            s0, t0 = parts[0]
            if len(parts) == 2:
                m = tsc(c, s0, parts[1][0], EPS, ALU.add, ALU.add, t0, parts[1][1])
            else:
                m = tsc(c, s0, EPS, None, ALU.add, None, t0)
            return power(c, m)

        hTv = S2[:, :].rearrange("p (k t) -> p k t", k=8)

        def norm_scale(src, tb, r, rt_, *free):
            return [tsc(S1[:, tb, 0:512], src[:, tb, 0:512], r, None, ALU.mult, None, rt_, list(free)),
                    act(lambda q: q.activation(S1[:, tb, 512:1024], src[:, tb, 512:1024], ACT.Copy, scale=r),
                        rt_, list(free))]

        def norm_turn(tb, tx, H, L, Av, Bv, *free):
            toks = []
            for i in range(2):
                b, tk = transposes([(j, S1[:, tb, (4 * i + j) * 128:(4 * i + j) * 128 + 128]) for j in range(4)], tx[i])
                ts = slice(tb * 128, tb * 128 + 128)
                ks = slice(4 * i, 4 * i + 4)
                sv, hv, lv = hTv[:, ks, ts], H[:, ks, ts], L[:, ks, ts]
                if i == 1:
                    ev = [act(lambda q, j=j: q.activation(
                        hTv[:, 4 + j, ts], bank[b][:, j * 128:j * 128 + 128], ACT.Identity,
                        bias=Bv[:, 4 + j:5 + j] if Bv is not None else 0.0, scale=Av[:, 4 + j:5 + j]), tk, list(free))
                        for j in range(4)]
                    bfree[b] = ev
                else:
                    pv = bank[b][:, :].rearrange("p (j n) -> p j n", j=4)
                    ev = tt(sv, pv, Av[:, ks].unsqueeze(2).to_broadcast([128, 4, 128]), ALU.mult, tk, list(free))
                    bfree[b] = [ev]
                    if Bv is not None:
                        ev = tt(sv, sv, Bv[:, ks].unsqueeze(2).to_broadcast([128, 4, 128]), ALU.add, ev)
                a = copy("act" if i else "dve", hv, sv, ev, list(free))
                c = tt(lv, sv, hv.bitcast(F32), ALU.subtract, a, ev, list(free))
                toks += [[a, c]] * 4
            return toks

        def residual(n, tb, bk, tok, gate, *free):
            xv = X[:, tb, 512 * n:512 * n + 512]
            yv = S1[:, tb, 512 * n:512 * n + 512]
            if gate is None:
                t = tt(xv, bank[bk][:, :], xv, ALU.add, tok, list(free))
                bfree[bk] = [t]
            else:
                t = tt(yv, bank[bk][:, :], gate[:, 512 * n:512 * n + 512], ALU.mult, tok, list(free))
                bfree[bk] = [t]
                t = tt(xv, xv, yv, ALU.add, t)
            return t

        def halves(n):
            return slice(512 * n, 512 * n + 512)

        def pairs(ktoks, k0, n, tb):
            return [ktoks[k][tb] for k in range(k0, k0 + n)]

        def chunk(us, stats, width=512, after=None, mid=None):
            res = []
            goals = [(s_, tb) for s_ in stats for tb in range(2)]
            for g, ((H, L, kt, bk), tb) in enumerate(goals):
                for i, u in enumerate(us):
                    pump(u)
                    nk = units[u][0][0]
                    tok = part(u, (H, L, nk * i, tb, bk[tb], (0, width), i == 0, i == len(us) - 1,
                                   pairs(kt, nk * i, nk, tb)), g == len(goals) - 1)
                    if after:
                        after()
                res.append(tok)
                if mid and g in mid:
                    mid[g]()
            return res

        def ada_unit(u, k0, bk, first, last):
            pump(u)
            sl = unit_slot[u]
            wh, wl = (x[sl][:, :].rearrange("p (k n) -> p k n", k=4) for x in (WH, WL))
            w = [t_csx] + ([bfree[bk]] if first else [])
            if first:
                bfree[bk] = []
            for k in range(4):
                mm(bank[bk][0:4, :], csx[:, k0 + k, :], wh[:, k, :], first and k == 0, False, w, unit_tok[u][k])
                tk = mm(bank[bk][0:2, :], csx[:, k0 + k, 0:2], wl[:, k, :], False, last and k == 3, inc=(k == 3))
                w = []
            rel_hl.append(tk)
            return tk

        def norm_in(src, ready, xh, *free):
            ts = []
            for tb in range(2):
                r, rt_ = rstd([square(src[:, tb, :], xh[:, tb, :], ready, list(free))])
                ts.append(tsc(xh[:, tb, :], src[:, tb, :], r, None, ALU.mult, None, rt_))
            return ts

        def turn_in(xh, hT, ts, quarters, *free):
            ev, pt = {}, []
            for i in quarters:
                b, tk = transposes([(2 * j + tb, xh[:, tb, (2 * i + j) * 128:(2 * i + j) * 128 + 128])
                                    for j in range(2) for tb in range(2)], ts)
                t = copy("act" if i % 2 else "dve", flat(hT[:, 2 * i:2 * i + 2, :]), bank[b][:, :], tk, list(free))
                bfree[b] = [t]
                ev[2 * i] = ev[2 * i + 1] = t
                pt.append(tk)
            return ev, pt

        def modulate(hT, ev, H, L, r, quarters, *free):
            toks = []
            for i in quarters:
                ab = t_mod[i // 2][r]
                e = []
                for k in (2 * i, 2 * i + 1):
                    A_, B_, h_ = A1[:, r, k:k + 1], modB[:, r, k:k + 1], hT[:, k, :]
                    if i % 2:
                        e.append(act(lambda q, A_=A_, B_=B_, h_=h_: q.activation(h_, h_, ACT.Identity, bias=B_, scale=A_),
                                     ev[k], ab))
                    else:
                        e.append(tsc(h_, h_, A_, B_, ALU.mult, ALU.add, ev[k], ab))
                hv, lv = flat(H[:, 2 * i:2 * i + 2, :]), flat(L[:, 2 * i:2 * i + 2, :])
                sv = flat(hT[:, 2 * i:2 * i + 2, :])
                a = copy("act" if i % 2 else "dve", hv, sv, e, list(free))
                c = tt(lv, sv, hv.bitcast(F32), ALU.subtract, a, e, list(free))
                toks += [[[a, c], [a, c]]] * 2
            return toks

        modB = at("modB", 104 + 17.6875, [128, 2, 8])
        t_mod = []

        def rows_of(n, tk, b, c0, w):
            t = copy("act" if n // 2 else "dve", rows1[n][:, :], bank[4 + n // 2][0:4, :], tk)
            bfree[4 + n // 2] = [t]
            for j in range(4):
                c = c0 + 2 * j
                m = mm(bank[b][:, c:c + 2], rows1[n][:, j * 128:j * 128 + 128], comb, True, True, t, t_vec, w,
                       inc=(j == 3))
            return m

        def first_mod(h, between=None):
            tk = [None, None]
            for g, n in enumerate((h, 2 + h)):
                if g and between:
                    between()
                for i in range(2):
                    tk[g] = ada_unit(u_ada1[n][i], 4 * i, 4 + g, i == 0, i == 1)
            state["ahead"] = (1, 1)[h]
            pump(u_ada1[2 + h][1])
            b, w = tbank()
            m = [rows_of(h, tk[0], b, 0, w), rows_of(2 + h, tk[1], b, 8, w)]
            ks, kc_ = slice(4 * h, 4 * h + 4), slice(8 + 4 * h, 12 + 4 * h)
            ts = []
            for g, k_ in ((1, kc_), (0, ks)):
                ts.append(tt(mod1[:, k_, :], bank[b][:, 8 * g:8 * g + 8].rearrange("p (k r) -> p k r", r=2),
                             v_b1[:, k_].unsqueeze(2).to_broadcast([128, 4, 2]), ALU.add, m[g], t_vec))
            bfree[b] = ts
            t_mod.append([])
            for r in range(2):
                t_mod[h].append([stt(A1[:, r, ks], mod1[:, kc_, r], 1.0, v_n1[:, ks], ALU.add, ALU.mult, ts[0], t_vec),
                                 dve(lambda q, r=r: q.tensor_copy(modB[:, r, ks], mod1[:, ks, r]), ts[1])])
            return ts, m

        tx_x = []
        first_mod(0, lambda: tx_x.extend(norm_in(X, t_x, S1)))
        ev_x, px = turn_in(S1, hTv, tx_x, (0, 1))
        kx = modulate(hTv, ev_x, AH, AL, 0, (0, 1))
        state["ahead"] = AHEAD_FIRST

        def first_parts(nm, h):
            u = u_in[nm][h]
            res = []
            for tb in range(2):
                pump(u)
                bk = 2 * (nm == "b") + tb
                res.append(part(u, (AH, AL, 4 * h, tb, bk, (0, 512), h == 0, h == 1, pairs(kx, 4 * h, 4, tb)), tb == 1))
            return res

        t_xc = dma("sp", XC[:, :, :], tokmaj(d["ctx"]), "d_xc")
        first_parts("a", 0)
        state["ahead"] = 1
        ev2, px2 = turn_in(S1, hTv, tx_x, (2, 3))
        t_mod1, rows_pe = first_mod(1)
        kx += modulate(hTv, ev2, AH, AL, 0, (2, 3))
        state["ahead"] = AHEAD
        first_parts("b", 0)
        tx_c = norm_in(XC, t_xc, XC2)
        ra = first_parts("a", 1)
        rb = first_parts("b", 1)
        t_rope1 = dma("pool", rope1[:, :, :, :], d["rope1"], "d_r1", ra)
        t_g1 = dma("pool", g1b[:, :], bada[0:1, 2048:3072].to_broadcast([128, D]), "d_g1", ra)
        t_g2 = dma("pool", g2b[:, :], bada[0:1, 5120:6144].to_broadcast([128, D]), "d_g2", ra)
        tu = []
        for tb in range(2):
            s = act(lambda q, tb=tb: q.activation(G[:, tb, :], bank[2 + tb][:, :], ACT.Sigmoid), rb[tb])
            bfree[2 + tb] = [s]
            t = tt(U[:, tb, :], bank[tb][:, :], G[:, tb, :], ALU.mult, s, ra[tb])
            bfree[tb] = [t]
            tu.append(t)
        ev_c, pc = turn_in(XC2, hTc, tx_c, range(4), px, px2)
        kc = modulate(hTc, ev_c, CH, CL, 1, range(4), rows_pe)
        t_z = op("pool", lambda q: q.memset(hp[:, :, 0:15], 0.0))
        t_z = op("pool", lambda q: q.memset(hp[:, :, 271:288], 0.0), t_z)
        t_hp = []

        def turn_u():
            for j in range(0, 4, 2):
                b, tk = transposes([(2 * i + tb, U[:, tb, (j + i) * 128:(j + i) * 128 + 128])
                                    for i in range(2) for tb in range(2)], tu)
                t = copy("act", hp[:, j:j + 2, 15:271], bank[b][:, :].rearrange("p (j n) -> p j n", j=2), tk)
                bfree[b] = [t]
                t_hp.append(t)
            bg.append(conv())

        bg = []
        conv_last = [None] * 4

        def conv():
            for j in range(31):
                for c in range(4):
                    src = hp[:, c, j:j + 256]
                    if j == 0:
                        conv_last[c] = tsc(cacc[:, c, :], src, v_dw[:, c, 0:1], v_dwb[:, c:c + 1], ALU.mult, ALU.add,
                                           t_hp, t_z, tu, t_vec)
                    else:
                        conv_last[c] = stt(cacc[:, c, :], src, v_dw[:, c, j:j + 1], cacc[:, c, :],
                                           ALU.mult, ALU.add, conv_last[c])
                    yield

        def background(n):
            def go():
                for _ in range(n):
                    while bg:
                        try:
                            next(bg[0])
                            break
                        except StopIteration:
                            bg.pop(0)
            return go

        def tm(b_, o_, e, scale, tk, *toks):
            pv, = (bank[b_][:, :],)
            if e == "act":
                t = act(lambda q: q.activation(o_, pv, ACT.Copy, scale=scale), tk, list(toks))
            elif scale == 1.0:
                t = dve(lambda q: q.tensor_copy(o_, pv), tk, list(toks))
            else:
                t = tsc(o_, pv, scale, None, ALU.mult, None, tk, list(toks))
            bfree[b_] = [t]
            return t

        def rope(dst, src, nh, tab, s, tb, ready, *free):
            cosv = tab[:, tb, 0, :].unsqueeze(1).to_broadcast([128, nh, 64])
            sv = src.rearrange("p (h e) -> p h e", e=64) if nh > 2 else src
            dv = dst.rearrange("p (h e) -> p h e", e=64)
            t1 = tt(dv, sv, cosv, ALU.mult, ready, list(free))
            tv = tmp[:, 0:nh * 64].rearrange("p (h e) -> p h e", e=64)
            t2 = []
            for lo in range(0, 64, 2 * s):
                for x, y in ((lo, lo + s), (lo + s, lo)):
                    snv = tab[:, tb, 1, x:x + s].unsqueeze(1).to_broadcast([128, nh, s])
                    t2.append(tt(tv[:, :, x:x + s], sv[:, :, y:y + s], snv, ALU.mult, ready, list(free)))
            return tt(dv, dv, tv, ALU.add, t1, t2)

        bias_free = [[kx]] * 4
        bias_tok = {}

        def load_bias(h):
            if h < NH:
                bias_tok[h] = dma("pool", bias[h % 4][:, :, :], tokmaj(d["rpb"][h]), f"d_b{h % 4}", bias_free[h % 4])

        for h in range(4):
            load_bias(h)
        rk = chunk(u_in["k"], [(AH, AL, kx, (4, 5)), (CH, CL, kc, (0, 1))], after=background(5),
                   mid={0: turn_u})
        cdone = [tx_c, ("pe", value["pe"])]
        tk_ = [tm(4 + tb, Kt[:, tb, :], "act", 1.0, rk[tb], tx_c) for tb in range(2)]
        tkc = [tm(tb, KC[:, tb, :], "act", 1.0, rk[2 + tb]) for tb in range(2)]
        rq = chunk(u_in["q"], [(AH, AL, kx, (2, 3))], after=background(5))
        tq_ = [tm(2 + tb, Q[:, tb, :], "act", 0.125, rq[tb], tx_c) for tb in range(2)]
        tkr = []
        prev = None
        for tb in range(2):
            prev = rope(KR[:, tb, :], Kt[:, tb, :], 8, rope1, 16, tb, [tk_[tb], t_rope1], prev, kc, tx_c,
                        ("pe", value["pe"]))
            tkr.append(prev)
        tqr = []
        for tb in range(2):
            prev = rope(QR[:, tb, :], Q[:, tb, :], 8, rope1, 16, tb, [tq_[tb], t_rope1], prev)
            tqr.append(prev)
        t_qk, t_pqk = [], []

        def turn_qk(*what):
            for src, dst, ts in what:
                e_, p_ = to_features(src, 4, dst, ["act", "dve"], ts, turn_free)
                t_qk.append(e_)
                t_pqk.append(p_)

        turn_free = []

        def ctx_done():
            turn_free.append(("pe", value["pe"]))

        rv = chunk(u_in["v"], [(CH, CL, kc, (4, 5)), (AH, AL, kx, (0, 1))], after=background(4),
                   mid={1: ctx_done, 2: lambda: turn_qk((KC, kcT, tkc), (Q, qT, tq_))})
        gdone = ("pe", value["pe"])
        tv_ = [tm(tb, V[:, tb, :], "act", 1.0, rv[2 + tb], tx_c) for tb in range(2)]
        tvc = [tm(4 + tb, VC[:, tb, :], "dve", 1.0, rv[tb]) for tb in range(2)]
        turn_qk((KR, kT, tkr), (QR, qrT, tqr))
        p1, p2 = t_pqk[2], t_pqk[0]
        p4 = t_pqk[3]

        ada2 = []

        def ada_tail(nm, n, t):
            r2 = rows2[n]
            b, w = tbank()
            if nm in ("sh", "sc"):
                for j in range(4):
                    tk = mm(bank[b][:, 2 * j:2 * j + 2], r2[:, j * 128:j * 128 + 128], comb,
                            True, True, t, w, inc=(j == 3))
                k0 = (0 if nm == "sh" else 8) + 4 * n
                t = tt(mod2[:, k0:k0 + 4, :], bank[b][:, 0:8].rearrange("p (k r) -> p k r", r=2),
                       v_b2[:, k0:k0 + 4].unsqueeze(2).to_broadcast([128, 4, 2]), ALU.add, tk)
            else:
                gt, tg = (g1b, t_g1) if nm == "g1" else (g2b, t_g2)
                gv = gt[:, 512 * n:512 * n + 512]
                tk = mm(bank[b][:, :], comb[:, 0:1].to_broadcast([4, 128]), r2[:, :], True, True, t, w, inc=True)
                t = tt(gv, bank[b][:, :], gv, ALU.add, tk, tg)
            rows2_free[n] = [tk]
            bfree[b] = [t]
            ada2.append(t)

        def ada_steps():
            tail = None
            for i8, (nm, n, us) in enumerate(u_ada2):
                bk = 4 + i8 % 2
                ada_unit(us[0], 0, bk, True, False)
                if tail:
                    ada_tail(*tail)
                yield
                tk = ada_unit(us[1], 4, bk, False, True)
                t = copy("act", rows2[n][:, :], bank[bk][0:4, :], tk, rows2_free[n])
                bfree[bk] = [t]
                tail = (nm, n, t)
                yield
            ada_tail(*tail)
            yield

        rows2_free = [[tkr, tqr, p1], [tkr, tqr, p1]]
        ada = ada_steps()

        def fill(n=1):
            for _ in range(n):
                next(ada, None)

        def conv_norm():
            b, w = tbank()
            for c in range(4):
                tk = mm(bank[b][:, 0:256], ones[:, :], cacc[:, c, :], c == 0, c == 3, w, conv_last, t_ones, inc=(c == 3))
            mu = bank[b]
            t = []
            for c in range(4):
                t.append(stt(ccen[:, c, :], mu[:, 0:256], -1.0 / 512, cacc[:, c, :], ALU.mult, ALU.add, tk, conv_last,
                             tu, t_hp))
            bfree[b] = t
            t_cc = t
            tsq = act(lambda q: q.activation(csq[:, :, :], ccen[:, :, :], ACT.Square), t_cc, conv_last)
            yield
            b, w = tbank()
            for c in range(4):
                tk = mm(bank[b][:, 0:256], ones[:, :], csq[:, c, :], c == 0, c == 3, w, tsq, inc=(c == 3))
            var = bank[b]
            t = act(lambda q: q.activation(crs[:, :], var[:, 0:256], ACT.Sqrt, bias=stat[:, 95:96], scale=1.0 / 512),
                    tk, t_eps2, p2)
            bfree[b] = [t]
            yield
            t = dve(lambda q: q.reciprocal(crs[:, :], crs[:, :]), t)
            yield
            t = tt(ccen[:, :, :], ccen[:, :, :], crs[:, :].unsqueeze(1).to_broadcast([128, 4, 256]), ALU.mult, t, tsq)
            tn = [act(lambda q, c=c: q.activation(cacc[:, c, :], ccen[:, c, :], ACT.Silu, bias=v_lnb[:, c:c + 1],
                                                  scale=v_lng[:, c:c + 1]), t) for c in range(4)]
            yield
            ch = act(lambda q: q.activation(flat(AH[:, 4:8, :]), flat(cacc[:, :, :]), ACT.Copy), tn, gdone)
            cl = tt(flat(AL[:, 4:8, :]), flat(cacc[:, :, :]), flat(AH[:, 4:8, :]).bitcast(F32), ALU.subtract, ch, tn, gdone)
            k_conv.extend([[[ch, cl], [ch, cl]]] * 4)
            yield

        k_conv = []
        cn = conv_norm()

        its = [(h, tb) for h in range(NH) for tb in range(2)]
        st = {}

        def scores1(n):
            h, tb = its[n]
            b = n % 2
            r = slice(64 * (h % 2), 64 * (h % 2) + 64)
            w = bfree[b]
            bfree[b] = []
            mm(bank[b][:, 0:256], qrT[r, h // 2, tb * 128:tb * 128 + 128], kT[r, h // 2, :], True, True, w, t_qk)
            st["s", n] = mm(bank[b][:, 256:512], qT[r, h // 2, tb * 128:tb * 128 + 128], kcT[r, h // 2, :],
                            True, True, inc=True)

        pv_tok = {}
        pe_tr = {}
        obank = (2, 3)

        def soft1(n):
            h, tb = its[n]
            b = n % 2
            m1, m2, mg = mneg[:, 2 * n:2 * n + 1], mneg[:, 2 * n + 1:2 * n + 2], rl[:, 16 + n:17 + n]
            a = dve(lambda q: q.reduce_max(m1, bank[b][:, 256:512], AX.X), st["s", n])
            bt = bias[h % 4][:, tb, :]
            a = dve(lambda q: q.tensor_tensor_reduce(out=s1[b][:, :], in0=bank[b][:, 0:256], in1=bt, scale=1.0,
                                                     scalar=m1, op0=ALU.add, op1=ALU.max, accum_out=m2),
                    a, bias_tok[h], t_pqk, st.get(("e", n - 2)))
            bias_free[h % 4] = [a]
            g = tsc(mg, m2, -1.0, None, ALU.mult, None, a)
            e1_ = act(lambda q: q.activation(P1[b][:, 0:256], s1[b][:, :], ACT.Exp, bias=mg,
                                             accum_out=lsum[:, 2 * n:2 * n + 1]), g, t_pqk, pe_tr.get(n - 2))
            e2_ = act(lambda q: q.activation(P1[b][:, 256:512], bank[b][:, 256:512], ACT.Exp, bias=mg,
                                             accum_out=lsum[:, 2 * n + 1:2 * n + 2]), g, pe_tr.get(n - 2))
            bfree[b] = [a, e2_]
            st["e", n] = [e1_, e2_]

        def turn1(n):
            b, tk = transposes([(i, P1[n % 2][:, i * 128:i * 128 + 128]) for i in range(4)], st["e", n])
            pe_tr[n] = tk
            t = copy("act" if n % 2 or n < 12 else "dve", PT1[n % 3][:, :], bank[b][:, :], tk, pv_tok.get(n - 3), t_pqk)
            bfree[b] = [t]
            st["t", n] = t

        def pv1(n):
            h, tb = its[n]
            ob = obank[tb]
            w = [st["t", n], tv_, tvc]
            if h == 0:
                w.append(bfree[ob])
                bfree[ob] = []
            for i in range(4):
                vv = (V if i < 2 else VC)[:, i % 2, h * 64:h * 64 + 64]
                tk = mm(bank[ob][:, h * 64:h * 64 + 64], PT1[n % 3][:, i * 128:i * 128 + 128], vv, i == 0, i == 3,
                        w, inc=(i == 3))
            pv_tok[n] = tk

        scores1(0)
        for n in range(16):
            soft1(n)
            if n + 1 < 16:
                scores1(n + 1)
            fill(1)
            if n < 8:
                background(5)()
            elif n == 8:
                background(500)()
            else:
                next(cn, None)
            if n > 1:
                pv1(n - 2)
            turn1(n)
            if n % 2 == 1:
                load_bias(n // 2 + 4)
        pv1(14)
        pv1(15)
        for _ in cn:
            pass
        n16 = lsum[:, 0:32].rearrange("p (n r) -> p n r", r=2)
        t = tt(rl[:, 32:48], n16[:, :, 0], n16[:, :, 1], ALU.add, st["e", 15])
        t_rl = dve(lambda q: q.reciprocal(rl[:, 48:64], rl[:, 32:48]), t)
        rlv = rl[:, 48:64].rearrange("p (h t) -> p h t", t=2)

        def o_out(O_, ob, tb, rv_, *toks):
            t = tt(O_[:, tb, :].rearrange("p (h e) -> p h e", e=64),
                   bank[ob][:, :].rearrange("p (h e) -> p h e", e=64),
                   rv_.unsqueeze(2).to_broadcast([128, 8, 64]), ALU.mult, list(toks))
            bfree[ob] = [t]
            return t

        t_o = [o_out(O1, 2 + tb, tb, rlv[:, :, tb], t_rl, pv_tok[14 + tb], t_pqk) for tb in range(2)]
        t_A2 = stt(A2[:, :], mod2[:, 8:16, 0], 1.0, v_n2, ALU.add, ALU.mult, ada2)
        t_B2 = dve(lambda q: q.tensor_copy(modB[:, 0, :], mod2[:, 0:8, 0]), ada2, kx)

        t_rope2 = dma("pool", rope2[:, :, :, :], d["rope2"], "d_r2", t_mod1)
        t_lnC = dma("pool", lnC[:, :], d["lnC"], "d_lc", t_mod1)
        t_caus = dma("pool", caus[:, :], d["caus"], "d_ca", t_mod1)

        fill(20)
        ready = [[], []]
        sq = [[], []]

        def out_parts(us, tb, ktoks, after):
            for u, n, k0, first, last in us:
                pump(u)
                tok = part(u, (AH, AL, k0, tb, 2 * n + tb, (0, 512), first, last, pairs(ktoks[k0 // 4], 0, 4, tb)), tb == 1)
                if last:
                    after(n, tb, tok)

        def out1(n, tb, tok):
            t = residual(n, tb, 2 * n + tb, tok, g1b, t_x, tx_x, ada2, t_o, kk_out[0])
            ready[tb].append(t)
            sq[tb].append(square(X[:, tb, halves(n)], S1[:, tb, halves(n)], t))

        kk_out = [None, k_conv]
        us_out = [(u_out[0], 0, 4, True, False), (u_out[1], 1, 4, True, False),
                  (u_out[2], 0, 0, False, True), (u_out[3], 1, 0, False, True)]
        out_parts(us_out[0:2], 0, kk_out, out1)
        sp_ = [split_tb(O1, 4, AH, AL, 0, tb, t_o[tb], gdone) for tb in range(2)]
        kk_out[0] = [[sp_[0][0], sp_[1][0]]] * 4
        out_parts(us_out[2:4], 0, kk_out, out1)
        r_, rt_ = rstd(sq[0])
        wo0 = ("pe", value["pe"])
        tx0 = norm_scale(X, 0, r_, rt_)
        out_parts(us_out[0:2], 1, kk_out, out1)
        kh0 = norm_turn(0, tx0, AH, AL, A2, modB[:, 0, :], t_A2, t_B2, wo0)
        out_parts(us_out[2:4], 1, kk_out, out1)
        wo_pe = ("pe", value["pe"])
        kh = [[kh0[k], None] for k in range(8)]
        tx_h = [tx0]

        r_, rt_ = rstd(sq[1])
        tx_h.append(norm_scale(X, 1, r_, rt_))
        t_fg = dma("pool", g1b[:, :], d["final_g"].to_broadcast([128, D]), "d_fg", ready)

        def turn_late(kt, tx, *args):
            for k, t in enumerate(norm_turn(1, tx, *args)):
                kt[k][1] = t

        hfree = [[wo_pe, t_qk, st["e", 15], pv_tok], [wo_pe]]
        hid_free = [[wo_pe], [wo_pe]]
        hh_free = [[wo_pe], [wo_pe]]
        attn_done = [pv_tok[15], pv_tok[14], p4]
        hh_tok = {}

        def half_chunk(us, kt, tb, bk):
            for i, u in enumerate(us):
                pump(u)
                tok = part(u, (AH, AL, 4 * i, tb, bk, (0, 512), i == 0, i == 1, pairs(kt, 4 * i, 4, tb)), tb == 1)
            return tok

        def up1(c, tb, bk=None):
            bk = 4 + tb if bk is None else bk
            r = half_chunk(u_m1[c], kh, tb, bk)
            rv_ = rel[tb][:, :]
            a = act(lambda q: q.activation(rv_, bank[bk][:, :], ACT.Relu), r, st.get(("sq", tb)), attn_done)
            bfree[bk] = [a]
            s = act(lambda q: q.activation(hid[c % 2][:, tb, :], rv_, ACT.Square), a, hid_free[c % 2], attn_done)
            st["sq", tb] = s
            st["hid", c, tb] = s

        def turn_hid(c, nj, tb):
            tk, p_ = split_tb(hid[c % 2], nj, HH[c % 2], HL[c % 2], 0, tb, st["hid", c, tb], hh_free[c % 2], attn_done)
            hh_tok.setdefault(c, [[None, None] for _ in range(nj)])
            for k in range(nj):
                hh_tok[c][k][tb] = tk
            if tb == 0:
                hid_free[c % 2] = []
            hid_free[c % 2] = hid_free[c % 2] + [p_]

        def down(us, c, tb, first, last, mid=None):
            r = []
            for n in range(2):
                if mid and n == 1:
                    mid()
                for j, u in enumerate(us):
                    pump(u)
                    tok = part(u, (HH[c % 2], HL[c % 2], 2 * j, tb, 2 * n + tb, (512 * n, 512),
                                   first and j == 0, last and j == len(us) - 1,
                                   pairs(hh_tok[c], 2 * j, 2, tb)), False)
                    if tb == 1 and n == 1:
                        rel_hl.append(tok)
                r.append(tok)
            if tb == 1:
                hh_free[c % 2] = [tok]
            return r

        def feed_forward(nc_, nj, up, dn, early, late=None):
            up(0, 0)
            early()
            up(1, 0, 0)
            up(0, 1)
            turn_hid(0, nj, 0)
            up(1, 1, 1)
            turn_hid(0, nj, 1)
            for c in range(1, nc_):
                if c > 1:
                    up(c, 0)
                if c == nc_ - 1:
                    down(dn[c - 1], c - 1, 0, False, False)
                    up(c, 1)
                    turn_hid(c, nj, 0)
                    r0 = down(dn[c], c, 0, False, True)
                    turn_hid(c, nj, 1)
                    yield r0, 0
                    down(dn[c - 1], c - 1, 1, False, False)
                    yield down(dn[c], c, 1, False, True, late), 1
                else:
                    if c > 1:
                        up(c, 1)
                    for tb in range(2):
                        down(dn[c - 1], c - 1, tb, c == 1, False)
                    for tb in range(2):
                        turn_hid(c, nj, tb)

        ff = feed_forward(8, 4, up1, u_m2,
                          lambda: turn_late(kh, tx_h[1], AH, AL, A2, modB[:, 0, :], t_A2, t_B2, wo_pe),
                          lambda: between_turn(0))
        r_, _ = next(ff)
        kh_pe = ("pe", value["pe"])
        xr = [[], []]
        k2 = [[None, None] for _ in range(8)]
        tx_2 = []

        def between_turn(tb):
            for k, t in enumerate(norm_turn(tb, tx_2[tb], AH, AL, v_mix, None, kh_pe)):
                k2[k][tb] = t

        def between_norms(tb, r):
            zs = []
            for n in range(2):
                t = residual(n, tb, 2 * n + tb, r[n], g2b, ada2, kh, ready[tb], tx_h)
                s1_ = square(X[:, tb, halves(n)], S1[:, tb, halves(n)], t)
                xv = X[:, tb, halves(n)]
                t = tt(xv, xv, g1b[:, halves(n)], ALU.mult, t, s1_[1], t_fg)
                zs.append((s1_, square(xv, S1[:, tb, halves(n)], t, s1_[1]), t))
            r1, t1 = rstd([z[0] for z in zs])
            cz, cr, c2 = col(), col(), col()
            tz = tsc(cz, zs[0][1][0], zs[1][1][0], None, ALU.add, None, zs[0][1][1], zs[1][1][1])
            t2 = tsc(cr, cz, r1, r1, ALU.mult, ALU.mult, tz, t1)
            r2, t2 = rstd([(cr, t2)])
            t2 = tsc(c2, r2, r1, None, ALU.mult, None, t2, t1)
            tx_ = norm_scale(X, tb, c2, t2, [z[2] for z in zs], [z[1][1] for z in zs])
            tx_2.append(tx_)
            xr[tb] = [tsc(X[:, tb, :], X[:, tb, :], r1, None, ALU.mult, None, t1, tx_)]

        between_norms(0, r_)
        r_, _ = next(ff)
        gdone2 = ("pe", value["pe"])
        between_norms(1, r_)


        hfin = [hh_tok[7], hh_tok[6], gdone2]
        rawf = [[hfin], [hfin]]
        rrf = [[hfin], [hfin]]
        cnt = {"n": 0}
        prev = None

        def project(nm, scale, after=None, r=None):
            nonlocal prev
            i = cnt["n"] % 2
            cnt["n"] += 1
            bk = (0, 1) if i else (2, 3)
            if r is None:
                r = chunk(u_in2[nm], [(AH, AL, k2, bk)], after=after)
            else:
                bk = (4, 5)
            ts = []
            for tb in range(2):
                t = tm(bk[tb], raw[i][:, tb, :], "act", scale, r[tb], rawf[i])
                prev = rope(rr[i][:, tb, :], raw[i][:, tb, :], 8, rope2, 32, tb, [t, t_rope2], prev, rrf[i])
                ts.append(prev)
            rawf[i] = ts
            return i, ts

        def small_part(tb):
            for i, u in enumerate(u_in2["s"]):
                pump(u)
                tok = part(u, (AH, AL, 4 * i, tb, 2 + tb, (0, 200), i == 0, i == 1, pairs(k2, 4 * i, 4, tb)), tb == 1)
            return tok

        r_qi = [half_chunk(u_in2["qi"], k2, 0, 4)]
        between_turn(1)
        r = [small_part(0)]
        r_qi.append(half_chunk(u_in2["qi"], k2, 1, 5))
        r.append(small_part(1))
        it_qi = project("qi", 1.0, r=r_qi)
        t_nf = dma("pool", g2b[:, :], d["norm_final"].to_broadcast([128, D]), "d_nf", xr)
        t_sm = []
        for tb in range(2):
            t = act(lambda q, tb=tb: q.activation(small[:, tb, :], bank[2 + tb][:, 0:200], ACT.Copy), r[tb], hfin)
            bfree[2 + tb] = [t]
            t_sm.append(t)
        t_kk = []
        for i, c0 in ((0, 0), (1, 128)):
            for tb in range(2):
                src = small[:, tb, c0:c0 + 64].unsqueeze(1).to_broadcast([128, 2, 64])
                prev = rope(skk[i][:, tb, :], src, 2, rope2, 32, tb, [t_sm, t_rope2], prev)
                t_kk.append(prev)
        it_qb = project("qb", 0.125)
        t_kiT = []
        for i, dst in ((1, kiT), (0, kbT)):
            b, tk = transposes([(tb, skk[i][:, tb, :]) for tb in range(2)], t_kk)
            t = copy("act", dst[:, :], bank[b][:, 0:256], tk, hfin)
            bfree[b] = [t]
            t_kiT.append(t)
        def turn_proj(it, dst, eng=("act", "dve")):
            i, ts = it
            e_, p_ = to_features(rr[i], 4, dst, eng, ts, hfin)
            rrf[i] = p_
            return e_

        t_qi = turn_proj(it_qi, qiT)

        def dots():
            acc = [None, None]
            for h in range(NH):
                b = 4 + h % 2
                rws = slice(64 * (h % 2), 64 * (h % 2) + 64)
                w = bfree[b]
                bfree[b] = []
                mm(bank[b][:, 128:256], qiT[rws, h // 2, 0:128], kiT[rws, 0:128], True, True, w, t_qi, t_kiT)
                tk = mm(bank[b][:, 256:512], qiT[rws, h // 2, 128:256], kiT[rws, :], True, True, inc=True)
                rv_ = rlu[h % 2]
                a = act(lambda q, rv_=rv_, b=b: q.activation(rv_[:, :], bank[b][:, 128:512], ACT.Relu), tk,
                        st.get(("rf", h % 2)), k2)
                bfree[b] = [a]
                yield
                new = []
                for tb in range(2):
                    cc = slice(0, 128) if tb == 0 else slice(128, 384)
                    wv = small[:, tb, 192 + h:193 + h]
                    if h == 0:
                        acc[tb] = tsc(sco[:, cc], rv_[:, cc], wv, None, ALU.mult, None, a, prev)
                    else:
                        acc[tb] = stt(sco[:, cc], rv_[:, cc], wv, sco[:, cc], ALU.mult, ALU.add, a, acc[tb])
                    new.append(acc[tb])
                st["rf", h % 2] = new
                yield
            t = stt(sco[:, :], sco[:, :], IDX_SCALE, caus[:, :], ALU.mult, ALU.add, acc, t_caus)
            lt = [t, t]
            for _ in range(8):
                for tb in range(2):
                    cc = slice(0, 128) if tb == 0 else slice(128, 384)
                    lt[tb] = dve(lambda q, tb=tb, cc=cc: q.max(best[:, tb, :], sco[:, cc]), lt[tb])
                    yield
                for tb in range(2):
                    cc = slice(0, 128) if tb == 0 else slice(128, 384)
                    lt[tb] = dve(lambda q, tb=tb, cc=cc: q.match_replace(sco[:, cc], best[:, tb, :], sco[:, cc], SENT),
                                 lt[tb])
                    yield
            t = tsc(mB[:, :], sco[:, :], SENT, None, ALU.is_equal, None, lt, hfin)
            t = tsc(mB[:, :], mB[:, :], -1.0, -NEG, ALU.add, ALU.mult, t)
            st["mB"] = tt(mB[:, :], mB[:, :], caus[:, :], ALU.add, t)
            yield

        it_qa = project("qa", 0.125)
        bg.append(dots())
        t_qb = turn_proj(it_qb, qbT)
        it_ka = project("ka", 1.0, background(4))
        t_qa = turn_proj(it_qa, qaT)
        bk = (0, 1) if cnt["n"] % 2 else (2, 3)
        r = chunk(u_in2["va"], [(AH, AL, k2, bk)], after=background(5))
        t_va = [tm(bk[tb], va[:, tb, :], "act", 1.0, r[tb], hfin) for tb in range(2)]
        t_ka = turn_proj(it_ka, kaT, ("act",))
        cnt["n"] += 1
        ring = {"n": 0}

        gsteps = []

        def gates():
            for nm, dst, n in (("ga0", ga, 0), ("ga1", ga, 1), ("gb0", gb, 0), ("gb1", gb, 1)):
                us = u_in2[nm]
                for tb in range(2):
                    for i, u in enumerate(us):
                        pump(u)
                        tok = part(u, (AH, AL, 4 * i, tb, 4 + tb, (0, 512), i == 0, i == 1, pairs(k2, 4 * i, 4, tb)),
                                   tb == 1)
                        if i == 0:
                            yield
                    o_ = dst[:, tb, 512 * n:512 * n + 512]
                    gsteps.append(tm(4 + tb, o_, "act", 1.0, tok, t_ka, t_qa, t_qb, rrf, rawf))
                    yield

        gs = gates()

        def gfill():
            next(gs, None)

        ky = []

        def split_a():
            sp_ = [split_tb(Oa, 4, YH[0], YL[0], 0, tb, t_oa[tb], a_done) for tb in range(2)]
            ky.append([[sp_[0][0], sp_[1][0]]] * 4)

        def attend(name, qT_, kTs, vs, bias_, O_, btok, col, obs, extra):
            S, E, TR, PTt, PVt = {}, {}, {}, {}, {}

            def scores(h):
                b = h % 2
                r_ = slice(64 * (h % 2), 64 * (h % 2) + 64)
                w = bfree[b]
                bfree[b] = []
                kk = kTs(h)
                mm(bank[b][:, 128:256], qT_[r_, h // 2, 0:128], kk[r_, 0:128], True, True, w, extra)
                S[h] = mm(bank[b][:, 256:512], qT_[r_, h // 2, 128:256], kk[r_, :], True, True, inc=True)

            def soft(h):
                b = h % 2
                es = []
                fr = []
                for tb in range(2):
                    cc = slice(0, 128) if tb == 0 else slice(128, 384)
                    pc = slice(128, 256) if tb == 0 else slice(256, 512)
                    i = col + 2 * h + tb
                    m1 = mneg[:, i:i + 1]
                    mg = rl[:, i:i + 1]
                    a = dve(lambda q, cc=cc, pc=pc, m1=m1: q.tensor_tensor_reduce(
                        out=s2[b][:, cc], in0=bank[b][:, pc], in1=bias_[:, cc], scale=1.0, scalar=SENT,
                        op0=ALU.add, op1=ALU.max, accum_out=m1), S[h], btok, E.get(h - 2))
                    fr.append(a)
                    g = tsc(mg, m1, -1.0, None, ALU.mult, None, a)
                    es.append(act(lambda q, cc=cc, mg=mg, i=i: q.activation(
                        P2[b][:, cc], s2[b][:, cc], ACT.Exp, bias=mg, accum_out=lsum[:, i:i + 1]), g, TR.get(h - 2)))
                bfree[b] = fr
                E[h] = es

            def turn(h):
                b, tk = transposes([(i, P2[h % 2][:, i * 128:i * 128 + 128]) for i in range(3)], E[h])
                TR[h] = tk
                t = copy("dve" if h % 2 else "act", PT2[h % 3][:, :], bank[b][:, 0:384], tk, PVt.get(h - 3))
                bfree[b] = [t]
                PTt[h] = t

            def pv(h):
                w = [PTt[h], extra]
                if h == 0:
                    w += [bfree[obs[0]], bfree[obs[1]]]
                    bfree[obs[0]] = bfree[obs[1]] = []
                v = vs(h)
                hc = slice(h * 64, h * 64 + 64)
                mm(bank[obs[0]][:, hc], PT2[h % 3][:, 0:128], v[0], True, True, w)
                mm(bank[obs[1]][:, hc], PT2[h % 3][:, 128:256], v[0], True, False)
                PVt[h] = mm(bank[obs[1]][:, hc], PT2[h % 3][:, 256:384], v[1], False, True, inc=True)

            scores(0)
            for h in range(NH):
                soft(h)
                if h + 1 < NH:
                    scores(h + 1)
                gfill()
                background(6)()
                if h > 1:
                    pv(h - 2)
                turn(h)
                if h == 4 and name == "b":
                    split_a()
            pv(NH - 2)
            pv(NH - 1)
            t = dve(lambda q: q.reciprocal(rl[:, 32 + col:48 + col], lsum[:, col:col + 16]), E[NH - 1])
            rv_ = rl[:, 32 + col:48 + col].rearrange("p (h t) -> p h t", t=2)
            return [o_out(O_, obs[tb], tb, rv_[:, :, tb], t, PVt[NH - 1]) for tb in range(2)], E[NH - 1]

        gfill()
        t_oa, _ = attend("a", qaT, lambda h: kaT[:, h // 2, :],
                         lambda h: [va[:, i, h * 64:h * 64 + 64] for i in range(2)], lnC, Oa, t_lnC, 0, (2, 3),
                         [t_qa, t_ka, t_va, k2, tx_2])
        a_done = ("pe", value["pe"])
        background(500)()
        gfill()
        t_ob, last_e = attend("b", qbT, lambda h: kbT[:, :],
                              lambda h: [small[:, i, 64:128] for i in range(2)], mB, Ob, st["mB"], 16, (2, 3),
                              [t_qb, t_kiT, k2, tx_2])
        for _ in range(20):
            gfill()
        t_ga = act(lambda q: q.activation(flat(ga[:, :, :]), flat(ga[:, :, :]), ACT.Sigmoid), gsteps)
        ypt = ("pe", value["pe"])
        t_m = {}

        def up(i, bks):
            us = (u_upa, u_upb)[i]
            for n in range(2):
                for tb in range(2):
                    pump(us[n])
                    bk = bks[n][tb]
                    t_m["r", i, n, tb] = part(us[n], (YH[i], YL[i], 0, tb, bk, (0, 512), True, True,
                                                      pairs(ky[i], 0, 4, tb)), tb == 1)

        bks = (((4, 5), (0, 1)), ((2, 3), (4, 5)))
        up(0, bks[0])
        sp_ = [split_tb(Ob, 4, YH[1], YL[1], 0, tb, t_ob[tb], ypt) for tb in range(2)]
        ky.append([[sp_[0][0], sp_[1][0]]] * 4)
        t_gb = act(lambda q: q.activation(flat(gb[:, :, :]), flat(gb[:, :, :]), ACT.Sigmoid), gsteps)
        for n in range(2):
            for tb in range(2):
                bk = bks[0][n][tb]
                t_m[n, tb] = tt(mrg[:, tb, halves(n)], bank[bk][:, :], ga[:, tb, halves(n)], ALU.mult,
                                t_m["r", 0, n, tb], t_ga, ypt)
                bfree[bk] = [t_m[n, tb]]
        up(1, bks[1])
        for tb in range(2):
            for n in range(2):
                bk = bks[1][n][tb]
                mv = mrg[:, tb, halves(n)]
                t = tt(mt[tb][:, :], bank[bk][:, :], gb[:, tb, halves(n)], ALU.mult, t_m["r", 1, n, tb], t_gb,
                       t_m.get(("f", tb)), ypt)
                bfree[bk] = [t]
                t_m[n, tb] = tt(mv, mv, mt[tb][:, :], ALU.add, t, t_m[n, tb])
                t_m["f", tb] = t_m[n, tb]
        allm = [t_m[n, tb] for n in range(2) for tb in range(2)]
        km = [[None, None] for _ in range(8)]
        for tb in range(2):
            for i in range(2):
                tk, _ = split_tb(mrg[:, :, 512 * i:512 * i + 512], 4, AH, AL, 4 * i, tb, t_m[0, tb], t_m[1, tb], ypt)
                for k in range(4):
                    km[4 * i + k][tb] = tk
        ready = [[], []]
        sq = [[], []]

        def out2(n, tb, tok):
            t = residual(n, tb, 2 * n + tb, tok, None, xr, tx_2)
            ready[tb].append(t)
            sq[tb].append(square(X[:, tb, halves(n)], S1[:, tb, halves(n)], t, allm, km))

        us_out = [(u_out2[n][i], n, 4 * i, i == 0, i == 1) for i in range(2) for n in range(2)]
        kk_out = [km[0:4], km[4:8]]
        out_parts(us_out, 0, kk_out, out2)
        wo0 = ("pe", value["pe"])
        r_, rt_ = rstd(sq[0])
        tx_f = [norm_scale(X, 0, r_, rt_)]
        out_parts(us_out[0:2], 1, kk_out, out2)
        kf = [[t, None] for t in norm_turn(0, tx_f[0], AH, AL, v_ffn, None, wo0)]
        out_parts(us_out[2:4], 1, kk_out, out2)
        wo_pe = ("pe", value["pe"])
        r_, rt_ = rstd(sq[1])
        tx_f.append(norm_scale(X, 1, r_, rt_))
        attn_done = [wo_pe, allm]
        hid_free = [[wo_pe, allm], [wo_pe, allm]]
        hh_free = [[wo_pe, allm], [wo_pe, allm]]
        hh_tok.clear()

        def upg(c, tb, bk=None):
            bk = 4 + tb if bk is None else bk
            r = half_chunk(u_gu[c], kf, tb, bk)
            rv_ = rel[tb][:, 0:256]
            a = act(lambda q: q.activation(rv_, bank[bk][:, 0:256], ACT.Silu), r, st.get(("sq2", tb)), attn_done)
            s = tt(hid[c % 2][:, tb, 0:256], bank[bk][:, 256:512], rv_, ALU.mult, a, hid_free[c % 2])
            bfree[bk] = [s]
            st["sq2", tb] = s
            st["hid", c, tb] = s

        ff = feed_forward(11, 2, upg, u_dn, lambda: turn_late(kf, tx_f[1], AH, AL, v_ffn, None, wo_pe))
        t_out = []
        for r_, tb in ff:
            sq_ = []
            for n in range(2):
                t = residual(n, tb, 2 * n + tb, r_[n], None, ready, tx_f)
                sq_.append(square(X[:, tb, halves(n)], S1[:, tb, halves(n)], t, kf))
            r_, rt_ = rstd(sq_)
            for n in range(2):
                hn = halves(n)
                t = stt(S1[:, tb, hn], X[:, tb, hn], r_, g2b[:, hn], ALU.mult, ALU.mult, rt_, t_nf, kf)
                t_out.append(dma("sp", out[tb * 128:tb * 128 + 128, hn], S1[:, tb, hn], f"d_o{tb}{n}", t))
        prog["sp"].append((t_out, None, None, 0))
        assert state["l"] == len(units) and state["s"] == len(units)

        sems = {s: ctx.enter_context(nc.semaphore(f"s_{s}")) for s in value}
        block = ctx.enter_context(nc.Block())

        def emit(name):
            def run(eng):
                for waits, fn, sem, by in prog[name]:
                    for s, v in waits:
                        eng.wait_ge(sems[s], v)
                    if fn is not None:
                        ins = fn(eng)
                        if sem is not None:
                            ins.then_inc(sems[sem], by)
            return run

        block.sync(emit("sp"))
        block.gpsimd(emit("pool"))
        block.scalar(emit("act"))
        block.vector(emit("dve"))
        block.tensor(emit("pe"))


def rope_tables(pos_of, width):
    n = width // 2
    t = np.arange(T)
    inv = np.float32(10000.0) ** (-np.arange(n, dtype=np.float32) / np.float32(n))
    cols_c, cols_s = [], []
    for pos in pos_of(t):
        ang = pos.astype(np.float32)[:, None] * inv[None, :].astype(np.float32)
        c, s = np.cos(ang.astype(np.float32)), np.sin(ang.astype(np.float32))
        cols_c += [c, c]
        cols_s += [-s, s]
    tab = np.stack([np.concatenate(cols_c, 1), np.concatenate(cols_s, 1)], 1).astype(np.float32)
    return np.ascontiguousarray(tab.reshape(2, 128, 2, 64).transpose(1, 0, 2, 3))


def packed(m):
    return np.ascontiguousarray(np.concatenate([m[:128, :128], m[128:, :]], 1).astype(np.float32))


def kernel(**inputs):
    import concourse.bacc as bacc
    from concourse.bass_utils import run_bass_kernel_spmd

    a = {k: np.asarray(v) for k, v in inputs.items()}

    def fm(v):
        v = v.reshape(-1)
        return v.reshape(-1, 128).T

    bada = a["b_ada"].reshape(-1)
    comb = np.zeros((128, 2), np.float32)
    comb[[0, 1, 2, 3], [0, 1, 0, 1]] = 1.0
    vec = np.concatenate([
        fm(a["norm1_g"]), fm(a["norm2_g"]), fm(bada[0:2048]), fm(bada[3072:5120]),
        a["dw_kernel"][0].reshape(31, 4, 128).transpose(2, 1, 0).reshape(128, 124),
        fm(a["dw_bias"]), fm(a["conv_ln_g"]), fm(a["conv_ln_b"]), fm(a["norm_mix_2"]), fm(a["norm_ffn_2"]),
        np.concatenate([comb, np.zeros((128, 22), np.float32)], 1)], 1)
    cs = np.stack([a["c"].reshape(8, 128), a["c_ctx"].reshape(8, 128)], -1).transpose(1, 0, 2).reshape(128, 16)

    t = np.arange(T)
    row, col = t // 64, t % 64
    start = np.clip(col - 8, 0, 48)
    roff = np.clip(row[None, :] - row[:, None] + 7, 0, 14)
    coff = col[None, :] - col[:, None] + 15
    inside = (col[None, :] >= start[:, None]) & (col[None, :] < start[:, None] + 16)
    rpb = a["rpb"][0]
    rb = np.where(inside[None], rpb[:, roff, np.clip(coff, 0, 30)], np.float32(NEG)).astype(np.float32)

    q, k = t[:, None], t[None, :]
    count = ((q - k >= 0) & (q - k <= 128)).astype(int) + ((q >= k) & ((q - k) % 4 == 0)) + ((q >= k) & ((q - k) % 16 == 0))
    lnC = np.where(count > 0, np.log(np.maximum(count, 1).astype(np.float32)), np.float32(NEG))
    caus = np.where(q >= k, np.float32(0), np.float32(NEG))

    arrays = {
        "vec": vec, "cs": cs, "x": a["x"][0], "ctx": a["ctx"][0], "ident": np.eye(128, dtype=np.float32),
        "rope1": rope_tables(lambda t: (t // 64, t % 64), 32), "rope2": rope_tables(lambda t: (t,), 64),
        "lnC": packed(lnC), "caus": packed(caus), "b_ada": bada.reshape(1, -1),
        "rpb": rb, "final_g": a["final_g"].reshape(1, -1), "norm_final": a["norm_final_2"].reshape(1, -1),
    }
    for n in ("w_ada", "w_in", "w_out", "w_mlp1", "w_mlp2", "w_in_2", "w_up_a_2", "w_up_b_2", "w_out_2",
              "w_gate_2", "w_up_2", "w_down_2"):
        arrays[n] = a[n][0]
    arrays = {f"in_{k}": np.ascontiguousarray(v) for k, v in arrays.items()}
    nc = bacc.Bacc("TRN2", target_bir_lowering=False, num_devices=1)
    d = {k[3:]: nc.dram_tensor(k, v.shape, mybir.dt.from_np(v.dtype), kind="ExternalInput").ap()
         for k, v in arrays.items()}
    out = nc.dram_tensor("out", (T, D), F32, kind="ExternalOutput").ap()
    build_program(nc, d, out)
    res = run_bass_kernel_spmd(nc, [arrays], core_ids=[0])
    return res.results[0]["out"].reshape(1, T, D)
```
